# Optimizing a Trainium2 kernel written in Bass

```python
import math
import jax, jax.numpy as jnp
from jax import lax
import numpy as np

D_MODEL = 1024
BATCH = 1
SEQ = 2048
DEPTH = 1

ATTN_HEADS = 16
ATTN_KV_HEADS = 4
HEAD_DIM = 64
ATTN_WIDTH = ATTN_HEADS * HEAD_DIM
KV_WIDTH = ATTN_KV_HEADS * HEAD_DIM
WINDOW = 128
BLOCK = 128
REL_BUCKETS = 32
REL_MAX_DIST = 128
SSM_EXPAND = 2
SSM_WIDTH = SSM_EXPAND * D_MODEL
SSM_HEAD_DIM = 64
SSM_HEADS = SSM_WIDTH // SSM_HEAD_DIM
SSM_GROUPS = 4
SSM_HEADS_PER_GROUP = SSM_HEADS // SSM_GROUPS
SSM_STATE = 128
CONV_WIDTH = 4
CHUNK = 128
XBC_WIDTH = SSM_WIDTH + 2 * SSM_GROUPS * SSM_STATE
DT_MIN = 0.001
DT_MAX = 0.1
N_BRANCH = 2
IN_WIDTH = ATTN_WIDTH + 2 * KV_WIDTH + ATTN_WIDTH + SSM_WIDTH + XBC_WIDTH + SSM_HEADS + N_BRANCH * D_MODEL
EPS = 1e-6

kernel_name = "hybrid_swa_sink_ssd_gated_merge"

def rms_norm(x, w, eps=EPS):
    xf = x.astype(jnp.float32)
    xf = xf * lax.rsqrt(jnp.mean(xf * xf, axis=-1, keepdims=True) + eps)
    return (xf * w.astype(jnp.float32)).astype(x.dtype)

def t5_causal_bucket(dist):
    n = jnp.maximum(dist, 0)
    max_exact = REL_BUCKETS // 2
    nf = jnp.maximum(n, 1).astype(jnp.float32)
    large = max_exact + (jnp.log(nf / max_exact) / math.log(REL_MAX_DIST / max_exact)
                         * (REL_BUCKETS - max_exact)).astype(jnp.int32)
    large = jnp.minimum(large, REL_BUCKETS - 1)
    return jnp.where(n < max_exact, n, large)

def sliding_window_attention(q, k, v, q_norm_w, k_norm_w, rel_bias, sinks):
    b, s = q.shape[0], q.shape[1]
    nb = s // BLOCK
    grp = ATTN_HEADS // ATTN_KV_HEADS
    q = rms_norm(q, q_norm_w)
    k = rms_norm(k, k_norm_w)
    qb = q.reshape(b, nb, BLOCK, ATTN_KV_HEADS, grp, HEAD_DIM)

    def banded(t):
        tb = t.reshape(b, nb, BLOCK, ATTN_KV_HEADS, HEAD_DIM)
        prev = jnp.concatenate([jnp.zeros_like(tb[:, :1]), tb[:, :-1]], axis=1)
        return jnp.concatenate([prev, tb], axis=2)

    kb, vb = banded(k), banded(v)
    scores = jnp.einsum("bnqhgd,bnkhd->bnhgqk", qb, kb).astype(jnp.float32) * (HEAD_DIM ** -0.5)

    qi = jnp.arange(BLOCK)[:, None]
    kj = jnp.arange(2 * BLOCK)[None, :]
    dist = qi + BLOCK - kj
    key_pos = jnp.arange(nb)[:, None, None] * BLOCK - BLOCK + kj[None]
    mask = (dist >= 0) & (dist < WINDOW) & (key_pos >= 0)
    bias = rel_bias.astype(jnp.float32)[t5_causal_bucket(dist)]
    bias = bias.reshape(BLOCK, 2 * BLOCK, ATTN_KV_HEADS, grp).transpose(2, 3, 0, 1)
    scores = jnp.where(mask[None, :, None, None], scores + bias[None, None], -jnp.inf)

    sink = sinks.astype(jnp.float32).reshape(ATTN_KV_HEADS, grp)[None, None, :, :, None, None]
    m = jnp.maximum(scores.max(axis=-1, keepdims=True), sink)
    p = jnp.exp(scores - m)
    probs = p / (p.sum(axis=-1, keepdims=True) + jnp.exp(sink - m))
    out = jnp.einsum("bnhgqk,bnkhd->bnqhgd", probs.astype(v.dtype), vb)
    return out.reshape(b, s, ATTN_WIDTH)

def causal_depthwise_conv(x, w, bias):
    out = lax.conv_general_dilated(
        x, w[:, None, :].astype(x.dtype), window_strides=(1,), padding=[(CONV_WIDTH - 1, 0)],
        dimension_numbers=("NWC", "WIO", "NWC"), feature_group_count=x.shape[-1])
    return out + bias

def ssd_chunked(xs, dt, a, bm, cm):
    b, s = xs.shape[0], xs.shape[1]
    nc = s // CHUNK
    G, R, P, N = SSM_GROUPS, SSM_HEADS_PER_GROUP, SSM_HEAD_DIM, SSM_STATE
    xs = xs.reshape(b, nc, CHUNK, G, R, P).astype(jnp.float32)
    dt = dt.reshape(b, nc, CHUNK, G, R)
    bm = bm.reshape(b, nc, CHUNK, G, N).astype(jnp.float32)
    cm = cm.reshape(b, nc, CHUNK, G, N).astype(jnp.float32)
    a_cum = jnp.cumsum(dt * a, axis=2)
    xdt = xs * dt[..., None]
    causal = jnp.tril(jnp.ones((CHUNK, CHUNK), dtype=bool))[:, :, None, None]
    seg = a_cum[:, :, :, None] - a_cum[:, :, None, :]
    decay = jnp.exp(jnp.where(causal, seg, -jnp.inf))
    cb = jnp.einsum("bclgn,bcsgn->bclsg", cm, bm)
    y_diag = jnp.einsum("bclsg,bclsgr,bcsgrp->bclgrp", cb, decay, xdt)
    decay_to_end = jnp.exp(a_cum[:, :, -1:] - a_cum)
    states = jnp.einsum("bclgn,bclgr,bclgrp->bcgrpn", bm, decay_to_end, xdt)
    chunk_decay = jnp.exp(a_cum[:, :, -1])

    def step(h, inp):
        st, dec = inp
        return h * dec[..., None, None] + st, h

    h0 = jnp.zeros((b, G, R, P, N), jnp.float32)
    _, h_prev = lax.scan(step, h0, (jnp.moveaxis(states, 1, 0), jnp.moveaxis(chunk_decay, 1, 0)))
    h_prev = jnp.moveaxis(h_prev, 0, 1)
    y_off = jnp.einsum("bclgn,bcgrpn,bclgr->bclgrp", cm, h_prev, jnp.exp(a_cum))
    return (y_diag + y_off).reshape(b, s, G, R, P)

def hybrid_layer(x, c, w_ada, b_ada, norm_w, w_in, q_norm_w, k_norm_w, rel_bias, sinks,
                 conv_w, conv_b, dt_bias, a_log, d_skip, ssm_norm_w,
                 w_attn_proj, w_ssm_proj, w_out):
    b, s, _ = x.shape
    G, R, P, N = SSM_GROUPS, SSM_HEADS_PER_GROUP, SSM_HEAD_DIM, SSM_STATE
    mod = jax.nn.silu(c) @ w_ada + b_ada
    shift, scale, gate = jnp.split(mod, 3, axis=-1)
    h = rms_norm(x, norm_w) * (1 + scale[:, None]) + shift[:, None]
    proj = h @ w_in
    widths = [ATTN_WIDTH, KV_WIDTH, KV_WIDTH, ATTN_WIDTH, SSM_WIDTH, XBC_WIDTH, SSM_HEADS, D_MODEL, D_MODEL]
    q, k, v, z_a, z_m, xbc, dt_raw, g_a, g_b = jnp.split(proj, list(np.cumsum(widths)[:-1]), axis=-1)

    y_a = sliding_window_attention(q.reshape(b, s, ATTN_HEADS, HEAD_DIM),
                                   k.reshape(b, s, ATTN_KV_HEADS, HEAD_DIM),
                                   v.reshape(b, s, ATTN_KV_HEADS, HEAD_DIM),
                                   q_norm_w, k_norm_w, rel_bias, sinks)
    y_a = (y_a * jax.nn.silu(z_a)) @ w_attn_proj

    xbc = jax.nn.silu(causal_depthwise_conv(xbc, conv_w, conv_b))
    xs, bm, cm = jnp.split(xbc, [SSM_WIDTH, SSM_WIDTH + G * N], axis=-1)
    xs = xs.reshape(b, s, G, R, P)
    dt = jax.nn.softplus((dt_raw + dt_bias).astype(jnp.float32)).reshape(b, s, G, R)
    a = -jnp.exp(a_log.astype(jnp.float32)).reshape(G, R)
    y = ssd_chunked(xs, dt, a, bm.reshape(b, s, G, N), cm.reshape(b, s, G, N))
    y = y + d_skip.astype(jnp.float32).reshape(G, R)[:, :, None] * xs.astype(jnp.float32)
    y = y.reshape(b, s, SSM_WIDTH).astype(x.dtype) * jax.nn.silu(z_m)
    y = rms_norm(y.reshape(b, s, G, SSM_WIDTH // G), ssm_norm_w.reshape(G, SSM_WIDTH // G))
    y_b = y.reshape(b, s, SSM_WIDTH) @ w_ssm_proj

    merged = jax.nn.sigmoid(g_a) * y_a + jax.nn.sigmoid(g_b) * y_b
    return x + gate[:, None] * (merged @ w_out)

def setup_inputs(seed: int = 0) -> dict:
    key = jax.random.key(seed)
    ks = jax.random.split(key, 20)
    nrm = jax.random.normal
    L, D = DEPTH, D_MODEL
    dt0 = jnp.exp(jax.random.uniform(ks[12], (L, SSM_HEADS)) * (math.log(DT_MAX) - math.log(DT_MIN)) + math.log(DT_MIN))
    return {
        "x": nrm(ks[0], (BATCH, SEQ, D), jnp.float32),
        "c": nrm(ks[1], (BATCH, D), jnp.float32),
        "w_ada": nrm(ks[2], (L, D, 3 * D)) * (0.5 * D ** -0.5),
        "b_ada": 0.01 * nrm(ks[3], (L, 3 * D)),
        "norm_w": 1 + 0.02 * nrm(ks[4], (L, D)),
        "w_in": nrm(ks[5], (L, D, IN_WIDTH)) * D ** -0.5,
        "q_norm_w": 1 + 0.02 * nrm(ks[6], (L, HEAD_DIM)),
        "k_norm_w": 1 + 0.02 * nrm(ks[7], (L, HEAD_DIM)),
        "rel_bias": 0.5 * nrm(ks[8], (REL_BUCKETS, ATTN_HEADS)),
        "sinks": 0.5 * nrm(ks[9], (L, ATTN_HEADS)),
        "conv_w": nrm(ks[10], (L, CONV_WIDTH, XBC_WIDTH)) * CONV_WIDTH ** -0.5,
        "conv_b": 0.01 * nrm(ks[11], (L, XBC_WIDTH)),
        "dt_bias": dt0 + jnp.log(-jnp.expm1(-dt0)),
        "a_log": jnp.log(jax.random.uniform(ks[13], (L, SSM_HEADS), minval=1.0, maxval=16.0)),
        "d_skip": 1 + 0.1 * nrm(ks[14], (L, SSM_HEADS)),
        "ssm_norm_w": 1 + 0.02 * nrm(ks[15], (L, SSM_WIDTH)),
        "w_attn_proj": nrm(ks[16], (L, ATTN_WIDTH, D)) * ATTN_WIDTH ** -0.5,
        "w_ssm_proj": nrm(ks[17], (L, SSM_WIDTH, D)) * SSM_WIDTH ** -0.5,
        "w_out": nrm(ks[18], (L, D, D)) * D ** -0.5,
    }

def reference(x, c, w_ada, b_ada, norm_w, w_in, q_norm_w, k_norm_w, rel_bias, sinks,
              conv_w, conv_b, dt_bias, a_log, d_skip, ssm_norm_w,
              w_attn_proj, w_ssm_proj, w_out):
    for i in range(DEPTH):
        x = hybrid_layer(x, c, w_ada[i], b_ada[i], norm_w[i], w_in[i], q_norm_w[i], k_norm_w[i],
                         rel_bias, sinks[i], conv_w[i], conv_b[i], dt_bias[i], a_log[i], d_skip[i],
                         ssm_norm_w[i], w_attn_proj[i], w_ssm_proj[i], w_out[i])
    return x


_drawn_inputs = setup_inputs


def setup_inputs(seed=0):
    import zlib

    import numpy as np

    out = dict(_drawn_inputs(seed))
    spreads = {}
    factors = {'b_ada': 8.0,
     'norm_w': 8.0,
     'q_norm_w': 8.0,
     'k_norm_w': 8.0,
     'rel_bias': 7.942,
     'sinks': 200.0,
     'conv_b': 64.0,
     'd_skip': 200.0,
     'ssm_norm_w': 200.0}
    for name, (base, spread) in spreads.items():
        noise = np.random.default_rng([zlib.crc32(name.encode()), seed]).standard_normal(out[name].shape)
        drawn = base * np.exp(spread * noise) if base else spread * noise
        out[name] = __import__('jax').numpy.asarray(drawn.astype(out[name].dtype))
    for name, factor in factors.items():
        out[name] = (out[name] * factor).astype(out[name].dtype)
    return out
```

```python
import math
from contextlib import ExitStack

import numpy as np
import concourse.bass as bass
from concourse import mybir

F32, F32R, U32 = mybir.dt.float32, mybir.dt.float32r, mybir.dt.uint32
ALU, ACT, AX = mybir.AluOpType, mybir.ActivationFunctionType, mybir.AxisListType.X

P = 128
D = 1024
S = 2048
KT = D // P
H, KV, HD = 16, 4, 64
GRP = H // KV
SW, SH, SG, SN = 2048, 32, 4, 128
R = SH // SG
CW = 4
NBLK = S // P
EPS = 1e-6
NEG = -1e30
BUCKETS, MAXDIST = 32, 128
MM = 512

C_Q = 0
C_K = C_Q + H * HD
C_V = C_K + KV * HD
C_ZA = C_V + KV * HD
C_ZM = C_ZA + H * HD
C_XBC = C_ZM + SW
XBC = SW + 2 * SG * SN
C_DT = C_XBC + XBC
C_G = C_DT + SH

KINDS = [("plain", C_DT, 1, "dt"), ("plain", C_V, 2, "v"), ("norm", C_K, 2, "k"), ("norm", C_Q, 8, "q"),
         ("silu", C_ZA, 8, "za"), ("silu", C_ZM, 16, "zm"), ("conv", C_XBC, 24, "xbc"), ("gate", C_G, 16, "g")]
NTILES = sum(k[2] for k in KINDS)


def bucket_onehot():
    n = (127 - np.arange(2 * P)) % P
    exact = BUCKETS // 2
    nf = np.maximum(n, 1).astype(np.float32)
    large = exact + (np.log(nf / np.float32(exact)) / np.float32(math.log(MAXDIST / exact))
                     * np.float32(BUCKETS - exact)).astype(np.int32)
    b = np.where(n < exact, n, np.minimum(large, BUCKETS - 1))
    return (b[None, :] == np.arange(BUCKETS)[:, None]).astype(np.float32)


def exists(n):
    return not isinstance(n, int) or n >= 0


def pairs(eng, count, body):
    for b in range(2):
        body(b, b, 0)
    with eng.Fori(1, count // 2) as i:
        for b in range(2):
            body(2 * i + b, b, i)


def dram_ap(t, offset, ap):
    return bass.AP(tensor=t.tensor, offset=offset, ap=ap)


def build(nc, a, out):
    scratch = {n: nc.dram_tensor("scr_" + n, (c * P, S), F32, kind="Internal").ap()
               for _, _, c, n in KINDS}
    scratch["attn"] = nc.dram_tensor("scr_attn", (D, S), F32, kind="Internal").ap()
    scratch["y"] = nc.dram_tensor("scr_y", (SW, S), F32, kind="Internal").ap()
    scratch["m"] = nc.dram_tensor("scr_m", (D, S), F32, kind="Internal").ap()
    scratch["rowcum"] = nc.dram_tensor("scr_rowcum", (NBLK * SH, P), F32, kind="Internal").ap()
    scratch["bias"] = nc.dram_tensor("scr_bias", (H, 2 * P), F32, kind="Internal").ap()
    with ExitStack() as ctx:
        def sb(n, s, d=F32):
            return ctx.enter_context(nc.sbuf_tensor(n, s, d))
        k = dict(
            ident=sb("ident", [P, P]), ones=sb("ones", [P, P]), headones=sb("headones", [P, P]),
            triu=sb("triu", [P, P]), tril=sb("tril", [P, P]), neg=sb("neg", [P, P]),
            negcur=sb("negcur", [P, P]),
            bias=sb("bias", [P, H, P]), sink=sb("sink", [P, H]),
            hscale=sb("hscale", [P, KT]), hshift=sb("hshift", [P, KT]), gate=sb("gate", [P, KT]),
            qw=sb("qw", [P, 1]), kw=sb("kw", [P, 1]), convw=sb("convw", [P, CW, XBC // P]),
            convb=sb("convb", [P, XBC // P]), dskip=sb("dskip", [P, SW // P]), ssmw=sb("ssmw", [P, SW // P]),
            dtb=sb("dtb", [SH, 1]), aneg=sb("aneg", [P, SH]), eps=sb("eps", [P, 1]),
        )
        setup(nc, a, scratch, k)
        with ExitStack() as hctx:
            h = [hctx.enter_context(nc.sbuf_tensor(n, [P, KT, S], F32R)) for n in ("h_hi", "h_lo")]
            normalise(nc, a, k, h)
            project(nc, a, scratch, k, h)
        with ExitStack() as dctx:
            dec = {n: dctx.enter_context(nc.sbuf_tensor("dec_" + n, [P, NBLK * SH], F32))
                   for n in ("dt", "cum", "dtend", "chunk")}
            decays(nc, scratch, k, dec)
            attention(nc, scratch, k)
            ssd(nc, scratch, k, dec)
        merge(nc, a, scratch, k, out)


class Stage:

    def __init__(self, nc, name):
        self.nc, self.name, self.ctx = nc, name, ExitStack()

    def __enter__(self):
        return self

    def __exit__(self, *e):
        return self.ctx.__exit__(*e)

    def sb(self, n, s, d=F32):
        return self.ctx.enter_context(self.nc.sbuf_tensor(f"{self.name}_{n}", s, d))

    def ps(self, n, s):
        return self.ctx.enter_context(self.nc.psum_tensor(f"{self.name}_psum_{n}", s, F32))

    def sem(self, n):
        return self.ctx.enter_context(self.nc.semaphore(f"{self.name}_{n}"))

    def block(self):
        return self.ctx.enter_context(self.nc.Block())


def setup(nc, a, scratch, k):
    with Stage(nc, "setup") as st:
        W3 = 3 * D
        wada = st.sb("wada", [P, 2, W3])
        acc = st.sb("acc", [P, W3])
        ccol = st.sb("ccol", [P, KT]); chalf = st.sb("chalf", [P, KT]); ctan = st.sb("ctan", [P, KT])
        bada = st.sb("bada", [P, 3 * KT]); mod = st.sb("mod", [P, 3 * KT]); nw = st.sb("nw", [P, KT])
        onehot = st.sb("onehot", [BUCKETS, 2 * P]); rel = st.sb("rel", [BUCKETS, H]); brow = st.sb("brow", [H, 2 * P])
        al = st.sb("al", [P, SH]); cw = st.sb("cw", [P, CW, XBC // P]); cb = st.sb("cb", [P, XBC // P])
        qk = st.sb("qk", [P, 2]); flip = st.sb("flip", [P, P]); skew = st.sb("skew", [P, H, P])
        pm = st.ps("mod", [P, 512]); pb = st.ps("bias", [H, 2 * P]); pf = st.ps("flipped", [P, H, P])
        small, onesem, wsem = st.sem("small_loaded"), st.sem("bias_in_loaded"), [st.sem("wada0_loaded"), st.sem("wada1_loaded")]
        consts = st.sem("consts_made")
        ctanh, silu, accd, modp, brp, brs, bst, bld, fin, al_e, chd, modd = [st.sem(n) for n in (
            "c_tanh", "c_silu", "ada_accumulated", "mod_product", "bias_rows_product", "bias_rows_copied",
            "bias_rows_stored", "skew_loaded", "columns_made", "a_exponential", "c_halved", "mod_made")]
        flipped, bias_made = st.sem("bias_flipped"), st.sem("bias_made")
        half = P // 2
        blk = st.block()
        NSMALL, CONSTS = 11, 17

        @blk.sync
        def _(sp):
            sp.dma_start(ccol[:, :], a["c"]).then_inc(small, 16)
            for j in range(KT):
                if j >= 2:
                    sp.wait_ge(accd, j - 1)
                sp.dma_start(wada[:, j % 2, :], a["w_ada"][0, j * P:(j + 1) * P, :]).then_inc(wsem[j % 2], 16)

        @blk.scalar
        def _(act):
            act.dma_start(onehot[:, :], a["onehot"]).then_inc(onesem, 16)
            act.dma_start(rel[:, :], a["rel_bias"]).then_inc(onesem, 16)
            n = 0
            for dst, src in (
                (bada[:, :], a["b_ada"]),
                (nw[:, :], a["norm_w"]),
                (cb[:, :], a["conv_b"]),
                (k["ssmw"][:, :], a["ssm_norm_w"]),
                (qk[:, 0:1], a["q_norm_w"]),
                (qk[:, 1:2], a["k_norm_w"]),
                (k["dtb"][:, :], a["dt_bias"]),
                (k["sink"][:, :], a["sinks"].to_broadcast([P, H])),
                (al[:, :], a["a_log"].to_broadcast([P, SH])),
                (k["dskip"][:, :], a["d_skip"]),
                (cw[:, :, :], a["conv_w"]),
            ):
                act.dma_start(dst, src).then_inc(small, 16)
                n += 1
            assert n == NSMALL
            act.wait_ge(chd, 1)
            nc.scalar.activation(ctan[:, :], chalf[:, :], ACT.Tanh).then_inc(ctanh, 1)
            nc.scalar.activation(al[:, :], al[:, :], ACT.Exp).then_inc(al_e, 1)
            act.wait_ge(brs, 1)
            act.dma_start(scratch["bias"], brow[:, :]).then_inc(bst, 16)
            act.wait_ge(bst, 16)
            act.dma_start(skew[:, :, :], dram_ap(scratch["bias"], 0, [[1, P], [2 * P, H], [1, P]])).then_inc(bld, 16)
            act.wait_ge(flipped, 1)
            nc.scalar.activation(k["bias"][:, :, :], pf[:, :, :], ACT.Copy).then_inc(bias_made, 1)
            act.wait_ge(bias_made, 1)

        @blk.gpsimd
        def _(pool):
            made = [0]

            def const(ins):
                made[0] += 1
                ins.then_inc(consts, 1)
                pool.wait_ge(consts, made[0])

            def select(t, keep, coefficients, fill):
                base, part, col = coefficients
                const(nc.gpsimd.affine_select(out=t[:, :], in_=t[:, :], compare_op=keep, fill=fill, base=base,
                                              pattern=[[col, P]], channel_multiplier=part))

            const(pool.memset(k["eps"][:, :], EPS))
            const(pool.memset(flip[:, :], 0.0))
            select(flip, ALU.not_equal, (1 - P, 1, 1), 1.0)
            const(pool.memset(k["ones"][:, :], 1.0))
            const(pool.memset(k["ident"][:, :], 0.0))
            select(k["ident"], ALU.not_equal, (0, 1, -1), 1.0)
            const(pool.memset(k["triu"][:, :], 1.0))
            select(k["triu"], ALU.is_ge, (0, -1, 1), 0.0)
            const(pool.memset(k["tril"][:, :], 1.0))
            select(k["tril"], ALU.is_gt, (0, 1, -1), 0.0)
            const(pool.memset(k["neg"][:, :], 0.0))
            select(k["neg"], ALU.is_ge, (0, 1, -1), NEG)
            const(pool.memset(k["negcur"][:, :], NEG))
            select(k["negcur"], ALU.is_ge, (0, 1, -1), 0.0)
            const(pool.memset(k["headones"][:, :], 0.0))
            for hh in range(P // HD):
                const(pool.memset(k["headones"][hh * HD:(hh + 1) * HD, hh * HD:(hh + 1) * HD], 1.0))
            assert made[0] == CONSTS

        @blk.tensor
        def _(pe):
            pe.wait_ge(onesem, 32)
            nc.tensor.matmul(pb[:, :], rel[:, :], onehot[:, :], start=True, stop=True).then_inc(brp, 1)
            pe.wait_ge(bld, 16)
            pe.wait_ge(consts, CONSTS)
            for g in range(H * P // MM):
                hs = slice(g * MM // P, (g + 1) * MM // P)
                last = nc.tensor.matmul(pf[:, hs, :], flip[:, :], skew[:, hs, :], start=True, stop=True)
            last.then_inc(flipped, 1)
            pe.wait_ge(accd, KT)
            for m in range(3 * KT):
                last = nc.tensor.matmul(pm[:, m:m + 1], acc[:, m * P:(m + 1) * P], k["ones"][:, 0:1], start=True, stop=True)
            last.then_inc(modp, 1)

        @blk.vector
        def _(dve):
            dve.wait_ge(small, 16 * (NSMALL + 1))
            nc.vector.tensor_scalar(chalf[:, :], ccol[:, :], 0.5, None, ALU.mult).then_inc(chd, 1)
            dve.wait_ge(ctanh, 1)
            nc.vector.scalar_tensor_tensor(chalf[:, :], ctan[:, :], 1.0, chalf[:, :], ALU.add, ALU.mult).then_inc(silu, 1)
            dve.wait_ge(brp, 1)
            nc.vector.tensor_copy(brow[:, :], pb[:, :]).then_inc(brs, 1)
            dve.wait_ge(silu, 1)
            for j in range(KT):
                dve.wait_ge(wsem[j % 2], 16 * (j // 2 + 1))
                if j == 0:
                    nc.vector.tensor_scalar(acc[:, :], wada[:, 0, :], chalf[:, 0:1], None, ALU.mult).then_inc(accd, 1)
                else:
                    dve.wait_ge(accd, j)
                    nc.vector.scalar_tensor_tensor(acc[:, :], wada[:, j % 2, :], chalf[:, j:j + 1], acc[:, :],
                                                   ALU.mult, ALU.add).then_inc(accd, 1)
            nc.vector.tensor_scalar(k["convw"][:, :, :], cw[:, :, :], 0.5, None, ALU.mult)
            nc.vector.tensor_scalar(k["convb"][:, :], cb[:, :], 0.5, None, ALU.mult)
            nc.vector.tensor_scalar(k["qw"][:, :], qk[:, 0:1], HD ** -0.5, None, ALU.mult)
            nc.vector.tensor_copy(k["kw"][:, :], qk[:, 1:2])
            dve.wait_ge(al_e, 1)
            nc.vector.tensor_scalar(k["aneg"][:, :], al[:, :], -1.0, None, ALU.mult)
            dve.wait_ge(modp, 1)
            nc.vector.tensor_tensor(mod[:, :], pm[:, 0:3 * KT], bada[:, :], ALU.add).then_inc(modd, 1)
            dve.wait_ge(modd, 1)
            nc.vector.tensor_copy(k["hshift"][:, :], mod[:, 0:KT])
            nc.vector.scalar_tensor_tensor(k["hscale"][:, :], mod[:, KT:2 * KT], 1.0, nw[:, :], ALU.add, ALU.mult)
            nc.vector.tensor_scalar(k["gate"][:, :], mod[:, 2 * KT:3 * KT], 0.5, None, ALU.mult).then_inc(fin, 1)
            dve.wait_ge(fin, 1)


def normalise(nc, a, k, h):
    h_hi, h_lo = h
    with Stage(nc, "norm") as st:
        x = st.sb("x", [P, 2, D]); xn = st.sb("xn", [P, 2, D]); h32 = st.sb("h32", [P, 2, D])
        ss = st.sb("ss", [P, 2]); root = st.sb("root", [P, 2]); rstd = st.sb("rstd", [P, 2])
        tp = st.ps("tp", [P, 2, D])
        x_loaded = [st.sem("x0_loaded"), st.sem("x1_loaded")]
        squares, rooted, rstd_made, x_normed, transposed, scaled, h_made, hi_made, lo_made = [st.sem(n) for n in (
            "squares", "rooted", "rstd_made", "x_normed", "transposed", "scaled", "h_made", "hi_made", "lo_made")]
        blk = st.block()

        @blk.sync
        def _(sp):
            def load(t, b, j):
                if exists(t - 2):
                    sp.wait_ge(x_normed, t - 1)
                sp.dma_start(x[:, b, :], a["x"][0, bass.ds(t * P, P), :]).then_inc(x_loaded[b], 16)
            pairs(sp, NBLK, load)

        @blk.scalar
        def _(act):
            def norm(t, b, j):
                act.wait_ge(x_loaded[b], 16 * j + 16)
                if exists(t - 2):
                    act.wait_ge(transposed, t - 1)
                nc.scalar.activation(xn[:, b, :], x[:, b, :], ACT.Square, accum_out=ss[:, b:b + 1]).then_inc(squares, 1)
                act.wait_ge(squares, t + 1)
                nc.scalar.activation(root[:, b:b + 1], ss[:, b:b + 1], ACT.Sqrt, bias=k["eps"][:, :], scale=1.0 / D).then_inc(rooted, 1)
                act.wait_ge(rstd_made, t + 1)
                nc.scalar.activation(xn[:, b, :], x[:, b, :], ACT.Copy, scale=rstd[:, b:b + 1]).then_inc(x_normed, 1)
                act.wait_ge(h_made, t + 1)
                nc.scalar.activation(h_hi[:, :, bass.ds(t * P, P)],
                                     h32[:, b, :].rearrange("p (k t) -> p k t", k=KT), ACT.Copy).then_inc(hi_made, 1)
            pairs(act, NBLK, norm)

        @blk.tensor
        def _(pe):
            def turn(t, b, j):
                pe.wait_ge(x_normed, t + 1)
                if exists(t - 2):
                    pe.wait_ge(scaled, t - 1)
                for kk in range(KT):
                    last = nc.tensor.transpose(tp[:, b, kk * P:(kk + 1) * P], xn[:, b, kk * P:(kk + 1) * P], k["ident"][:, :])
                last.then_inc(transposed, 1)
            pairs(pe, NBLK, turn)

        @blk.vector
        def _(dve):
            def split(t, b, j):
                dve.wait_ge(rooted, t + 1)
                nc.vector.reciprocal(rstd[:, b:b + 1], root[:, b:b + 1]).then_inc(rstd_made, 1)
                dve.wait_ge(transposed, t + 1)
                hv = h32[:, b, :].rearrange("p (k t) -> p k t", k=KT)
                nc.vector.tensor_tensor(hv, tp[:, b, :].rearrange("p (k t) -> p k t", k=KT),
                                        k["hscale"][:, :, None].to_broadcast([P, KT, P]), ALU.mult).then_inc(scaled, 1)
                dve.wait_ge(scaled, t + 1)
                nc.vector.tensor_tensor(hv, hv, k["hshift"][:, :, None].to_broadcast([P, KT, P]), ALU.add).then_inc(h_made, 1)
                dve.wait_ge(hi_made, t + 1)
                nc.vector.tensor_tensor(h_lo[:, :, bass.ds(t * P, P)], hv, h_hi[:, :, bass.ds(t * P, P)],
                                        ALU.subtract).then_inc(lo_made, 1)
            pairs(dve, NBLK, split)
            dve.wait_ge(lo_made, NBLK)


def project(nc, a, scratch, k, h):
    h_hi, h_lo = h
    with Stage(nc, "proj") as st:
        raw = st.sb("raw", [P, 2, KT, P])
        w_hi = [st.sb(f"w_hi{b}", [P, KT, P], F32R) for b in range(2)]
        w_lo = [st.sb(f"w_lo{b}", [P, KT, P], F32R) for b in range(2)]
        xin = st.sb("xin", [P, CW - 1 + S]); u = st.sb("u", [P, S]); res = st.sb("res", [P, 2, S])
        acc = st.ps("acc", [P, 2, S])
        w_loaded = [st.sem("w0_loaded"), st.sem("w1_loaded")]
        stored = [st.sem("res0_stored"), st.sem("res1_stored")]
        hi_made, lo_made, multiplied, squared, summed, res_begun, tapped, u_made, inverted, res_made, padded = [
            st.sem(n) for n in ("hi_made", "lo_made", "multiplied", "squared", "summed", "res_begun",
                                "tapped", "u_made", "inverted", "res_made", "padded")]
        blk = st.block()

        def tiles(eng, body):
            n0 = 0
            for kind, col, count, name in KINDS:
                last = n0 + count == NTILES
                looped = 0 if kind == "plain" else (count - 2 if last else count)
                if looped:
                    with eng.Fori(0, looped // 2) as i:
                        for e in range(2):
                            body(2 * i + (n0 + e), (n0 + e) % 2, i + (n0 + e) // 2, kind, col, name, 2 * i + e)
                for e in range(looped, count):
                    body(n0 + e, (n0 + e) % 2, (n0 + e) // 2, kind, col, name, e)
                n0 += count

        before = {}
        for kind, _, count, name in KINDS:
            before[name] = sum(c for kk, _, c, nm in KINDS[:[x[3] for x in KINDS].index(name)] if kk == kind)

        @blk.sync
        def _(sp):
            def load(n, b, j, kind, col, name, e):
                if exists(n - 2):
                    sp.wait_ge(lo_made, n - 1)
                sp.dma_start(raw[:, b, :, :], a["w_in_" + name][bass.ds(e, 1)].rearrange("o p k c -> (o p) k c")).then_inc(w_loaded[b], 16)
            tiles(sp, load)

        @blk.tensor
        def _(pe):
            def product(n, b, j, kind, col, name, e):
                pe.wait_ge(lo_made, n + 1)
                if exists(n - 2):
                    pe.wait_ge(u_made, n - 1)
                for kk in range(KT):
                    for step, (wv, hv) in enumerate(((w_hi[b], h_hi), (w_hi[b], h_lo), (w_lo[b], h_hi))):
                        for c in range(S // MM):
                            last = nc.tensor.matmul(acc[:, b, c * MM:(c + 1) * MM], wv[:, kk, :], hv[:, kk, c * MM:(c + 1) * MM],
                                                    start=(kk == 0 and step == 0), stop=(kk == KT - 1 and step == 2))
                last.then_inc(multiplied, 1)
                if kind == "norm":
                    pe.wait_ge(squared, e + (before[name] + 1))
                    for c in range(S // MM):
                        last = nc.tensor.matmul(acc[:, b, c * MM:(c + 1) * MM], k["headones"][:, :], u[:, c * MM:(c + 1) * MM],
                                                start=True, stop=True)
                    last.then_inc(summed, 1)
            tiles(pe, product)

        @blk.scalar
        def _(act):
            def high(b, j):
                act.wait_ge(w_loaded[b], 16 * j + 16)
                nc.scalar.activation(w_hi[b][:, :, :], raw[:, b, :, :], ACT.Copy).then_inc(hi_made, 1)

            def finish(n, b, j, kind, col, name, e):
                if not (isinstance(n, int) and n == NTILES - 1):
                    high(1 - b, j + b)
                if exists(n - 2):
                    act.wait_ge(stored[b], 16 * j)
                act.wait_ge(multiplied, n + 1)
                src = acc[:, b, :]
                if kind == "plain":
                    nc.scalar.activation(u[:, :], src, ACT.Copy).then_inc(u_made, 1)
                elif kind == "gate":
                    nc.scalar.activation(u[:, :], src, ACT.Tanh, scale=0.5).then_inc(u_made, 1)
                elif kind == "silu":
                    nc.scalar.activation(res[:, b, :], src, ACT.Copy, scale=0.5).then_inc(res_begun, 1)
                    nc.scalar.activation(u[:, :], src, ACT.Tanh, scale=0.5).then_inc(u_made, 1)
                elif kind == "conv":
                    nc.scalar.activation(xin[:, CW - 1:], src, ACT.Copy)
                    nc.scalar.activation(res[:, b, :], src, ACT.Identity, bias=k["convb"][:, bass.ds(e, 1)],
                                         scale=k["convw"][:, CW - 1, bass.ds(e, 1)]).then_inc(res_begun, 1)
                    act.wait_ge(tapped, 3 * e + 3)
                    nc.scalar.activation(u[:, :], res[:, b, :], ACT.Tanh).then_inc(u_made, 1)
                elif kind == "norm":
                    nc.scalar.activation(res[:, b, :], src, ACT.Copy).then_inc(res_begun, 1)
                    nc.scalar.activation(u[:, :], src, ACT.Square).then_inc(squared, 1)
                    act.wait_ge(summed, e + (before[name] + 1))
                    nc.scalar.activation(u[:, :], src, ACT.Sqrt, bias=k["eps"][:, :], scale=1.0 / HD).then_inc(u_made, 1)
                act.wait_ge(res_made, n + 1)
                act.dma_start(scratch[name][bass.ds(e * P, P), :], res[:, b, :]).then_inc(stored[b], 16)

            high(0, 0)
            tiles(act, finish)
            for b in range(2):
                act.wait_ge(stored[b], 16 * ((NTILES + 1 - b) // 2))

        @blk.vector
        def _(dve):
            def low(n, b):
                dve.wait_ge(hi_made, n + 1)
                if exists(n - 2):
                    dve.wait_ge(multiplied, n - 1)
                nc.vector.tensor_tensor(w_lo[b][:, :, :], raw[:, b, :, :], w_hi[b][:, :, :], ALU.subtract).then_inc(lo_made, 1)

            def finish(n, b, j, kind, col, name, e):
                if not (isinstance(n, int) and n == NTILES - 1):
                    low(n + 1, 1 - b)
                if kind == "conv":
                    for c in range(CW - 1):
                        if c == 0:
                            dve.wait_ge(res_begun, e + 1 + BEGUN[name])
                        else:
                            dve.wait_ge(tapped, 3 * e + c)
                        nc.vector.scalar_tensor_tensor(res[:, b, :], xin[:, c:c + S], k["convw"][:, c, bass.ds(e, 1)],
                                                       res[:, b, :], ALU.mult, ALU.add).then_inc(tapped, 1)
                dve.wait_ge(u_made, n + 1)
                if kind == "plain":
                    nc.vector.tensor_copy(res[:, b, :], u[:, :]).then_inc(res_made, 1)
                elif kind == "gate":
                    nc.vector.tensor_scalar(res[:, b, :], u[:, :], 1.0, None, ALU.add).then_inc(res_made, 1)
                elif kind in ("silu", "conv"):
                    nc.vector.scalar_tensor_tensor(res[:, b, :], u[:, :], 1.0, res[:, b, :], ALU.add, ALU.mult).then_inc(res_made, 1)
                elif kind == "norm":
                    nc.vector.reciprocal(u[:, :], u[:, :]).then_inc(inverted, 1)
                    dve.wait_ge(inverted, e + (before[name] + 1))
                    nc.vector.scalar_tensor_tensor(res[:, b, :], res[:, b, :], k[name + "w"][:, :], u[:, :],
                                                   ALU.mult, ALU.mult).then_inc(res_made, 1)

            order = [x for x in KINDS if x[0] in ("norm", "silu", "conv")]
            BEGUN = {x[3]: sum(y[2] for y in order[:i]) for i, x in enumerate(order)}
            dve.memset(xin[:, 0:CW - 1], 0.0).then_inc(padded, 1)
            dve.wait_ge(padded, 1)
            low(0, 0)
            tiles(dve, finish)
            dve.wait_ge(res_made, NTILES)


def decays(nc, scratch, k, dec):
    NCH = NBLK * SH
    TERMS = 8
    with Stage(nc, "decay") as st:
        dtt = st.sb("dtt", [SH, S]); x = st.sb("x", [P, NCH]); u = st.sb("u", [P, NCH]); v = st.sb("v", [P, NCH])
        w = st.sb("w", [P, NCH]); rows = st.sb("rows", [P, 4, P]); dta = st.sb("dta", [P, NCH])
        pt = st.ps("pt", [P, NCH]); pc = st.ps("pc", [P, NCH]); pe_ = st.ps("pe", [P, NCH]); pr = st.ps("pr", [P, 4, P])
        loaded, biased, turned, cumulated, v1, a1, stored, done = [st.sem(n) for n in (
            "loaded", "biased", "turned", "cumulated", "vector_step", "scalar_step", "rows_stored", "done")]
        blk = st.block()

        @blk.sync
        def _(sp):
            sp.dma_start(dtt[:, :], scratch["dt"][0:SH, :]).then_inc(loaded, 16)
            sp.wait_ge(done, 1)
            sp.dma_start(scratch["rowcum"].rearrange("(m p) l -> p m l", p=P), rows[:, :, :]).then_inc(stored, 16)
            sp.wait_ge(stored, 16)

        @blk.tensor
        def _(pe):
            pe.wait_ge(biased, 1)
            for c in range(NBLK):
                last = nc.tensor.transpose(pt[:, c * SH:(c + 1) * SH], dtt[:, c * P:(c + 1) * P], k["ident"][0:SH, 0:SH])
            last.then_inc(turned, 1)
            pe.wait_ge(cumulated, 1)
            nc.tensor.matmul(pc[:, :], k["triu"][:, :], dta[:, :], start=True, stop=True)
            nc.tensor.matmul(pe_[:, :], k["ones"][:, :], dta[:, :], start=True, stop=True)
            for m in range(4):
                last = nc.tensor.matmul(pr[:, m, :], dta[:, m * P:(m + 1) * P], k["triu"][:, :], start=True, stop=True)
            last.then_inc(turned, 1)

        @blk.scalar
        def _(act):
            act.wait_ge(v1, 2)
            nc.scalar.activation(u[:, :], u[:, :], ACT.Exp, scale=-1.0).then_inc(a1, 1)
            act.wait_ge(turned, 2)
            nc.scalar.activation(dec["chunk"][:, :], pe_[:, :], ACT.Exp).then_inc(a1, 1)
            act.wait_ge(v1, 3 + 4 + TERMS + 3)
            nc.scalar.activation(w[:, :], w[:, :], ACT.Exp).then_inc(a1, 1)
            act.wait_ge(a1, 3)

        @blk.vector
        def _(dve):
            dve.wait_ge(loaded, 16)
            nc.vector.tensor_scalar(dtt[:, :], dtt[:, :], k["dtb"][:, :], None, ALU.add).then_inc(biased, 1)
            dve.wait_ge(turned, 1)
            step = [0]

            def chain(ins):
                step[0] += 1
                ins.then_inc(v1, 1)
                dve.wait_ge(v1, step[0])

            chain(nc.vector.tensor_copy(x[:, :], pt[:, :]))
            chain(nc.vector.scalar_tensor_tensor(u[:, :], x[:, :], -1.0, x[:, :], ALU.mult, ALU.max))
            dve.wait_ge(a1, 1)
            chain(nc.vector.tensor_scalar(v[:, :], u[:, :], 2.0, None, ALU.add))
            chain(nc.vector.reciprocal(v[:, :], v[:, :]))
            chain(nc.vector.tensor_tensor(u[:, :], u[:, :], v[:, :], ALU.mult))
            chain(nc.vector.tensor_tensor(v[:, :], u[:, :], u[:, :], ALU.mult))
            chain(nc.vector.tensor_scalar(w[:, :], v[:, :], 1.0 / (2 * TERMS + 1), None, ALU.mult))
            for n in range(TERMS - 1, 0, -1):
                chain(nc.vector.scalar_tensor_tensor(w[:, :], w[:, :], 1.0 / (2 * n + 1), v[:, :], ALU.add, ALU.mult))
            chain(nc.vector.scalar_tensor_tensor(w[:, :], w[:, :], 1.0, u[:, :], ALU.add, ALU.mult))
            chain(nc.vector.tensor_scalar(x[:, :], x[:, :], 0.0, None, ALU.max))
            chain(nc.vector.scalar_tensor_tensor(dec["dt"][:, :], w[:, :], 2.0, x[:, :], ALU.mult, ALU.add))
            assert step[0] == 3 + 4 + TERMS + 2
            nc.vector.tensor_tensor(dta[:, :].rearrange("p (c h) -> p c h", h=SH),
                                    dec["dt"][:, :].rearrange("p (c h) -> p c h", h=SH),
                                    k["aneg"][:, None, :].to_broadcast([P, NBLK, SH]), ALU.mult).then_inc(cumulated, 1)
            dve.wait_ge(turned, 2)
            nc.vector.tensor_copy(rows[:, :, :], pr[:, :, :]).then_inc(done, 1)
            nc.vector.tensor_copy(dec["cum"][:, :], pc[:, :]).then_inc(done, 1)
            dve.wait_ge(done, 2)
            dve.wait_ge(a1, 2)
            chain(nc.vector.tensor_tensor(w[:, :], pe_[:, :], dec["cum"][:, :], ALU.subtract))
            dve.wait_ge(a1, 3)
            chain(nc.vector.tensor_tensor(dec["dtend"][:, :], dec["dt"][:, :], w[:, :], ALU.mult))


def attention(nc, scratch, k):
    with Stage(nc, "attn") as st:
        q = st.sb("q", [P, 2, 2, P]); za = st.sb("za", [P, 2, 2, P]); vt = st.sb("vt", [HD, 2, P])
        bias_cur = st.sb("bias_cur", [P, H, P]); bias_prev = st.sb("bias_prev", [P, H, P])
        kk = [[st.sb(f"k{g}_{s}", [P, P]) for s in range(2)] for g in range(KV)]
        vv = [[st.sb(f"v{g}_{s}", [P, HD]) for s in range(2)] for g in range(KV)]
        sc = st.sb("sc", [P, 2, GRP, P]); pcur = st.sb("pcur", [P, 2, GRP, P]); pprev = st.sb("pprev", [P, 2, GRP, P])
        mx = st.sb("mx", [P, 2, GRP]); es = st.sb("es", [P, 2, GRP]); den = st.sb("den", [P, 2, GRP]); o = st.sb("o", [P, 2, 2, P])
        score = st.ps("score", [P, 2, 2, GRP // 2, 2, P])
        pt = st.ps("pt", [P, 2, GRP, P]); av = st.ps("av", [P, 2, 4, P])
        loaded = [[st.sem(f"in{s}_loaded")] for s in range(2)]
        loaded = [x[0] for x in loaded]
        stored = [st.sem("o0_stored"), st.sem("o1_stored")]
        names = ("bias_masked", "v_turned", "scored", "v_made", "chosen", "biased", "prev_biased", "maxed", "sinkmaxed", "shifted",
                 "sink_shifted", "exp_made", "sink_exp", "summed", "denominated", "inverted", "normalised", "p_turned",
                 "cur_made", "prev_made", "weighed", "gated")
        (bias_masked, v_turned, scored, v_made, chosen, biased, prev_biased, maxed, sinkmaxed, shifted, sink_shifted, exp_made,
         sink_exp, summed, denominated, inverted, normalised, p_turned, cur_made, prev_made, weighed, gated) = [st.sem(n) for n in names]
        blk = st.block()
        UNITS = 2 * KV
        IN = 5 * 16

        def units(eng, order):
            order(0, True)
            with eng.Fori(1, NBLK // 2) as i:
                order(i, False)

        @blk.sync
        def _(sp):
            def turn(i, first):
                for m in range(UNITS):
                    n, g, b, blkn = i * UNITS + m, m % KV, m % 2, i * 2 + m // KV
                    t = bass.ds(blkn * P, P)
                    if exists(n - 2):
                        sp.wait_ge(gated, n - 1)
                    kd = kk[g][m // KV]
                    sp.dma_start(q[:, b, :, :], scratch["q"][g * GRP * HD:(g + 1) * GRP * HD, t].rearrange("(c p) t -> p c t", p=P)).then_inc(loaded[b], 16)
                    sp.dma_start(za[:, b, :, :], scratch["za"][g * GRP * HD:(g + 1) * GRP * HD, t].rearrange("(c p) t -> p c t", p=P)).then_inc(loaded[b], 16)
                    sp.dma_start(kd[0:HD, :], scratch["k"][g * HD:(g + 1) * HD, t]).then_inc(loaded[b], 16)
                    sp.dma_start(kd[HD:P, :], scratch["k"][g * HD:(g + 1) * HD, t]).then_inc(loaded[b], 16)
                    sp.dma_start(vt[:, b, :], scratch["v"][g * HD:(g + 1) * HD, t]).then_inc(loaded[b], 16)
            units(sp, turn)

        @blk.gpsimd
        def _(pool):
            def turn(i, first):
                for m in range(UNITS):
                    n, g, b, blkn = i * UNITS + m, m % KV, m % 2, i * 2 + m // KV
                    pool.wait_ge(gated, n + 1)
                    pool.dma_start(scratch["attn"][g * GRP * HD:(g + 1) * GRP * HD, bass.ds(blkn * P, P)].rearrange("(c p) t -> p c t", p=P),
                                   o[:, b, :, :]).then_inc(stored[b], 16)
            units(pool, turn)
            for b in range(2):
                pool.wait_ge(stored[b], 16 * NBLK * KV // 2)

        @blk.tensor
        def _(pe):
            def scores(i, m):
                n, g, b, s = i * UNITS + m, m % KV, m % 2, m // KV
                pe.wait_ge(loaded[b], IN * (i * (UNITS // 2) + (m // 2 + 1)))
                if exists(n - 2):
                    pe.wait_ge(gated, n - 1)
                for h in range(GRP):
                    half, pair = h % 2, h // 2
                    r = slice(HD * half, HD * half + HD)
                    last = nc.tensor.matmul(score[:, b, half, pair, 1, :], q[r, b, pair, :], kk[g][s][r, :], start=True, stop=True)
                    if exists(n - KV):
                        last = nc.tensor.matmul(score[:, b, half, pair, 0, :], q[r, b, pair, :], kk[g][1 - s][r, :], start=True, stop=True)
                last.then_inc(scored, 1)
                nc.tensor.transpose(av[:, b, 2, 0:HD], vt[:, b, :], k["ident"][0:HD, 0:HD]).then_inc(v_turned, 1)

            def turn_p(i, m):
                n, b = i * UNITS + m, m % 2
                pe.wait_ge(normalised, n + 1)
                for h in range(GRP):
                    last = nc.tensor.transpose(pt[:, b, h, :], sc[:, b, h, :], k["ident"][:, :])
                last.then_inc(p_turned, 1)

            def weigh(i, m):
                n, g, b, s = i * UNITS + m, m % KV, m % 2, m // KV
                pe.wait_ge(cur_made, n + 1)
                pe.wait_ge(v_made, n + 1)
                if exists(n - KV):
                    pe.wait_ge(prev_made, n + 1 - KV)
                for hh in range(2):
                    to = av[HD * hh:HD * hh + HD, b, 0:2, :]
                    last = nc.tensor.matmul(to, vv[g][s][:, :], pcur[:, b, 2 * hh:2 * hh + 2, :], start=True, stop=not exists(n - KV))
                    if exists(n - KV):
                        last = nc.tensor.matmul(to, vv[g][1 - s][:, :], pprev[:, b, 2 * hh:2 * hh + 2, :], start=False, stop=True)
                last.then_inc(weighed, 1)

            def turn(i, first):
                scores(i, 0)
                for m in range(UNITS):
                    if m + 1 < UNITS:
                        scores(i, m + 1)
                    turn_p(i, m)
                    weigh(i, m)
            units(pe, turn)

        @blk.scalar
        def _(act):
            def turn(i, first):
                for m in range(UNITS):
                    n, b = i * UNITS + m, m % 2
                    act.wait_ge(v_turned, n + 1)
                    nc.scalar.activation(vv[m % KV][m // KV][:, :], av[:, b, 2, 0:HD], ACT.Copy).then_inc(v_made, 1)
                    act.wait_ge(shifted, n + 1)
                    nc.scalar.activation(sc[:, b, :, :], sc[:, b, :, :], ACT.Exp).then_inc(exp_made, 1)
                    act.wait_ge(sink_shifted, n + 1)
                    nc.scalar.activation(es[:, b, :], es[:, b, :], ACT.Exp).then_inc(sink_exp, 1)
            units(act, turn)

        @blk.vector
        def _(dve):
            nc.vector.tensor_tensor(bias_cur[:, :, :], k["bias"][:, :, :], k["neg"][:, None, :].to_broadcast([P, H, P]), ALU.add).then_inc(bias_masked, 1)
            nc.vector.tensor_tensor(bias_prev[:, :, :], k["bias"][:, :, :], k["negcur"][:, None, :].to_broadcast([P, H, P]), ALU.add).then_inc(bias_masked, 1)
            dve.wait_ge(bias_masked, 2)

            def softmax_in(i, m):
                n, g, b = i * UNITS + m, m % KV, m % 2
                hs = slice(g * GRP, (g + 1) * GRP)
                dve.wait_ge(scored, n + 1)
                scv = sc[:, b, :, :].rearrange("q (half pair) k -> q half pair k", half=2)
                spv = pprev[:, b, :, :].rearrange("q (half pair) k -> q half pair k", half=2)
                bcv, bpv = (t[:, hs, :].rearrange("q (pair half) k -> q half pair k", half=2) for t in (bias_cur, bias_prev))
                nc.vector.tensor_tensor(scv, score[:, b, :, :, 1, :], bcv, ALU.add).then_inc(biased, 1)
                if exists(n - KV):
                    nc.vector.tensor_tensor(spv, score[:, b, :, :, 0, :], bpv, ALU.add).then_inc(prev_biased, 1)
                    dve.wait_ge(biased, n + 1)
                    dve.wait_ge(prev_biased, n + 1 - KV)
                    nc.vector.tensor_tensor(sc[:, b, :, :], sc[:, b, :, :], pprev[:, b, :, :], ALU.max).then_inc(chosen, 1)
                    dve.wait_ge(chosen, n + 1 - KV)
                dve.wait_ge(biased, n + 1)
                nc.vector.tensor_reduce(mx[:, b, :], sc[:, b, :, :], AX, ALU.max).then_inc(maxed, 1)
                dve.wait_ge(maxed, n + 1)
                mxv, esv = (t[:, b, :].rearrange("q (half pair) -> q half pair", half=2) for t in (mx, es))
                sink = k["sink"][:, g * GRP:(g + 1) * GRP].rearrange("q (pair half) -> q half pair", half=2)
                nc.vector.tensor_tensor(mxv, mxv, sink, ALU.max).then_inc(sinkmaxed, 1)
                dve.wait_ge(sinkmaxed, n + 1)
                nc.vector.tensor_tensor(sc[:, b, :, :], sc[:, b, :, :], mx[:, b, :, None].to_broadcast([P, GRP, P]), ALU.subtract).then_inc(shifted, 1)
                nc.vector.tensor_tensor(esv, sink, mxv, ALU.subtract).then_inc(sink_shifted, 1)

            def softmax_out(i, m):
                n, b = i * UNITS + m, m % 2
                dve.wait_ge(exp_made, n + 1)
                nc.vector.tensor_reduce(den[:, b, :], sc[:, b, :, :], AX, ALU.add).then_inc(summed, 1)
                dve.wait_ge(sink_exp, n + 1)
                dve.wait_ge(summed, n + 1)
                nc.vector.tensor_tensor(den[:, b, :], den[:, b, :], es[:, b, :], ALU.add).then_inc(denominated, 1)
                dve.wait_ge(denominated, n + 1)
                nc.vector.reciprocal(den[:, b, :], den[:, b, :]).then_inc(inverted, 1)
                dve.wait_ge(inverted, n + 1)
                nc.vector.tensor_tensor(sc[:, b, :, :], sc[:, b, :, :], den[:, b, :, None].to_broadcast([P, GRP, P]), ALU.mult).then_inc(normalised, 1)

            def masks(i, m):
                n, b = i * UNITS + m, m % 2
                dve.wait_ge(p_turned, n + 1)
                if exists(n - KV):
                    nc.vector.tensor_tensor(pprev[:, b, :, :], pt[:, b, :, :], k["tril"][:, None, :].to_broadcast([P, GRP, P]), ALU.mult).then_inc(prev_made, 1)
                nc.vector.tensor_tensor(pcur[:, b, :, :], pt[:, b, :, :], k["triu"][:, None, :].to_broadcast([P, GRP, P]), ALU.mult).then_inc(cur_made, 1)

            def gate(i, m):
                n, b = i * UNITS + m, m % 2
                dve.wait_ge(weighed, n + 1)
                if exists(n - 2):
                    dve.wait_ge(stored[b], 16 * (i * (UNITS // 2) + m // 2))
                nc.vector.tensor_tensor(o[:, b, :, :], av[:, b, 0:2, :], za[:, b, :, :], ALU.mult).then_inc(gated, 1)

            def turn(i, first):
                softmax_in(i, 0)
                for m in range(UNITS):
                    softmax_out(i, m)
                    if m + 1 < UNITS:
                        softmax_in(i, m + 1)
                    masks(i, m)
                    gate(i, m)
            units(dve, turn)
            dve.wait_ge(gated, NBLK * KV)


def ssd(nc, scratch, k, dec):
    XT = R * HD // P
    with Stage(nc, "ssd") as st:
        bt = st.sb("bt", [P, 2, P]); ct = st.sb("ct", [P, 2, P]); xt = st.sb("xt", [P, 2, XT, P]); zt = st.sb("zt", [P, 2, XT, P])
        row = st.sb("row", [P, 2, R, P]); seg = st.sb("seg", [P, 2, R, P]); cx = st.sb("cx", [P, 2, R, P])
        cbm = st.sb("cbm", [P, 2, P]); btok = st.sb("btok", [P, 2, P]); xdt = st.sb("xdt", [P, 2, R, HD]); xend = st.sb("xend", [P, 2, R, HD])
        state = [st.sb(f"state{g}", [P, R, HD]) for g in range(SG)]
        y = st.sb("y", [P, 2, XT, P]); ysq = st.sb("ysq", [P, 2, XT, P]); rs = st.sb("rs", [P, 2, P])
        p_xt = [st.ps(f"xt{b}", [P, XT, P]) for b in range(2)]
        p_cb = [st.ps(f"cb{b}", [P, 4, P]) for b in range(2)]
        p_y = [st.ps(f"y{b}", [P, XT, P]) for b in range(2)]
        p_st = [st.ps(f"st{b}", [P, R, HD]) for b in range(2)]
        loaded = [st.sem("in0_loaded"), st.sem("in1_loaded")]
        stored = [st.sem("y0_stored"), st.sem("y1_stored")]
        names = ("cleared", "cb_made", "b_turned", "x_turned", "masked", "b_copied", "xdt_made", "xend_made", "seg_made", "seg_exp",
                 "row_exp", "m_made", "c_scaled", "y_made", "states_made", "decayed", "state_new", "skipped", "z_gated",
                 "squared", "y_summed", "logged", "rstd_made", "y_done")
        (cleared, cb_made, b_turned, x_turned, masked, b_copied, xdt_made, xend_made, seg_made, seg_exp, row_exp, m_made, c_scaled,
         y_made, states_made, decayed, state_new, skipped, z_gated, squared, y_summed, logged, rstd_made, y_done) = [st.sem(n) for n in names]
        blk = st.block()
        IN = 5 * 16

        def chunks(eng, turn):
            turn(0)
            with eng.Fori(1, NBLK) as i:
                turn(i)

        def decay_col(name, i, g):
            return dec[name][:, bass.ds(i * SH + g * R, R)]

        @blk.sync
        def _(sp):
            def turn(i):
                t = bass.ds(i * P, P)
                for g in range(SG):
                    n, b = i * SG + g, g % 2
                    if exists(n - 2):
                        sp.wait_ge(y_done, n - 1)
                    gc = g * R * HD
                    sp.dma_start(bt[:, b, :], scratch["xbc"][SW + g * SN:SW + (g + 1) * SN, t]).then_inc(loaded[b], 16)
                    sp.dma_start(ct[:, b, :], scratch["xbc"][SW + (SG + g) * SN:SW + (SG + g + 1) * SN, t]).then_inc(loaded[b], 16)
                    sp.dma_start(xt[:, b, :, :], scratch["xbc"][gc:gc + R * HD, t].rearrange("(c p) t -> p c t", p=P)).then_inc(loaded[b], 16)
                    sp.dma_start(zt[:, b, :, :], scratch["zm"][gc:gc + R * HD, t].rearrange("(c p) t -> p c t", p=P)).then_inc(loaded[b], 16)
                    src = scratch["rowcum"][bass.ds(i * SH + g * R, R), :].rearrange("(o h) l -> o h l", o=1)
                    sp.dma_start(row[:, b, :, :], src.to_broadcast([P, R, P])).then_inc(loaded[b], 16)
            chunks(sp, turn)

        @blk.gpsimd
        def _(pool):
            def turn(i):
                for g in range(SG):
                    n, b = i * SG + g, g % 2
                    pool.wait_ge(y_done, n + 1)
                    pool.dma_start(scratch["y"][g * R * HD:(g + 1) * R * HD, bass.ds(i * P, P)].rearrange("(c p) t -> p c t", p=P),
                                   y[:, b, :, :]).then_inc(stored[b], 16)
            chunks(pool, turn)
            for b in range(2):
                pool.wait_ge(stored[b], 16 * NBLK * SG // 2)

        @blk.tensor
        def _(pe):
            def prepare(i, g):
                n, b = i * SG + g, g % 2
                pe.wait_ge(loaded[b], IN * (i * (SG // 2) + (g // 2 + 1)))
                if exists(n - 2):
                    pe.wait_ge(y_done, n - 1)
                nc.tensor.matmul(p_cb[b][:, 0, :], bt[:, b, :], ct[:, b, :], start=True, stop=True).then_inc(cb_made, 1)
                nc.tensor.transpose(p_st[b][:, 0:P // HD, :].rearrange("p r d -> p (r d)"), bt[:, b, :], k["ident"][:, :]).then_inc(b_turned, 1)
                for c in range(XT):
                    last = nc.tensor.transpose(p_xt[b][:, c, :], xt[:, b, c, :], k["ident"][:, :])
                last.then_inc(x_turned, 1)

            def outputs(i, g):
                n, b = i * SG + g, g % 2
                pe.wait_ge(xdt_made, n + 1)
                pe.wait_ge(m_made, n + 1)
                pe.wait_ge(c_scaled, n + 1)
                pe.wait_ge(state_new, n + 1)
                for r in range(R):
                    to = p_y[b][HD * (r % 2):HD * (r % 2) + HD, r // 2, :]
                    nc.tensor.matmul(to, xdt[:, b, r, :], seg[:, b, r, :], start=True, stop=False)
                    last = nc.tensor.matmul(to, state[g][:, r, :], cx[:, b, r, :], start=False, stop=True)
                last.then_inc(y_made, 1)
                pe.wait_ge(b_copied, n + 1)
                pe.wait_ge(xend_made, n + 1)
                nc.tensor.matmul(p_st[b][:, :, :], btok[:, b, :], xend[:, b, :, :], start=True, stop=True).then_inc(states_made, 1)

            def norm(i, g):
                n, b = i * SG + g, g % 2
                pe.wait_ge(squared, n + 1)
                for c in range(XT):
                    last = nc.tensor.matmul(p_cb[b][:, 2, :], k["ones"][:, :], ysq[:, b, c, :], start=(c == 0), stop=(c == XT - 1))
                last.then_inc(y_summed, 1)

            def turn(i):
                prepare(i, 0)
                for g in range(SG):
                    if g + 1 < SG:
                        prepare(i, g + 1)
                    outputs(i, g)
                    norm(i, g)
            chunks(pe, turn)

        @blk.scalar
        def _(act):
            def first(i, g):
                n, b = i * SG + g, g % 2
                act.wait_ge(loaded[b], IN * (i * (SG // 2) + (g // 2 + 1)))
                act.wait_ge(b_turned, n + 1)
                nc.scalar.activation(btok[:, b, :], p_st[b][:, 0:P // HD, :].rearrange("p r d -> p (r d)"), ACT.Copy).then_inc(b_copied, 1)
                if exists(n - 2):
                    act.wait_ge(y_made, n - 1)
                nc.scalar.activation(cx[:, b, :, :], row[:, b, :, :], ACT.Exp).then_inc(row_exp, 1)
                act.wait_ge(seg_made, n + 1)
                nc.scalar.activation(seg[:, b, :, :], seg[:, b, :, :], ACT.Exp).then_inc(seg_exp, 1)

            def second(i, g):
                n, b = i * SG + g, g % 2
                act.wait_ge(z_gated, n + 1)
                nc.scalar.activation(ysq[:, b, :, :], y[:, b, :, :], ACT.Square).then_inc(squared, 1)
                act.wait_ge(y_summed, n + 1)
                nc.scalar.activation(rs[:, b, :], p_cb[b][:, 2, :], ACT.Ln, bias=k["eps"][:, :], scale=1.0 / (R * HD)).then_inc(logged, 1)
                act.wait_ge(logged, n + 1)
                nc.scalar.activation(rs[:, b, :], rs[:, b, :], ACT.Exp, scale=-0.5).then_inc(rstd_made, 1)

            def turn(i):
                first(i, 0)
                for g in range(SG):
                    if g + 1 < SG:
                        first(i, g + 1)
                    second(i, g)
            chunks(act, turn)

        @blk.vector
        def _(dve):
            def first(i, g):
                n, b = i * SG + g, g % 2
                dve.wait_ge(loaded[b], IN * (i * (SG // 2) + (g // 2 + 1)))
                if exists(n - 2):
                    dve.wait_ge(y_made, n - 1)
                for r in range(R):
                    last = nc.vector.tensor_scalar(seg[:, b, r, :], row[:, b, r, :], dec["cum"][:, bass.ds(i * SH + (g * R + r), 1)], 0.0,
                                                   ALU.subtract, ALU.min)
                last.then_inc(seg_made, 1)
                dve.wait_ge(cb_made, n + 1)
                nc.vector.tensor_tensor(cbm[:, b, :], p_cb[b][:, 0, :], k["triu"][:, :], ALU.mult).then_inc(masked, 1)
                dve.wait_ge(x_turned, n + 1)
                xv = p_xt[b][:, :, :].rearrange("p c (h d) -> p (c h) d", d=HD)
                nc.vector.tensor_tensor(xdt[:, b, :, :], xv, decay_col("dt", i, g)[:, :, None].to_broadcast([P, R, HD]), ALU.mult).then_inc(xdt_made, 1)
                if exists(n - 2):
                    dve.wait_ge(states_made, n - 1)
                nc.vector.tensor_tensor(xend[:, b, :, :], xv, decay_col("dtend", i, g)[:, :, None].to_broadcast([P, R, HD]), ALU.mult).then_inc(xend_made, 1)
                dve.wait_ge(row_exp, n + 1)
                nc.vector.tensor_tensor(cx[:, b, :, :], cx[:, b, :, :], ct[:, b, None, :].to_broadcast([P, R, P]), ALU.mult).then_inc(c_scaled, 1)
                dve.wait_ge(seg_exp, n + 1)
                dve.wait_ge(masked, n + 1)
                nc.vector.tensor_tensor(seg[:, b, :, :], seg[:, b, :, :], cbm[:, b, None, :].to_broadcast([P, R, P]), ALU.mult).then_inc(m_made, 1)

            def second(i, g):
                n, b = i * SG + g, g % 2
                dve.wait_ge(y_made, n + 1)
                if exists(n - 2):
                    dve.wait_ge(stored[b], 16 * (i * (SG // 2) + g // 2))
                for c in range(XT):
                    last = nc.vector.scalar_tensor_tensor(y[:, b, c, :], xt[:, b, c, :], k["dskip"][:, g * XT + c:g * XT + c + 1], p_y[b][:, c, :],
                                                          ALU.mult, ALU.add)
                last.then_inc(skipped, 1)
                nc.vector.tensor_tensor(state[g][:, :, :], state[g][:, :, :], decay_col("chunk", i, g)[:, :, None].to_broadcast([P, R, HD]),
                                        ALU.mult).then_inc(decayed, 1)
                dve.wait_ge(skipped, n + 1)
                nc.vector.tensor_tensor(y[:, b, :, :], y[:, b, :, :], zt[:, b, :, :], ALU.mult).then_inc(z_gated, 1)
                dve.wait_ge(states_made, n + 1)
                dve.wait_ge(decayed, n + 1)
                nc.vector.tensor_tensor(state[g][:, :, :], state[g][:, :, :], p_st[b][:, :, :], ALU.add).then_inc(state_new, 1)

            def third(i, g):
                n, b = i * SG + g, g % 2
                dve.wait_ge(rstd_made, n + 1)
                for c in range(XT):
                    last = nc.vector.scalar_tensor_tensor(y[:, b, c, :], y[:, b, c, :], k["ssmw"][:, g * XT + c:g * XT + c + 1], rs[:, b, :],
                                                          ALU.mult, ALU.mult)
                last.then_inc(y_done, 1)

            for g in range(SG):
                nc.vector.memset(state[g][:, :, :], 0.0).then_inc(state_new, 1)
            dve.wait_ge(state_new, SG)

            def turn(i):
                first(i, 0)
                for g in range(SG):
                    second(i, g)
                    if g + 1 < SG:
                        first(i, g + 1)
                    third(i, g)
            chunks(dve, turn)
            dve.wait_ge(y_done, NBLK * SG)


def merge(nc, a, scratch, k, out):
    HALF = S // 2
    PASSES = [(half, what) for half in range(2) for what in ("attn", "y0", "y1")] + [(0, "out"), (1, "out")]
    NJ = D // P
    TT = HALF // P
    LAST = NJ * len(PASSES) - 1
    with Stage(nc, "merge") as st:
        a_raw = st.sb("a_raw", [P, 2, HALF])
        a_hi = [st.sb(f"a_hi{b}", [P, KT, HALF], F32R) for b in range(2)]
        a_lo = [st.sb(f"a_lo{b}", [P, KT, HALF], F32R) for b in range(2)]
        raw = st.sb("raw", [P, 2, KT, P])
        w_hi = [st.sb(f"w_hi{b}", [P, KT, P], F32R) for b in range(2)]
        w_lo = [st.sb(f"w_lo{b}", [P, KT, P], F32R) for b in range(2)]
        side = st.sb("side", [P, 2, HALF])
        prev = st.sb("prev", [P, 2, HALF])
        res = st.sb("res", [P, 2, HALF])
        acc = st.ps("acc", [P, 2, HALF]); tok = st.ps("tok", [P, 2, TT, P])
        w_loaded = [st.sem(f"w{b}_loaded") for b in range(2)]
        a_loaded = [st.sem(f"a{b}_loaded") for b in range(2)]
        side_loaded = [st.sem(f"side{b}_loaded") for b in range(2)]
        prev_loaded = [st.sem(f"prev{b}_loaded") for b in range(2)]
        stored = [st.sem(f"res{b}_stored") for b in range(2)]
        w_hi_made, w_lo_made, a_hi_made, a_lo_made, multiplied, gated, added, out_gated, turned, res_made = [st.sem(n) for n in (
            "w_hi_made", "w_lo_made", "a_hi_made", "a_lo_made", "multiplied", "gated", "added", "out_gated", "turned", "res_made")]
        blk = st.block()
        weight = {"attn": a["w_attn_proj"], "y0": a["w_ssm_proj_0"], "y1": a["w_ssm_proj_1"], "out": a["w_out"]}
        source = {"attn": scratch["attn"], "y0": scratch["y"][0:D, :], "y1": scratch["y"][D:2 * D, :], "out": scratch["m"]}
        OUT0 = NJ * sum(w != "out" for _, w in PASSES)

        def tiles(eng, body):
            for p in range(len(PASSES)):
                lo, hi = (1 if p == 0 else 0), NJ // 2 - (1 if p == len(PASSES) - 1 else 0)
                n0 = NJ * p
                if lo:
                    for b in range(2):
                        body(b, b, 0, p, b)
                with eng.Fori(lo, hi) as i:
                    for b in range(2):
                        body(2 * i + (n0 + b), b, i + n0 // 2, p, 2 * i + b)
                if hi < NJ // 2:
                    for b in range(2):
                        body(LAST - 1 + b, b, LAST // 2, p, NJ - 2 + b)

        @blk.sync
        def _(sp):
            def chunk(c, b, h, p, j):
                half, what = PASSES[p]
                if exists(c - 2):
                    sp.wait_ge(a_lo_made, c - 1)
                sp.dma_start(a_raw[:, b, :], source[what][bass.ds(j * P, P), half * HALF:(half + 1) * HALF]).then_inc(a_loaded[b], 16)

            def load(n, b, h, p, j):
                half, what = PASSES[p]
                cols = slice(half * HALF, (half + 1) * HALF)
                row = j * P if isinstance(j, int) else sp.snap(j * P)
                if exists(n - 2):
                    sp.wait_ge(w_lo_made, n - 1)
                sp.dma_start(raw[:, b, :, :], weight[what][bass.ds(j, 1)].rearrange("o p k c -> (o p) k c")).then_inc(w_loaded[b], 16)
                if p + 1 < len(PASSES):
                    if PASSES[p + 1][1] == "out":
                        for bb in range(2):
                            sp.wait_ge(stored[bb], 16 * (NJ // 2) * (3 * (PASSES[p + 1][0] + 1)))
                    chunk(n + KT, b, h + KT // 2, p + 1, j)
                if what in ("y0", "y1"):
                    sp.wait_ge(stored[b], 16 * (h - 3))
                if what == "out":
                    sp.wait_ge(a_lo_made, KT)
                if exists(n - 2):
                    sp.wait_ge(res_made, n - 1)
                if what == "out":
                    sp.dma_start(side[:, b, :].rearrange("p (t c) -> p t c", c=P),
                                 a["x"][0, cols, bass.ds(row, P)].rearrange("(t p) c -> p t c", p=P)).then_inc(side_loaded[b], 16)
                else:
                    g0 = 0 if what == "attn" else D
                    sp.dma_start(side[:, b, :], scratch["g"][g0:g0 + D][bass.ds(row, P), cols]).then_inc(side_loaded[b], 16)
                if what in ("y0", "y1"):
                    sp.dma_start(prev[:, b, :], scratch["m"][bass.ds(row, P), cols]).then_inc(prev_loaded[b], 16)

            for b in range(2):
                chunk(b, b, 0, 0, b)
            with sp.Fori(1, KT // 2) as i:
                for b in range(2):
                    chunk(2 * i + b, b, i, 0, 2 * i + b)
            tiles(sp, load)

        @blk.gpsimd
        def _(pool):
            def store(n, b, h, p, j):
                half, what = PASSES[p]
                pool.wait_ge(res_made, n + 1)
                if what == "out":
                    pool.dma_start(out[0, half * HALF:(half + 1) * HALF, bass.ds(j * P, P)].rearrange("(t p) c -> p t c", p=P),
                                   res[:, b, :].rearrange("p (t c) -> p t c", c=P)).then_inc(stored[b], 16)
                else:
                    pool.dma_start(scratch["m"][bass.ds(j * P, P), half * HALF:(half + 1) * HALF], res[:, b, :]).then_inc(stored[b], 16)
            tiles(pool, store)
            for b in range(2):
                pool.wait_ge(stored[b], 16 * (LAST + 1) // 2)

        @blk.tensor
        def _(pe):
            def product(n, b, h, p, j):
                half, what = PASSES[p]
                s = p % 2
                pe.wait_ge(w_lo_made, n + 1)
                pe.wait_ge(a_lo_made, KT * (p + 1))
                if exists(n - 2):
                    pe.wait_ge(res_made, n - 1)
                for kk in range(KT):
                    for step, (wv, av) in enumerate(((w_hi[b], a_hi[s]), (w_hi[b], a_lo[s]), (w_lo[b], a_hi[s]))):
                        for c in range(HALF // MM):
                            last = nc.tensor.matmul(acc[:, b, c * MM:(c + 1) * MM], wv[:, kk, :], av[:, kk, c * MM:(c + 1) * MM],
                                                    start=(kk == 0 and step == 0), stop=(kk == KT - 1 and step == 2))
                last.then_inc(multiplied, 1)
                if what == "out":
                    pe.wait_ge(out_gated, n - (OUT0 - 1))
                    for t in range(TT):
                        last = nc.tensor.transpose(tok[:, b, t, :], prev[:, b, t * P:(t + 1) * P], k["ident"][:, :])
                    last.then_inc(turned, 1)
            tiles(pe, product)

        @blk.scalar
        def _(act):
            def high_w(b, h):
                act.wait_ge(w_loaded[b], 16 * h + 16)
                nc.scalar.activation(w_hi[b][:, :, :], raw[:, b, :, :], ACT.Copy).then_inc(w_hi_made, 1)

            def high_a(c, b, h, p, j):
                act.wait_ge(a_loaded[b], 16 * h + 16)
                nc.scalar.activation(a_hi[p % 2][:, bass.ds(j, 1), :], a_raw[:, b, None, :], ACT.Copy).then_inc(a_hi_made, 1)

            def step(n, b, h, p, j):
                if not (isinstance(n, int) and n == LAST):
                    if exists(n - 1):
                        act.wait_ge(multiplied, n)
                    high_w(1 - b, h + b)
                if p + 1 < len(PASSES):
                    high_a(n + KT, b, h + KT // 2, p + 1, j)
                if PASSES[p][1] == "out":
                    act.wait_ge(multiplied, n + 1)
                    nc.scalar.activation(prev[:, b, :], acc[:, b, :], ACT.Copy, scale=k["gate"][:, bass.ds(j, 1)]).then_inc(out_gated, 1)

            for b in range(2):
                high_a(b, b, 0, 0, b)
            with act.Fori(1, KT // 2) as i:
                for b in range(2):
                    high_a(2 * i + b, b, i, 0, 2 * i + b)
            high_w(0, 0)
            tiles(act, step)

        @blk.vector
        def _(dve):
            def low_w(n, b):
                dve.wait_ge(w_hi_made, n + 1)
                if exists(n - 2):
                    dve.wait_ge(multiplied, n - 1)
                nc.vector.tensor_tensor(w_lo[b][:, :, :], raw[:, b, :, :], w_hi[b][:, :, :], ALU.subtract).then_inc(w_lo_made, 1)

            def low_a(c, b, h, p, j):
                dve.wait_ge(a_hi_made, c + 1)
                nc.vector.tensor_tensor(a_lo[p % 2][:, bass.ds(j, 1), :], a_raw[:, b, None, :], a_hi[p % 2][:, bass.ds(j, 1), :],
                                        ALU.subtract).then_inc(a_lo_made, 1)

            def step(n, b, h, p, j):
                what = PASSES[p][1]
                if not (isinstance(n, int) and n == LAST):
                    low_w(n + 1, 1 - b)
                if p + 1 < len(PASSES):
                    low_a(n + KT, b, h + KT // 2, p + 1, j)
                dve.wait_ge(side_loaded[b], 16 * h + 16)
                if exists(n - 2):
                    dve.wait_ge(stored[b], 16 * h)
                if what == "out":
                    dve.wait_ge(turned, n - (OUT0 - 1))
                    nc.vector.tensor_tensor(res[:, b, :], tok[:, b, :, :].rearrange("p t c -> p (t c)"), side[:, b, :], ALU.add).then_inc(res_made, 1)
                    return
                dve.wait_ge(multiplied, n + 1)
                if what == "attn":
                    nc.vector.tensor_tensor(res[:, b, :], acc[:, b, :], side[:, b, :], ALU.mult).then_inc(res_made, 1)
                    return
                nc.vector.tensor_tensor(res[:, b, :], acc[:, b, :], side[:, b, :], ALU.mult).then_inc(gated, 1)
                seen = NJ * (1 + PASSES[p][0])
                dve.wait_ge(gated, n - (seen - 1))
                dve.wait_ge(prev_loaded[b], 16 * (h - (seen // 2 - 1)))
                nc.vector.tensor_tensor(res[:, b, :], res[:, b, :], prev[:, b, :], ALU.add).then_inc(res_made, 1)

            for b in range(2):
                low_a(b, b, 0, 0, b)
            with dve.Fori(1, KT // 2) as i:
                for b in range(2):
                    low_a(2 * i + b, b, i, 0, 2 * i + b)
            low_w(0, 0)
            tiles(dve, step)
            dve.wait_ge(res_made, LAST + 1)


def columns(v, copies=1):
    v = np.asarray(v).reshape(-1)
    v = np.concatenate([v] * copies)
    return np.ascontiguousarray(v.reshape(-1, P).T)


def weight_tiles(w):
    rows, cols = w.shape
    return np.ascontiguousarray(w.reshape(rows // P, P, cols // P, P).transpose(2, 1, 0, 3))


def layouts(i):
    w_in = i["w_in"][0]
    o = {"x": i["x"], "w_ada": i["w_ada"], "rel_bias": i["rel_bias"], "onehot": bucket_onehot(),
         "c": columns(i["c"]), "b_ada": columns(i["b_ada"]), "norm_w": columns(i["norm_w"]), "conv_b": columns(i["conv_b"]),
         "ssm_norm_w": columns(i["ssm_norm_w"]), "q_norm_w": columns(i["q_norm_w"], P // HD), "k_norm_w": columns(i["k_norm_w"], P // HD),
         "dt_bias": i["dt_bias"].reshape(SH, 1), "sinks": i["sinks"].reshape(1, H), "a_log": i["a_log"].reshape(1, SH),
         "d_skip": columns(np.repeat(i["d_skip"].reshape(-1), HD)),
         "conv_w": np.ascontiguousarray(i["conv_w"][0].reshape(CW, XBC // P, P).transpose(2, 0, 1)),
         "w_attn_proj": weight_tiles(i["w_attn_proj"][0]), "w_out": weight_tiles(i["w_out"][0]),
         "w_ssm_proj_0": weight_tiles(i["w_ssm_proj"][0, 0:D]), "w_ssm_proj_1": weight_tiles(i["w_ssm_proj"][0, D:2 * D])}
    for _, col, count, name in KINDS:
        o["w_in_" + name] = weight_tiles(w_in[:, col:col + count * P])
    return {n: np.ascontiguousarray(v) for n, v in o.items()}


def kernel(**inputs):
    import concourse.bacc as bacc
    from concourse.bass_utils import run_bass_kernel_spmd

    nc = bacc.Bacc("TRN2", target_bir_lowering=False, num_devices=1)
    arrays, aps = {}, {}
    for name, v in layouts({n: np.asarray(v) for n, v in inputs.items()}).items():
        arrays["in_" + name] = v
        aps[name] = nc.dram_tensor("in_" + name, v.shape, mybir.dt.from_np(v.dtype), kind="ExternalInput").ap()
    out = nc.dram_tensor("out", (1, S, D), F32, kind="ExternalOutput").ap()
    build(nc, aps, out)
    r = run_bass_kernel_spmd(nc, [arrays], core_ids=[0])
    return r.results[0]["out"]
```

```python
import math
from contextlib import ExitStack

import numpy as np
import concourse.bass as bass
from concourse import mybir

F32, F32R, U32 = mybir.dt.float32, mybir.dt.float32r, mybir.dt.uint32
ALU, ACT, AX = mybir.AluOpType, mybir.ActivationFunctionType, mybir.AxisListType.X

P = 128
D = 1024
S = 2048
KT = D // P
H, KV, HD = 16, 4, 64
GRP = H // KV
SW, SH, SG, SN = 2048, 32, 4, 128
R = SH // SG
CW = 4
NBLK = S // P
EPS = 1e-6
NEG = -1e30
BUCKETS, MAXDIST = 32, 128
MM = 512

C_Q = 0
C_K = C_Q + H * HD
C_V = C_K + KV * HD
C_ZA = C_V + KV * HD
C_ZM = C_ZA + H * HD
C_XBC = C_ZM + SW
XBC = SW + 2 * SG * SN
C_DT = C_XBC + XBC
C_G = C_DT + SH

KINDS = [("plain", C_DT, 1, "dt"), ("plain", C_V, 2, "v"), ("norm", C_K, 2, "k"), ("norm", C_Q, 8, "q"),
         ("silu", C_ZA, 8, "za"), ("silu", C_ZM, 16, "zm"), ("conv", C_XBC, 24, "xbc"), ("gate", C_G, 16, "g")]
NTILES = sum(k[2] for k in KINDS)


def bucket_onehot():
    n = (127 - np.arange(2 * P)) % P
    exact = BUCKETS // 2
    nf = np.maximum(n, 1).astype(np.float32)
    large = exact + (np.log(nf / np.float32(exact)) / np.float32(math.log(MAXDIST / exact))
                     * np.float32(BUCKETS - exact)).astype(np.int32)
    b = np.where(n < exact, n, np.minimum(large, BUCKETS - 1))
    return (b[None, :] == np.arange(BUCKETS)[:, None]).astype(np.float32)


def exists(n):
    return not isinstance(n, int) or n >= 0


def pairs(eng, count, body):
    for b in range(2):
        body(b, b, 0)
    with eng.Fori(1, count // 2) as i:
        for b in range(2):
            body(2 * i + b, b, i)


def dram_ap(t, offset, ap):
    return bass.AP(tensor=t.tensor, offset=offset, ap=ap)


def build(nc, a, out):
    scratch = {n: nc.dram_tensor("scr_" + n, (c * P, S), F32, kind="Internal").ap()
               for _, _, c, n in KINDS}
    scratch["attn"] = nc.dram_tensor("scr_attn", (D, S), F32, kind="Internal").ap()
    scratch["y"] = nc.dram_tensor("scr_y", (SW, S), F32, kind="Internal").ap()
    scratch["m"] = nc.dram_tensor("scr_m", (D, S), F32, kind="Internal").ap()
    scratch["rs"] = nc.dram_tensor("scr_rs", (SW // P, S), F32, kind="Internal").ap()
    scratch["rowcum"] = nc.dram_tensor("scr_rowcum", (NBLK * SH, P), F32, kind="Internal").ap()
    scratch["bias"] = nc.dram_tensor("scr_bias", (H, 2 * P), F32, kind="Internal").ap()
    with ExitStack() as ctx:
        def sb(n, s, d=F32):
            return ctx.enter_context(nc.sbuf_tensor(n, s, d))
        k = dict(
            ident=sb("ident", [P, P]), ones=sb("ones", [P, P]), headones=sb("headones", [P, P]),
            triu=sb("triu", [P, P]), tril=sb("tril", [P, P]), neg=sb("neg", [P, P]),
            negcur=sb("negcur", [P, P]),
            bias=sb("bias", [P, H, P]), sink=sb("sink", [P, H]),
            hscale=sb("hscale", [P, KT]), hshift=sb("hshift", [P, KT]), gate=sb("gate", [P, KT]),
            qw=sb("qw", [P, 1]), kw=sb("kw", [P, 1]), convw=sb("convw", [P, CW, XBC // P]),
            convb=sb("convb", [P, XBC // P]), dskip=sb("dskip", [P, SW // P]), ssmw=sb("ssmw", [P, SW // P]),
            dtb=sb("dtb", [SH, 1]), aneg=sb("aneg", [P, SH]), eps=sb("eps", [P, 1]),
        )
        setup(nc, a, scratch, k)
        with ExitStack() as hctx:
            h = [hctx.enter_context(nc.sbuf_tensor(n, [P, KT, S], F32R)) for n in ("h_hi", "h_lo")]
            normalise(nc, a, k, h)
            project(nc, a, scratch, k, h)
        with ExitStack() as dctx:
            dec = {n: dctx.enter_context(nc.sbuf_tensor("dec_" + n, [P, NBLK * SH], F32))
                   for n in ("dt", "cum", "toend", "chunk")}
            decays(nc, scratch, k, dec)
            mixers(nc, scratch, k, dec)
        merge(nc, a, scratch, k, out)


class Stage:

    def __init__(self, nc, name):
        self.nc, self.name, self.ctx = nc, name, ExitStack()

    def __enter__(self):
        return self

    def __exit__(self, *e):
        return self.ctx.__exit__(*e)

    def sb(self, n, s, d=F32):
        return self.ctx.enter_context(self.nc.sbuf_tensor(f"{self.name}_{n}", s, d))

    def ps(self, n, s):
        return self.ctx.enter_context(self.nc.psum_tensor(f"{self.name}_psum_{n}", s, F32))

    def sem(self, n):
        return self.ctx.enter_context(self.nc.semaphore(f"{self.name}_{n}"))

    def block(self):
        return self.ctx.enter_context(self.nc.Block())


def setup(nc, a, scratch, k):
    with Stage(nc, "setup") as st:
        W3 = 3 * D
        wada = st.sb("wada", [P, 2, W3])
        acc = st.sb("acc", [P, W3])
        ccol = st.sb("ccol", [P, KT]); chalf = st.sb("chalf", [P, KT]); ctan = st.sb("ctan", [P, KT])
        bada = st.sb("bada", [P, 3 * KT]); mod = st.sb("mod", [P, 3 * KT]); nw = st.sb("nw", [P, KT])
        onehot = st.sb("onehot", [BUCKETS, 2 * P]); rel = st.sb("rel", [BUCKETS, H]); brow = st.sb("brow", [H, 2 * P])
        al = st.sb("al", [P, SH]); cw = st.sb("cw", [P, CW, XBC // P]); cb = st.sb("cb", [P, XBC // P])
        qk = st.sb("qk", [P, 2]); flip = st.sb("flip", [P, P]); skew = st.sb("skew", [P, H, P])
        pm = st.ps("mod", [P, 512]); pb = st.ps("bias", [H, 2 * P]); pf = st.ps("flipped", [P, H, P])
        small, onesem, wsem = st.sem("small_loaded"), st.sem("bias_in_loaded"), [st.sem("wada0_loaded"), st.sem("wada1_loaded")]
        consts = st.sem("consts_made")
        ctanh, silu, accd, modp, brp, brs, bst, bld, fin, al_e, chd, modd = [st.sem(n) for n in (
            "c_tanh", "c_silu", "ada_accumulated", "mod_product", "bias_rows_product", "bias_rows_copied",
            "bias_rows_stored", "skew_loaded", "columns_made", "a_exponential", "c_halved", "mod_made")]
        flipped, bias_made = st.sem("bias_flipped"), st.sem("bias_made")
        half = P // 2
        blk = st.block()
        NSMALL, CONSTS = 11, 17

        @blk.sync
        def _(sp):
            sp.dma_start(ccol[:, :], a["c"]).then_inc(small, 16)
            for j in range(KT):
                if j >= 2:
                    sp.wait_ge(accd, j - 1)
                sp.dma_start(wada[:, j % 2, :], a["w_ada"][0, j * P:(j + 1) * P, :]).then_inc(wsem[j % 2], 16)

        @blk.scalar
        def _(act):
            act.dma_start(onehot[:, :], a["onehot"]).then_inc(onesem, 16)
            act.dma_start(rel[:, :], a["rel_bias"]).then_inc(onesem, 16)
            n = 0
            for dst, src in (
                (bada[:, :], a["b_ada"]),
                (nw[:, :], a["norm_w"]),
                (cb[:, :], a["conv_b"]),
                (k["ssmw"][:, :], a["ssm_norm_w"]),
                (qk[:, 0:1], a["q_norm_w"]),
                (qk[:, 1:2], a["k_norm_w"]),
                (k["dtb"][:, :], a["dt_bias"]),
                (k["sink"][:, :], a["sinks"].to_broadcast([P, H])),
                (al[:, :], a["a_log"].to_broadcast([P, SH])),
                (k["dskip"][:, :], a["d_skip"]),
                (cw[:, :, :], a["conv_w"]),
            ):
                act.dma_start(dst, src).then_inc(small, 16)
                n += 1
            assert n == NSMALL
            act.wait_ge(chd, 1)
            nc.scalar.activation(ctan[:, :], chalf[:, :], ACT.Tanh).then_inc(ctanh, 1)
            nc.scalar.activation(al[:, :], al[:, :], ACT.Exp).then_inc(al_e, 1)
            act.wait_ge(brs, 1)
            act.dma_start(scratch["bias"], brow[:, :]).then_inc(bst, 16)
            act.wait_ge(bst, 16)
            act.dma_start(skew[:, :, :], dram_ap(scratch["bias"], 0, [[1, P], [2 * P, H], [1, P]])).then_inc(bld, 16)
            act.wait_ge(flipped, 1)
            nc.scalar.activation(k["bias"][:, :, :], pf[:, :, :], ACT.Copy).then_inc(bias_made, 1)
            act.wait_ge(bias_made, 1)

        @blk.gpsimd
        def _(pool):
            made = [0]

            def const(ins):
                made[0] += 1
                ins.then_inc(consts, 1)
                pool.wait_ge(consts, made[0])

            def select(t, keep, coefficients, fill):
                base, part, col = coefficients
                const(nc.gpsimd.affine_select(out=t[:, :], in_=t[:, :], compare_op=keep, fill=fill, base=base,
                                              pattern=[[col, P]], channel_multiplier=part))

            const(pool.memset(k["eps"][:, :], EPS))
            const(pool.memset(flip[:, :], 0.0))
            select(flip, ALU.not_equal, (1 - P, 1, 1), 1.0)
            const(pool.memset(k["ones"][:, :], 1.0))
            const(pool.memset(k["ident"][:, :], 0.0))
            select(k["ident"], ALU.not_equal, (0, 1, -1), 1.0)
            const(pool.memset(k["triu"][:, :], 1.0))
            select(k["triu"], ALU.is_ge, (0, -1, 1), 0.0)
            const(pool.memset(k["tril"][:, :], 1.0))
            select(k["tril"], ALU.is_gt, (0, 1, -1), 0.0)
            const(pool.memset(k["neg"][:, :], 0.0))
            select(k["neg"], ALU.is_ge, (0, 1, -1), NEG)
            const(pool.memset(k["negcur"][:, :], NEG))
            select(k["negcur"], ALU.is_ge, (0, 1, -1), 0.0)
            const(pool.memset(k["headones"][:, :], 0.0))
            for hh in range(P // HD):
                const(pool.memset(k["headones"][hh * HD:(hh + 1) * HD, hh * HD:(hh + 1) * HD], 1.0))
            assert made[0] == CONSTS

        @blk.tensor
        def _(pe):
            pe.wait_ge(onesem, 32)
            nc.tensor.matmul(pb[:, :], rel[:, :], onehot[:, :], start=True, stop=True).then_inc(brp, 1)
            pe.wait_ge(bld, 16)
            pe.wait_ge(consts, CONSTS)
            for g in range(H * P // MM):
                hs = slice(g * MM // P, (g + 1) * MM // P)
                last = nc.tensor.matmul(pf[:, hs, :], flip[:, :], skew[:, hs, :], start=True, stop=True)
            last.then_inc(flipped, 1)
            pe.wait_ge(accd, KT)
            for m in range(3 * KT):
                last = nc.tensor.matmul(pm[:, m:m + 1], acc[:, m * P:(m + 1) * P], k["ones"][:, 0:1], start=True, stop=True)
            last.then_inc(modp, 1)

        @blk.vector
        def _(dve):
            dve.wait_ge(small, 16 * (NSMALL + 1))
            nc.vector.tensor_scalar(chalf[:, :], ccol[:, :], 0.5, None, ALU.mult).then_inc(chd, 1)
            dve.wait_ge(ctanh, 1)
            nc.vector.scalar_tensor_tensor(chalf[:, :], ctan[:, :], 1.0, chalf[:, :], ALU.add, ALU.mult).then_inc(silu, 1)
            dve.wait_ge(brp, 1)
            nc.vector.tensor_copy(brow[:, :], pb[:, :]).then_inc(brs, 1)
            dve.wait_ge(silu, 1)
            for j in range(KT):
                dve.wait_ge(wsem[j % 2], 16 * (j // 2 + 1))
                if j == 0:
                    nc.vector.tensor_scalar(acc[:, :], wada[:, 0, :], chalf[:, 0:1], None, ALU.mult).then_inc(accd, 1)
                else:
                    dve.wait_ge(accd, j)
                    nc.vector.scalar_tensor_tensor(acc[:, :], wada[:, j % 2, :], chalf[:, j:j + 1], acc[:, :],
                                                   ALU.mult, ALU.add).then_inc(accd, 1)
            nc.vector.tensor_scalar(k["convw"][:, :, :], cw[:, :, :], 0.5, None, ALU.mult)
            nc.vector.tensor_scalar(k["convb"][:, :], cb[:, :], 0.5, None, ALU.mult)
            nc.vector.tensor_scalar(k["qw"][:, :], qk[:, 0:1], HD ** -0.5, None, ALU.mult)
            nc.vector.tensor_copy(k["kw"][:, :], qk[:, 1:2])
            dve.wait_ge(al_e, 1)
            nc.vector.tensor_scalar(k["aneg"][:, :], al[:, :], -1.0, None, ALU.mult)
            dve.wait_ge(modp, 1)
            nc.vector.tensor_tensor(mod[:, :], pm[:, 0:3 * KT], bada[:, :], ALU.add).then_inc(modd, 1)
            dve.wait_ge(modd, 1)
            nc.vector.tensor_copy(k["hshift"][:, :], mod[:, 0:KT])
            nc.vector.scalar_tensor_tensor(k["hscale"][:, :], mod[:, KT:2 * KT], 1.0, nw[:, :], ALU.add, ALU.mult)
            nc.vector.tensor_scalar(k["gate"][:, :], mod[:, 2 * KT:3 * KT], 0.5, None, ALU.mult).then_inc(fin, 1)
            dve.wait_ge(fin, 1)


def normalise(nc, a, k, h):
    h_hi, h_lo = h
    with Stage(nc, "norm") as st:
        x = st.sb("x", [P, 2, D]); xn = st.sb("xn", [P, 2, D]); h32 = st.sb("h32", [P, 2, D])
        ss = st.sb("ss", [P, 2]); root = st.sb("root", [P, 2]); rstd = st.sb("rstd", [P, 2])
        tp = st.ps("tp", [P, 2, D])
        x_loaded = [st.sem("x0_loaded"), st.sem("x1_loaded")]
        squares, rooted, rstd_made, x_normed, transposed, scaled, h_made, hi_made, lo_made = [st.sem(n) for n in (
            "squares", "rooted", "rstd_made", "x_normed", "transposed", "scaled", "h_made", "hi_made", "lo_made")]
        blk = st.block()

        @blk.sync
        def _(sp):
            def load(t, b, j):
                if exists(t - 2):
                    sp.wait_ge(x_normed, t - 1)
                sp.dma_start(x[:, b, :], a["x"][0, bass.ds(t * P, P), :]).then_inc(x_loaded[b], 16)
            pairs(sp, NBLK, load)

        @blk.scalar
        def _(act):
            def norm(t, b, j):
                act.wait_ge(x_loaded[b], 16 * j + 16)
                if exists(t - 2):
                    act.wait_ge(transposed, t - 1)
                nc.scalar.activation(xn[:, b, :], x[:, b, :], ACT.Square, accum_out=ss[:, b:b + 1]).then_inc(squares, 1)
                act.wait_ge(squares, t + 1)
                nc.scalar.activation(root[:, b:b + 1], ss[:, b:b + 1], ACT.Sqrt, bias=k["eps"][:, :], scale=1.0 / D).then_inc(rooted, 1)
                act.wait_ge(rstd_made, t + 1)
                nc.scalar.activation(xn[:, b, :], x[:, b, :], ACT.Copy, scale=rstd[:, b:b + 1]).then_inc(x_normed, 1)
                act.wait_ge(h_made, t + 1)
                nc.scalar.activation(h_hi[:, :, bass.ds(t * P, P)],
                                     h32[:, b, :].rearrange("p (k t) -> p k t", k=KT), ACT.Copy).then_inc(hi_made, 1)
            pairs(act, NBLK, norm)

        @blk.tensor
        def _(pe):
            def turn(t, b, j):
                pe.wait_ge(x_normed, t + 1)
                if exists(t - 2):
                    pe.wait_ge(scaled, t - 1)
                for kk in range(KT):
                    last = nc.tensor.transpose(tp[:, b, kk * P:(kk + 1) * P], xn[:, b, kk * P:(kk + 1) * P], k["ident"][:, :])
                last.then_inc(transposed, 1)
            pairs(pe, NBLK, turn)

        @blk.vector
        def _(dve):
            def split(t, b, j):
                dve.wait_ge(rooted, t + 1)
                nc.vector.reciprocal(rstd[:, b:b + 1], root[:, b:b + 1]).then_inc(rstd_made, 1)
                dve.wait_ge(transposed, t + 1)
                hv = h32[:, b, :].rearrange("p (k t) -> p k t", k=KT)
                nc.vector.tensor_tensor(hv, tp[:, b, :].rearrange("p (k t) -> p k t", k=KT),
                                        k["hscale"][:, :, None].to_broadcast([P, KT, P]), ALU.mult).then_inc(scaled, 1)
                dve.wait_ge(scaled, t + 1)
                nc.vector.tensor_tensor(hv, hv, k["hshift"][:, :, None].to_broadcast([P, KT, P]), ALU.add).then_inc(h_made, 1)
                dve.wait_ge(hi_made, t + 1)
                nc.vector.tensor_tensor(h_lo[:, :, bass.ds(t * P, P)], hv, h_hi[:, :, bass.ds(t * P, P)],
                                        ALU.subtract).then_inc(lo_made, 1)
            pairs(dve, NBLK, split)
            dve.wait_ge(lo_made, NBLK)


def project(nc, a, scratch, k, h):
    h_hi, h_lo = h
    with Stage(nc, "proj") as st:
        raw = st.sb("raw", [P, 2, KT, P])
        w_hi = [st.sb(f"w_hi{b}", [P, KT, P], F32R) for b in range(2)]
        w_lo = [st.sb(f"w_lo{b}", [P, KT, P], F32R) for b in range(2)]
        xin = st.sb("xin", [P, CW - 1 + S]); u = st.sb("u", [P, S]); res = st.sb("res", [P, 2, S])
        acc = st.ps("acc", [P, 2, S])
        w_loaded = [st.sem("w0_loaded"), st.sem("w1_loaded")]
        stored = [st.sem("res0_stored"), st.sem("res1_stored")]
        hi_made, lo_made, multiplied, squared, summed, res_begun, tapped, u_made, inverted, res_made, padded = [
            st.sem(n) for n in ("hi_made", "lo_made", "multiplied", "squared", "summed", "res_begun",
                                "tapped", "u_made", "inverted", "res_made", "padded")]
        blk = st.block()

        def tiles(eng, body):
            n0 = 0
            for kind, col, count, name in KINDS:
                last = n0 + count == NTILES
                looped = 0 if kind == "plain" else (count - 2 if last else count)
                if looped:
                    with eng.Fori(0, looped // 2) as i:
                        for e in range(2):
                            body(2 * i + (n0 + e), (n0 + e) % 2, i + (n0 + e) // 2, kind, col, name, 2 * i + e)
                for e in range(looped, count):
                    body(n0 + e, (n0 + e) % 2, (n0 + e) // 2, kind, col, name, e)
                n0 += count

        before = {}
        for kind, _, count, name in KINDS:
            before[name] = sum(c for kk, _, c, nm in KINDS[:[x[3] for x in KINDS].index(name)] if kk == kind)

        @blk.sync
        def _(sp):
            def load(n, b, j, kind, col, name, e):
                if exists(n - 2):
                    sp.wait_ge(lo_made, n - 1)
                sp.dma_start(raw[:, b, :, :], a["w_in_" + name][bass.ds(e, 1)].rearrange("o p k c -> (o p) k c")).then_inc(w_loaded[b], 16)
            tiles(sp, load)

        @blk.tensor
        def _(pe):
            def product(n, b, j, kind, col, name, e):
                pe.wait_ge(lo_made, n + 1)
                if exists(n - 2):
                    pe.wait_ge(u_made, n - 1)
                for kk in range(KT):
                    for step, (wv, hv) in enumerate(((w_hi[b], h_hi), (w_hi[b], h_lo), (w_lo[b], h_hi))):
                        for c in range(S // MM):
                            last = nc.tensor.matmul(acc[:, b, c * MM:(c + 1) * MM], wv[:, kk, :], hv[:, kk, c * MM:(c + 1) * MM],
                                                    start=(kk == 0 and step == 0), stop=(kk == KT - 1 and step == 2))
                last.then_inc(multiplied, 1)
                if kind == "norm":
                    pe.wait_ge(squared, e + (before[name] + 1))
                    for c in range(S // MM):
                        last = nc.tensor.matmul(acc[:, b, c * MM:(c + 1) * MM], k["headones"][:, :], u[:, c * MM:(c + 1) * MM],
                                                start=True, stop=True)
                    last.then_inc(summed, 1)
            tiles(pe, product)

        @blk.scalar
        def _(act):
            def high(b, j):
                act.wait_ge(w_loaded[b], 16 * j + 16)
                nc.scalar.activation(w_hi[b][:, :, :], raw[:, b, :, :], ACT.Copy).then_inc(hi_made, 1)

            def finish(n, b, j, kind, col, name, e):
                if not (isinstance(n, int) and n == NTILES - 1):
                    high(1 - b, j + b)
                if exists(n - 2):
                    act.wait_ge(stored[b], 16 * j)
                act.wait_ge(multiplied, n + 1)
                src = acc[:, b, :]
                if kind == "plain":
                    nc.scalar.activation(u[:, :], src, ACT.Copy).then_inc(u_made, 1)
                elif kind == "gate":
                    nc.scalar.activation(u[:, :], src, ACT.Tanh, scale=0.5).then_inc(u_made, 1)
                elif kind == "silu":
                    nc.scalar.activation(res[:, b, :], src, ACT.Copy, scale=0.5).then_inc(res_begun, 1)
                    nc.scalar.activation(u[:, :], src, ACT.Tanh, scale=0.5).then_inc(u_made, 1)
                elif kind == "conv":
                    nc.scalar.activation(xin[:, CW - 1:], src, ACT.Copy)
                    nc.scalar.activation(res[:, b, :], src, ACT.Identity, bias=k["convb"][:, bass.ds(e, 1)],
                                         scale=k["convw"][:, CW - 1, bass.ds(e, 1)]).then_inc(res_begun, 1)
                    act.wait_ge(tapped, 3 * e + 3)
                    nc.scalar.activation(u[:, :], res[:, b, :], ACT.Tanh).then_inc(u_made, 1)
                elif kind == "norm":
                    nc.scalar.activation(res[:, b, :], src, ACT.Copy).then_inc(res_begun, 1)
                    nc.scalar.activation(u[:, :], src, ACT.Square).then_inc(squared, 1)
                    act.wait_ge(summed, e + (before[name] + 1))
                    nc.scalar.activation(u[:, :], src, ACT.Sqrt, bias=k["eps"][:, :], scale=1.0 / HD).then_inc(u_made, 1)
                act.wait_ge(res_made, n + 1)
                act.dma_start(scratch[name][bass.ds(e * P, P), :], res[:, b, :]).then_inc(stored[b], 16)

            high(0, 0)
            tiles(act, finish)
            for b in range(2):
                act.wait_ge(stored[b], 16 * ((NTILES + 1 - b) // 2))

        @blk.vector
        def _(dve):
            def low(n, b):
                dve.wait_ge(hi_made, n + 1)
                if exists(n - 2):
                    dve.wait_ge(multiplied, n - 1)
                nc.vector.tensor_tensor(w_lo[b][:, :, :], raw[:, b, :, :], w_hi[b][:, :, :], ALU.subtract).then_inc(lo_made, 1)

            def finish(n, b, j, kind, col, name, e):
                if not (isinstance(n, int) and n == NTILES - 1):
                    low(n + 1, 1 - b)
                if kind == "conv":
                    for c in range(CW - 1):
                        if c == 0:
                            dve.wait_ge(res_begun, e + 1 + BEGUN[name])
                        else:
                            dve.wait_ge(tapped, 3 * e + c)
                        nc.vector.scalar_tensor_tensor(res[:, b, :], xin[:, c:c + S], k["convw"][:, c, bass.ds(e, 1)],
                                                       res[:, b, :], ALU.mult, ALU.add).then_inc(tapped, 1)
                dve.wait_ge(u_made, n + 1)
                if kind == "plain":
                    nc.vector.tensor_copy(res[:, b, :], u[:, :]).then_inc(res_made, 1)
                elif kind == "gate":
                    nc.vector.tensor_scalar(res[:, b, :], u[:, :], 1.0, None, ALU.add).then_inc(res_made, 1)
                elif kind in ("silu", "conv"):
                    nc.vector.scalar_tensor_tensor(res[:, b, :], u[:, :], 1.0, res[:, b, :], ALU.add, ALU.mult).then_inc(res_made, 1)
                elif kind == "norm":
                    nc.vector.reciprocal(u[:, :], u[:, :]).then_inc(inverted, 1)
                    dve.wait_ge(inverted, e + (before[name] + 1))
                    nc.vector.scalar_tensor_tensor(res[:, b, :], res[:, b, :], k[name + "w"][:, :], u[:, :],
                                                   ALU.mult, ALU.mult).then_inc(res_made, 1)

            order = [x for x in KINDS if x[0] in ("norm", "silu", "conv")]
            BEGUN = {x[3]: sum(y[2] for y in order[:i]) for i, x in enumerate(order)}
            dve.memset(xin[:, 0:CW - 1], 0.0).then_inc(padded, 1)
            dve.wait_ge(padded, 1)
            low(0, 0)
            tiles(dve, finish)
            dve.wait_ge(res_made, NTILES)


def decays(nc, scratch, k, dec):
    NCH = NBLK * SH
    TERMS = 8
    with Stage(nc, "decay") as st:
        dtt = st.sb("dtt", [SH, S]); x = st.sb("x", [P, NCH]); u = st.sb("u", [P, NCH]); v = st.sb("v", [P, NCH])
        w = st.sb("w", [P, NCH]); rows = st.sb("rows", [P, 4, P]); dta = st.sb("dta", [P, NCH])
        pt = st.ps("pt", [P, NCH]); pc = st.ps("pc", [P, NCH]); pe_ = st.ps("pe", [P, NCH]); pr = st.ps("pr", [P, 4, P])
        loaded, biased, turned, cumulated, v1, a1, stored, done = [st.sem(n) for n in (
            "loaded", "biased", "turned", "cumulated", "vector_step", "scalar_step", "rows_stored", "done")]
        blk = st.block()

        @blk.sync
        def _(sp):
            sp.dma_start(dtt[:, :], scratch["dt"][0:SH, :]).then_inc(loaded, 16)
            sp.wait_ge(done, 1)
            sp.dma_start(scratch["rowcum"].rearrange("(m p) l -> p m l", p=P), rows[:, :, :]).then_inc(stored, 16)
            sp.wait_ge(stored, 16)

        @blk.tensor
        def _(pe):
            pe.wait_ge(biased, 1)
            for c in range(NBLK):
                last = nc.tensor.transpose(pt[:, c * SH:(c + 1) * SH], dtt[:, c * P:(c + 1) * P], k["ident"][0:SH, 0:SH])
            last.then_inc(turned, 1)
            pe.wait_ge(cumulated, 1)
            nc.tensor.matmul(pc[:, :], k["triu"][:, :], dta[:, :], start=True, stop=True)
            nc.tensor.matmul(pe_[:, :], k["ones"][:, :], dta[:, :], start=True, stop=True)
            for m in range(4):
                last = nc.tensor.matmul(pr[:, m, :], dta[:, m * P:(m + 1) * P], k["triu"][:, :], start=True, stop=True)
            last.then_inc(turned, 1)

        @blk.scalar
        def _(act):
            act.wait_ge(v1, 2)
            nc.scalar.activation(u[:, :], u[:, :], ACT.Exp, scale=-1.0).then_inc(a1, 1)
            act.wait_ge(turned, 2)
            nc.scalar.activation(dec["chunk"][:, :], pe_[:, :], ACT.Exp).then_inc(a1, 1)
            act.wait_ge(v1, 3 + 4 + TERMS + 3)
            nc.scalar.activation(dec["toend"][:, :], w[:, :], ACT.Exp).then_inc(a1, 1)
            act.wait_ge(a1, 3)

        @blk.vector
        def _(dve):
            dve.wait_ge(loaded, 16)
            nc.vector.tensor_scalar(dtt[:, :], dtt[:, :], k["dtb"][:, :], None, ALU.add).then_inc(biased, 1)
            dve.wait_ge(turned, 1)
            step = [0]

            def chain(ins):
                step[0] += 1
                ins.then_inc(v1, 1)
                dve.wait_ge(v1, step[0])

            chain(nc.vector.tensor_copy(x[:, :], pt[:, :]))
            chain(nc.vector.scalar_tensor_tensor(u[:, :], x[:, :], -1.0, x[:, :], ALU.mult, ALU.max))
            dve.wait_ge(a1, 1)
            chain(nc.vector.tensor_scalar(v[:, :], u[:, :], 2.0, None, ALU.add))
            chain(nc.vector.reciprocal(v[:, :], v[:, :]))
            chain(nc.vector.tensor_tensor(u[:, :], u[:, :], v[:, :], ALU.mult))
            chain(nc.vector.tensor_tensor(v[:, :], u[:, :], u[:, :], ALU.mult))
            chain(nc.vector.tensor_scalar(w[:, :], v[:, :], 1.0 / (2 * TERMS + 1), None, ALU.mult))
            for n in range(TERMS - 1, 0, -1):
                chain(nc.vector.scalar_tensor_tensor(w[:, :], w[:, :], 1.0 / (2 * n + 1), v[:, :], ALU.add, ALU.mult))
            chain(nc.vector.scalar_tensor_tensor(w[:, :], w[:, :], 1.0, u[:, :], ALU.add, ALU.mult))
            chain(nc.vector.tensor_scalar(x[:, :], x[:, :], 0.0, None, ALU.max))
            chain(nc.vector.scalar_tensor_tensor(dec["dt"][:, :], w[:, :], 2.0, x[:, :], ALU.mult, ALU.add))
            assert step[0] == 3 + 4 + TERMS + 2
            nc.vector.tensor_tensor(dta[:, :].rearrange("p (c h) -> p c h", h=SH),
                                    dec["dt"][:, :].rearrange("p (c h) -> p c h", h=SH),
                                    k["aneg"][:, None, :].to_broadcast([P, NBLK, SH]), ALU.mult).then_inc(cumulated, 1)
            dve.wait_ge(turned, 2)
            nc.vector.tensor_copy(rows[:, :, :], pr[:, :, :]).then_inc(done, 1)
            nc.vector.tensor_copy(dec["cum"][:, :], pc[:, :]).then_inc(done, 1)
            dve.wait_ge(done, 2)
            dve.wait_ge(a1, 2)
            chain(nc.vector.tensor_tensor(w[:, :], pe_[:, :], dec["cum"][:, :], ALU.subtract))


def mixers(nc, scratch, k, dec):
    assert KV == SG
    G = SG
    XT = R * HD // P
    PAIRS = GRP // 2
    UNITS = 2 * G
    TURNS = NBLK // 2
    with Stage(nc, "mix") as st:
        q = st.sb("q", [P, 2, PAIRS, P]); za = st.sb("za", [P, 2, PAIRS, P]); vt = st.sb("vt", [HD, 2, P])
        bias_cur = st.sb("bias_cur", [P, H, P]); bias_prev = st.sb("bias_prev", [P, H, P])
        keys = [st.sb(f"keys{g}", [P, 2, P]) for g in range(G)]
        vals = [[st.sb(f"vals{g}_{s}", [P, HD]) for s in range(2)] for g in range(G)]
        sc = st.sb("sc", [P, 2, GRP, P]); sp_ = st.sb("sp", [P, GRP, P]); probs = st.sb("probs", [P, GRP, P])
        pcur = st.sb("pcur", [P, GRP, P]); pprev = st.sb("pprev", [P, GRP, P]); carrier = st.sb("carrier", [P, 1])
        mx = st.sb("mx", [P, 2, GRP]); nmx = st.sb("nmx", [P, 2, GRP]); es = st.sb("es", [P, 2, GRP])
        den = st.sb("den", [P, 2, GRP]); rden = st.sb("rden", [P, 2, GRP]); o = st.sb("o", [P, 2, PAIRS, P])
        score = st.ps("score", [P, 2, PAIRS, 2, P])
        p_pt = st.ps("pt", [P, GRP, P]); p_av = st.ps("av", [P, 4, P])
        bt = st.sb("bt", [P, 2, P]); ct = st.sb("ct", [P, 2, P]); xt = st.sb("xt", [P, 2, XT, P]); zt = st.sb("zt", [P, 2, XT, P])
        row = st.sb("row", [P, 2, R, P]); seg = st.sb("seg", [P, 2, R, P]); cx = st.sb("cx", [P, 2, R, P])
        cbm = st.sb("cbm", [P, 2, P]); btok = st.sb("btok", [P, 2, P]); xdt = st.sb("xdt", [P, 2, R, HD]); xend = st.sb("xend", [P, 2, R, HD])
        state = [st.sb(f"state{g}", [P, R, HD]) for g in range(G)]
        y = st.sb("y", [P, 2, XT, P]); ysq = st.sb("ysq", [P, XT, P]); ysum = st.sb("ysum", [P, P])
        logs = st.sb("logs", [P, NBLK * G]); rs = st.sb("rs", [P, NBLK * G]); rs_rows = st.sb("rs_rows", [NBLK * G, P])
        p_xt = st.ps("xt", [P, XT, P]); p_cb = st.ps("cb", [P, 4, P]); p_y = st.ps("y", [P, XT, P]); p_st = st.ps("st", [P, R, HD])
        a_loaded = [st.sem(f"attention_in{b}_loaded") for b in range(2)]
        s_loaded = [st.sem(f"scan_in{b}_loaded") for b in range(2)]
        o_stored = [st.sem(f"o{b}_stored") for b in range(2)]
        y_stored = [st.sem(f"y{b}_stored") for b in range(2)]
        za_loaded = [st.sem(f"attention_gate{b}_loaded") for b in range(2)]
        x_loaded = [st.sem(f"scan_values{b}_loaded") for b in range(2)]
        rs_stored = st.sem("rs_stored")
        A_LOADS, S_LOADS, X_LOADS = 4 * 16, 3 * 16, 2 * 16
        ready, scored, v_turned, v_made, cur_biased, prev_biased, chosen, maxed, sink_maxed, negated, sink_shifted, exp_made, sink_exp, \
            denominated, inverted, normalised, p_turned, p_copied, cur_made, prev_made, weighed, gated = [st.sem(n) for n in (
                "ready", "scored", "v_turned", "v_made", "cur_biased", "prev_biased", "chosen", "maxed", "sink_maxed", "negated",
                "sink_shifted", "exp_made", "sink_exp", "denominated", "inverted", "normalised", "p_turned", "p_copied", "cur_made",
                "prev_made", "weighed", "gated")]
        cb_made, x_turned, b_turned, b_copied, seg_made, masked, xdt_made, xend_made, row_exp, seg_exp, c_scaled, m_made, y_made, \
            states_made, decayed, state_new, skipped, z_gated, squared, halved, y_added, y_summed, logged, rstd_made, rs_turned, rs_copied = [st.sem(n) for n in (
                "cb_made", "x_turned", "b_turned", "b_copied", "seg_made", "masked", "xdt_made", "xend_made", "row_exp", "seg_exp",
                "c_scaled", "m_made", "y_made", "states_made", "decayed", "state_new", "skipped", "z_gated", "squared", "halved",
                "y_added", "y_summed", "logged", "rstd_made", "rs_turned", "rs_copied")]
        blk = st.block()
        p_sums = p_cb[:, 2, 0:NBLK * G].rearrange("p (s g i) -> p s g i", s=2, g=G)
        b_psum = p_st[:, 0:P // HD, :].rearrange("p r d -> p (r d)")

        def ahead(i, m, by):
            return (i, m + by) if m + by < UNITS else (i + 1, m + by - UNITS)

        def steps(eng, step):
            for m in range(UNITS):
                step(0, m, UNITS)
            with eng.Fori(1, TURNS - 1) as i:
                for m in range(UNITS):
                    step(i, m, UNITS)
            for m in range(UNITS):
                step(TURNS - 1, m, UNITS - 1 - m)

        def heads(t):
            return t.rearrange("q (half pair) k -> q half pair k", half=2)

        def loads(b, i, m):
            return i * (UNITS // 2) + (m // 2 + 1)

        @blk.sync
        def _(sp):
            def load_first(i, m):
                g, b, s = m % G, m % 2, m // G
                t = bass.ds((i * 2 + s) * P, P)
                src = scratch["rowcum"][bass.ds((i * 2 + s) * SH + g * R, R), :].rearrange("(o h) l -> o h l", o=1)
                sp.dma_start(row[:, b, :, :], src.to_broadcast([P, R, P])).then_inc(s_loaded[b], 16)
                sp.dma_start(bt[:, b, :], scratch["xbc"][SW + g * SN:SW + (g + 1) * SN, t]).then_inc(s_loaded[b], 16)
                sp.dma_start(ct[:, b, :], scratch["xbc"][SW + (SG + g) * SN:SW + (SG + g + 1) * SN, t]).then_inc(s_loaded[b], 16)
                sp.dma_start(q[:, b, :, :], scratch["q"][g * GRP * HD:(g + 1) * GRP * HD, t].rearrange("(c p) t -> p c t", p=P)).then_inc(a_loaded[b], 16)
                sp.dma_start(keys[g][0:HD, s, :], scratch["k"][g * HD:(g + 1) * HD, t]).then_inc(a_loaded[b], 16)
                sp.dma_start(keys[g][HD:P, s, :], scratch["k"][g * HD:(g + 1) * HD, t]).then_inc(a_loaded[b], 16)
                sp.dma_start(vt[:, b, :], scratch["v"][g * HD:(g + 1) * HD, t]).then_inc(a_loaded[b], 16)

            def load_values(i, m):
                g, b, s = m % G, m % 2, m // G
                t, xr = bass.ds((i * 2 + s) * P, P), slice(g * R * HD, (g + 1) * R * HD)
                sp.dma_start(xt[:, b, :, :], scratch["xbc"][xr, t].rearrange("(c p) t -> p c t", p=P)).then_inc(x_loaded[b], 16)
                sp.dma_start(zt[:, b, :, :], scratch["zm"][xr, t].rearrange("(c p) t -> p c t", p=P)).then_inc(x_loaded[b], 16)

            def load_gate(i, m):
                g, b, s = m % G, m % 2, m // G
                sp.dma_start(za[:, b, :, :], scratch["za"][g * GRP * HD:(g + 1) * GRP * HD, bass.ds((i * 2 + s) * P, P)]
                             .rearrange("(c p) t -> p c t", p=P)).then_inc(za_loaded[b], 16)

            def step(i, m, left):
                n, g, b, s = i * UNITS + m, m % G, m % 2, m // G
                t = bass.ds((i * 2 + s) * P, P)
                if left >= 2:
                    sp.wait_ge(b_turned, n + 1)
                    sp.wait_ge(seg_made, n + 1)
                    sp.wait_ge(c_scaled, n + 1)
                    load_first(*ahead(i, m, 2))
                sp.wait_ge(ready, 1)
                sp.wait_ge(z_gated, n + 1)
                sp.dma_start(scratch["y"][g * R * HD:(g + 1) * R * HD, t].rearrange("(c p) t -> p c t", p=P), y[:, b, :, :]).then_inc(y_stored[b], 16)
                if left >= 2:
                    load_values(*ahead(i, m, 2))
                sp.wait_ge(gated, n + 1)
                sp.dma_start(scratch["attn"][g * GRP * HD:(g + 1) * GRP * HD, t].rearrange("(c p) t -> p c t", p=P), o[:, b, :, :]).then_inc(o_stored[b], 16)
                if left >= 2:
                    load_gate(*ahead(i, m, 2))

            for m in range(2):
                load_first(0, m)
                load_values(0, m)
                load_gate(0, m)
            steps(sp, step)
            sp.wait_ge(rs_copied, 1)
            to = scratch["rs"].rearrange("(g c) (i s t) -> s g i c t", c=XT, s=2, t=P)
            for s in range(2):
                for g in range(G):
                    r0 = (s * G + g) * TURNS
                    sp.dma_start(to[s, g], rs_rows[r0:r0 + TURNS, None, :].to_broadcast([TURNS, XT, P])).then_inc(rs_stored, 16)
            sp.wait_ge(rs_stored, 16 * 2 * G)
            for b in range(2):
                sp.wait_ge(o_stored[b], 16 * NBLK * G // 2)
                sp.wait_ge(y_stored[b], 16 * NBLK * G // 2)

        @blk.tensor
        def _(pe):
            def scores(i, m):
                n, g, b, s = i * UNITS + m, m % G, m % 2, m // G
                if exists(n - 2):
                    pe.wait_ge(gated, n - 1)
                pe.wait_ge(a_loaded[b], A_LOADS * loads(b, i, m))
                if exists(n - 1):
                    if exists(n - 1 - G):
                        pe.wait_ge(prev_biased, n - G)
                    else:
                        pe.wait_ge(cur_biased, n)
                both = exists(n - G)
                for h in range(GRP):
                    half, pair = h % 2, h // 2
                    r = slice(HD * half, HD * half + HD)
                    if both:
                        last = nc.tensor.matmul(score[:, half, pair, :, :], q[r, b, pair, :], keys[g][r, :, :], start=True, stop=True)
                    else:
                        last = nc.tensor.matmul(score[:, half, pair, s, :], q[r, b, pair, :], keys[g][r, s, :], start=True, stop=True)
                last.then_inc(scored, 1)
                nc.tensor.transpose(p_av[:, 2, 0:HD], vt[:, b, :], k["ident"][0:HD, 0:HD]).then_inc(v_turned, 1)

            def turn_p(i, m):
                n, b = i * UNITS + m, m % 2
                pe.wait_ge(normalised, n + 1)
                if exists(n - 1):
                    pe.wait_ge(p_copied, n)
                for h in range(GRP):
                    last = nc.tensor.transpose(p_pt[:, h, :], sc[:, b, h, :], k["ident"][:, :])
                last.then_inc(p_turned, 1)

            def weigh(i, m, more):
                n, g, s = i * UNITS + m, m % G, m // G
                both = exists(n - G)
                pe.wait_ge(v_made, n + (2 if more else 1))
                if exists(n - 1):
                    pe.wait_ge(gated, n)
                pe.wait_ge(cur_made, n + 1)
                if both:
                    pe.wait_ge(prev_made, n + 1 - G)
                for half in range(2):
                    to = p_av[HD * half:HD * half + HD, 0:PAIRS, :]
                    hs = slice(PAIRS * half, PAIRS * half + PAIRS)
                    last = nc.tensor.matmul(to, vals[g][s][:, :], pcur[:, hs, :], start=True, stop=not both)
                    if both:
                        last = nc.tensor.matmul(to, vals[g][1 - s][:, :], pprev[:, hs, :], start=False, stop=True)
                last.then_inc(weighed, 1)

            def prepare(i, m):
                n, b = i * UNITS + m, m % 2
                pe.wait_ge(s_loaded[b], S_LOADS * loads(b, i, m))
                if exists(n - 1):
                    pe.wait_ge(masked, n)
                nc.tensor.matmul(p_cb[:, 0, :], bt[:, b, :], ct[:, b, :], start=True, stop=True).then_inc(cb_made, 1)
                if exists(n - 1):
                    pe.wait_ge(xdt_made, n)
                pe.wait_ge(x_loaded[b], X_LOADS * loads(b, i, m))
                for c in range(XT):
                    last = nc.tensor.transpose(p_xt[:, c, :], xt[:, b, c, :], k["ident"][:, :])
                last.then_inc(x_turned, 1)
                if exists(n - 1):
                    pe.wait_ge(state_new, n + G)
                nc.tensor.transpose(b_psum, bt[:, b, :], k["ident"][:, :]).then_inc(b_turned, 1)

            def outputs(i, m):
                n, g, b = i * UNITS + m, m % G, m % 2
                pe.wait_ge(xdt_made, n + 1)
                pe.wait_ge(m_made, n + 1)
                pe.wait_ge(c_scaled, n + 1)
                pe.wait_ge(state_new, n + 1)
                if exists(n - 1):
                    pe.wait_ge(skipped, n)
                for r in range(R):
                    to = p_y[HD * (r % 2):HD * (r % 2) + HD, r // 2, :]
                    nc.tensor.matmul(to, xdt[:, b, r, :], seg[:, b, r, :], start=True, stop=False)
                    last = nc.tensor.matmul(to, state[g][:, r, :], cx[:, b, r, :], start=False, stop=True)
                last.then_inc(y_made, 1)
                pe.wait_ge(b_copied, n + 1)
                pe.wait_ge(xend_made, n + 1)
                nc.tensor.matmul(p_st[:, :, :], btok[:, b, :], xend[:, b, :, :], start=True, stop=True).then_inc(states_made, 1)

            def norm(i, m, more):
                n = i * UNITS + m
                pe.wait_ge(y_added, n + 1)
                if more:
                    pe.wait_ge(masked, n + 2)
                nc.tensor.matmul(p_sums[:, m // G, m % G, bass.ds(i, 1)], ysum[:, :], k["ones"][:, 0:1], start=True, stop=True).then_inc(y_summed, 1)

            def step(i, m, left):
                outputs(i, m)
                turn_p(i, m)
                if left:
                    scores(*ahead(i, m, 1))
                    prepare(*ahead(i, m, 1))
                weigh(i, m, left)
                norm(i, m, left)

            pe.wait_ge(ready, 1)
            scores(0, 0)
            prepare(0, 0)
            steps(pe, step)
            pe.wait_ge(rstd_made, 1)
            nc.tensor.transpose(p_cb[0:NBLK * G, 0, :], rs[:, :], k["ident"][:, :]).then_inc(rs_turned, 1)

        @blk.scalar
        def _(act):
            def copies(i, m):
                n, g, b, s = i * UNITS + m, m % G, m % 2, m // G
                act.wait_ge(v_turned, n + 1)
                nc.scalar.activation(vals[g][s][:, :], p_av[:, 2, 0:HD], ACT.Copy).then_inc(v_made, 1)
                act.wait_ge(b_turned, n + 1)
                nc.scalar.activation(btok[:, b, :], b_psum, ACT.Copy).then_inc(b_copied, 1)
                act.wait_ge(seg_made, n + 1)
                nc.scalar.activation(seg[:, b, :, :], seg[:, b, :, :], ACT.Exp).then_inc(seg_exp, 1)

            def row_exponential(i, m):
                n, b = i * UNITS + m, m % 2
                act.wait_ge(s_loaded[b], S_LOADS * loads(b, i, m))
                if exists(n - 2):
                    act.wait_ge(y_made, n - 1)
                nc.scalar.activation(cx[:, b, :, :], row[:, b, :, :], ACT.Exp).then_inc(row_exp, 1)

            def step(i, m, left):
                n, b = i * UNITS + m, m % 2
                act.wait_ge(negated, n + 1)
                for h in range(GRP):
                    last = nc.scalar.activation(sc[:, b, h, :], sc[:, b, h, :], ACT.Exp, bias=nmx[:, b, h:h + 1], accum_out=den[:, b, h:h + 1])
                last.then_inc(exp_made, 1)
                act.wait_ge(sink_shifted, n + 1)
                nc.scalar.activation(es[:, b, :], es[:, b, :], ACT.Exp).then_inc(sink_exp, 1)
                if left:
                    row_exponential(*ahead(i, m, 1))
                act.wait_ge(p_turned, n + 1)
                if exists(n - 1):
                    act.wait_ge(cur_made, n)
                nc.scalar.activation(probs[:, :, :], p_pt[:, :, :], ACT.Copy).then_inc(p_copied, 1)
                act.wait_ge(z_gated, n + 1)
                if exists(n - 1):
                    act.wait_ge(halved, n)
                nc.scalar.activation(ysq[:, :, :], y[:, b, :, :], ACT.Square).then_inc(squared, 1)
                if left:
                    copies(*ahead(i, m, 1))

            row_exponential(0, 0)
            copies(0, 0)
            steps(act, step)
            act.wait_ge(y_summed, NBLK * G)
            act.wait_ge(masked, NBLK * G)
            nc.scalar.activation(logs[:, :], p_cb[:, 2, 0:NBLK * G], ACT.Ln, bias=k["eps"][:, :], scale=1.0 / (R * HD)).then_inc(logged, 1)
            act.wait_ge(logged, 1)
            nc.scalar.activation(rs[:, :], logs[:, :], ACT.Exp, scale=-0.5).then_inc(rstd_made, 1)
            act.wait_ge(rs_turned, 1)
            nc.scalar.activation(rs_rows[:, :], p_cb[0:NBLK * G, 0, :], ACT.Copy).then_inc(rs_copied, 1)

        @blk.gpsimd
        def _(pool):
            def end_inputs(i, m):
                n, g, b, s = i * UNITS + m, m % G, m % 2, m // G
                pool.wait_ge(ready, 1)
                pool.wait_ge(xdt_made, n + 1)
                if exists(n - 2):
                    pool.wait_ge(states_made, n - 1)
                nc.gpsimd.tensor_tensor(xend[:, b, :, :], xdt[:, b, :, :],
                                        dec["toend"][:, bass.ds((i * 2 + s) * SH + g * R, R)][:, :, None].to_broadcast([P, R, HD]),
                                        ALU.mult).then_inc(xend_made, 1)

            def step(i, m, left):
                n, g, b, s = i * UNITS + m, m % G, m % 2, m // G
                pool.wait_ge(ready, 1)
                pool.wait_ge(y_made, n + 1)
                nc.gpsimd.tensor_tensor(state[g][:, :, :], state[g][:, :, :],
                                        dec["chunk"][:, bass.ds((i * 2 + s) * SH + g * R, R)][:, :, None].to_broadcast([P, R, HD]),
                                        ALU.mult).then_inc(decayed, 1)
                pool.wait_ge(ready, 1)
                pool.wait_ge(p_copied, n + 1)
                if exists(n - 1):
                    pool.wait_ge(weighed, n)
                if m == 0:
                    nc.gpsimd.tensor_tensor(carrier[:, :], k["ones"][:, 0:1], k["ones"][:, 0:1], ALU.add)
                if exists(n - G):
                    nc.gpsimd.affine_select(out=pprev[:, :, :], in_=probs[:, :, :], compare_op=ALU.is_gt, fill=0.0, base=0,
                                            pattern=[[0, GRP], [-1, P]], channel_multiplier=1).then_inc(prev_made, 1)
                nc.gpsimd.affine_select(out=pcur[:, :, :], in_=probs[:, :, :], compare_op=ALU.is_ge, fill=0.0, base=0,
                                        pattern=[[0, GRP], [1, P]], channel_multiplier=-1).then_inc(cur_made, 1)
                pool.wait_ge(squared, n + 1)
                nc.gpsimd.tensor_tensor(ysq[:, 0:XT // 2, :], ysq[:, 0:XT // 2, :], ysq[:, XT // 2:XT, :], ALU.add).then_inc(halved, 1)
                pool.wait_ge(halved, n + 1)
                if exists(n - 1):
                    pool.wait_ge(y_summed, n)
                nc.gpsimd.tensor_tensor(ysum[:, :], ysq[:, 0, :], ysq[:, 1, :], ALU.add).then_inc(y_added, 1)
                if left:
                    end_inputs(*ahead(i, m, 1))

            end_inputs(0, 0)
            steps(pool, step)
            pool.wait_ge(y_added, NBLK * G)

        @blk.vector
        def _(dve):
            def softmax_in(i, m):
                n, g, b, s = i * UNITS + m, m % G, m % 2, m // G
                hs = slice(g * GRP, (g + 1) * GRP)
                bcv, bpv = (t[:, hs, :].rearrange("q (pair half) k -> q half pair k", half=2) for t in (bias_cur, bias_prev))
                dve.wait_ge(scored, n + 1)
                nc.vector.tensor_tensor(heads(sc[:, b, :, :]), score[:, :, :, s, :], bcv, ALU.add).then_inc(cur_biased, 1)
                if exists(n - G):
                    nc.vector.tensor_tensor(heads(sp_[:, :, :]), score[:, :, :, 1 - s, :], bpv, ALU.add).then_inc(prev_biased, 1)
                    dve.wait_ge(cur_biased, n + 1)
                    dve.wait_ge(prev_biased, n + 1 - G)
                    nc.vector.tensor_tensor(sc[:, b, :, :], sc[:, b, :, :], sp_[:, :, :], ALU.max).then_inc(chosen, 1)
                    dve.wait_ge(chosen, n + 1 - G)
                dve.wait_ge(cur_biased, n + 1)
                nc.vector.tensor_reduce(mx[:, b, :], sc[:, b, :, :], AX, ALU.max).then_inc(maxed, 1)
                dve.wait_ge(maxed, n + 1)
                mxv, nmv, esv = (t[:, b, :].rearrange("q (half pair) -> q half pair", half=2) for t in (mx, nmx, es))
                sink = k["sink"][:, hs].rearrange("q (pair half) -> q half pair", half=2)
                nc.vector.tensor_tensor(mxv, mxv, sink, ALU.max).then_inc(sink_maxed, 1)
                dve.wait_ge(sink_maxed, n + 1)
                nc.vector.tensor_scalar(nmx[:, b, :], mx[:, b, :], -1.0, None, ALU.mult).then_inc(negated, 1)
                nc.vector.tensor_tensor(esv, sink, mxv, ALU.subtract).then_inc(sink_shifted, 1)

            def softmax_out(i, m):
                n, b = i * UNITS + m, m % 2
                dve.wait_ge(exp_made, n + 1)
                dve.wait_ge(sink_exp, n + 1)
                nc.vector.tensor_tensor(den[:, b, :], den[:, b, :], es[:, b, :], ALU.add).then_inc(denominated, 1)
                dve.wait_ge(denominated, n + 1)
                nc.vector.reciprocal(rden[:, b, :], den[:, b, :]).then_inc(inverted, 1)
                dve.wait_ge(inverted, n + 1)
                nc.vector.tensor_tensor(sc[:, b, :, :], sc[:, b, :, :], rden[:, b, :, None].to_broadcast([P, GRP, P]), ALU.mult).then_inc(normalised, 1)

            def gate(i, m):
                n, b = i * UNITS + m, m % 2
                dve.wait_ge(weighed, n + 1)
                dve.wait_ge(za_loaded[b], 16 * loads(b, i, m))
                if exists(n - 2):
                    dve.wait_ge(o_stored[b], 16 * (i * (UNITS // 2) + m // 2))
                nc.vector.tensor_tensor(o[:, b, :, :], p_av[:, 0:PAIRS, :], za[:, b, :, :], ALU.mult).then_inc(gated, 1)

            def segments(i, m):
                n, g, b, s = i * UNITS + m, m % G, m % 2, m // G
                dve.wait_ge(s_loaded[b], S_LOADS * loads(b, i, m))
                if exists(n - 2):
                    dve.wait_ge(y_made, n - 1)
                for r in range(R):
                    last = nc.vector.tensor_scalar(seg[:, b, r, :], row[:, b, r, :], dec["cum"][:, bass.ds((i * 2 + s) * SH + (g * R + r), 1)], 0.0,
                                                   ALU.subtract, ALU.min)
                last.then_inc(seg_made, 1)
                dve.wait_ge(cb_made, n + 1)
                nc.vector.tensor_tensor(cbm[:, b, :], p_cb[:, 0, :], k["triu"][:, :], ALU.mult).then_inc(masked, 1)
                dve.wait_ge(x_turned, n + 1)
                if exists(n - 2):
                    dve.wait_ge(xend_made, n - 1)
                nc.vector.tensor_tensor(xdt[:, b, :, :], p_xt[:, :, :].rearrange("p c (h d) -> p (c h) d", d=HD),
                                        dec["dt"][:, bass.ds((i * 2 + s) * SH + g * R, R)][:, :, None].to_broadcast([P, R, HD]), ALU.mult).then_inc(xdt_made, 1)

            def scaled(i, m):
                n, b = i * UNITS + m, m % 2
                dve.wait_ge(row_exp, n + 1)
                nc.vector.tensor_tensor(cx[:, b, :, :], cx[:, b, :, :], ct[:, b, None, :].to_broadcast([P, R, P]), ALU.mult).then_inc(c_scaled, 1)
                dve.wait_ge(seg_exp, n + 1)
                dve.wait_ge(masked, n + 1)
                nc.vector.tensor_tensor(seg[:, b, :, :], seg[:, b, :, :], cbm[:, b, None, :].to_broadcast([P, R, P]), ALU.mult).then_inc(m_made, 1)

            def outputs(i, m):
                n, g, b = i * UNITS + m, m % G, m % 2
                dve.wait_ge(y_made, n + 1)
                dve.wait_ge(x_loaded[b], X_LOADS * loads(b, i, m))
                if exists(n - 2):
                    dve.wait_ge(squared, n - 1)
                    dve.wait_ge(y_stored[b], 16 * (i * (UNITS // 2) + m // 2))
                for c in range(XT):
                    last = nc.vector.scalar_tensor_tensor(y[:, b, c, :], xt[:, b, c, :], k["dskip"][:, g * XT + c:g * XT + c + 1], p_y[:, c, :],
                                                          ALU.mult, ALU.add)
                last.then_inc(skipped, 1)
                dve.wait_ge(skipped, n + 1)
                nc.vector.tensor_tensor(y[:, b, :, :], y[:, b, :, :], zt[:, b, :, :], ALU.mult).then_inc(z_gated, 1)
                dve.wait_ge(states_made, n + 1)
                dve.wait_ge(decayed, n + 1)
                nc.vector.tensor_tensor(state[g][:, :, :], state[g][:, :, :], p_st[:, :, :], ALU.add).then_inc(state_new, 1)

            def step(i, m, left):
                softmax_out(i, m)
                outputs(i, m)
                if left:
                    segments(*ahead(i, m, 1))
                    softmax_in(*ahead(i, m, 1))
                gate(i, m)
                if left:
                    scaled(*ahead(i, m, 1))

            for g in range(G):
                nc.vector.memset(state[g][:, :, :], 0.0).then_inc(state_new, 1)
            nc.vector.tensor_tensor(bias_cur[:, :, :], k["bias"][:, :, :], k["neg"][:, None, :].to_broadcast([P, H, P]), ALU.add).then_inc(ready, 1)
            nc.vector.tensor_tensor(bias_prev[:, :, :], k["bias"][:, :, :], k["negcur"][:, None, :].to_broadcast([P, H, P]), ALU.add).then_inc(ready, 1)
            dve.wait_ge(state_new, G)
            dve.wait_ge(ready, 2)
            segments(0, 0)
            softmax_in(0, 0)
            scaled(0, 0)
            steps(dve, step)
            dve.wait_ge(state_new, G + NBLK * G)


def merge(nc, a, scratch, k, out):
    HALF = S // 2
    PASSES = [(half, what) for half in range(2) for what in ("attn", "y0", "y1")] + [(0, "out"), (1, "out")]
    NJ = D // P
    TT = HALF // P
    LAST = NJ * len(PASSES) - 1
    PART = {"y0": 0, "y1": KT}
    normed_before = [KT * sum(w in PART for _, w in PASSES[:p]) for p in range(len(PASSES) + 1)]

    with Stage(nc, "merge") as st:
        a_raw = st.sb("a_raw", [P, 2, HALF]); rs_row = st.sb("rs_row", [P, 2, HALF])
        rs_loaded = [st.sem(f"rs{b}_loaded") for b in range(2)]
        a_hi = [st.sb(f"a_hi{b}", [P, KT, HALF], F32R) for b in range(2)]
        a_lo = [st.sb(f"a_lo{b}", [P, KT, HALF], F32R) for b in range(2)]
        raw = st.sb("raw", [P, 2, KT, P])
        w_hi = [st.sb(f"w_hi{b}", [P, KT, P], F32R) for b in range(2)]
        w_lo = [st.sb(f"w_lo{b}", [P, KT, P], F32R) for b in range(2)]
        side = st.sb("side", [P, 2, HALF])
        prev = st.sb("prev", [P, 2, HALF])
        res = st.sb("res", [P, 2, HALF])
        acc = st.ps("acc", [P, 2, HALF]); tok = st.ps("tok", [P, 2, TT, P])
        w_loaded = [st.sem(f"w{b}_loaded") for b in range(2)]
        a_loaded = [st.sem(f"a{b}_loaded") for b in range(2)]
        side_loaded = [st.sem(f"side{b}_loaded") for b in range(2)]
        prev_loaded = [st.sem(f"prev{b}_loaded") for b in range(2)]
        stored = [st.sem(f"res{b}_stored") for b in range(2)]
        a_normed, w_hi_made, w_lo_made, a_hi_made, a_lo_made, multiplied, gated, out_gated, turned, res_made = [st.sem(n) for n in (
            "a_normed", "w_hi_made", "w_lo_made", "a_hi_made", "a_lo_made", "multiplied", "gated", "out_gated", "turned", "res_made")]
        blk = st.block()
        weight = {"attn": a["w_attn_proj"], "y0": a["w_ssm_proj_0"], "y1": a["w_ssm_proj_1"], "out": a["w_out"]}
        source = {"attn": scratch["attn"], "y0": scratch["y"][0:D, :], "y1": scratch["y"][D:2 * D, :], "out": scratch["m"]}
        OUT0 = NJ * sum(w != "out" for _, w in PASSES)

        def tiles(eng, body):
            for p in range(len(PASSES)):
                lo, hi = (1 if p == 0 else 0), NJ // 2 - (1 if p == len(PASSES) - 1 else 0)
                n0 = NJ * p
                if lo:
                    for b in range(2):
                        body(b, b, 0, p, b)
                with eng.Fori(lo, hi) as i:
                    for b in range(2):
                        body(2 * i + (n0 + b), b, i + n0 // 2, p, 2 * i + b)
                if hi < NJ // 2:
                    for b in range(2):
                        body(LAST - 1 + b, b, LAST // 2, p, NJ - 2 + b)

        @blk.sync
        def _(sp):
            def chunk(c, b, h, p, j):
                half, what = PASSES[p]
                if exists(c - 2):
                    sp.wait_ge(a_lo_made, c - 1)
                sp.dma_start(a_raw[:, b, :], source[what][bass.ds(j * P, P), half * HALF:(half + 1) * HALF]).then_inc(a_loaded[b], 16)
                if what in PART:
                    rs = scratch["rs"][PART[what]:PART[what] + KT, half * HALF:(half + 1) * HALF][bass.ds(j, 1), :]
                    sp.dma_start(rs_row[:, b, :], rs.to_broadcast([P, HALF])).then_inc(rs_loaded[b], 16)

            def load(n, b, h, p, j):
                half, what = PASSES[p]
                cols = slice(half * HALF, (half + 1) * HALF)
                row = j * P if isinstance(j, int) else sp.snap(j * P)
                if exists(n - 2):
                    sp.wait_ge(w_lo_made, n - 1)
                sp.dma_start(raw[:, b, :, :], weight[what][bass.ds(j, 1)].rearrange("o p k c -> (o p) k c")).then_inc(w_loaded[b], 16)
                if p + 1 < len(PASSES):
                    if PASSES[p + 1][1] == "out":
                        for bb in range(2):
                            sp.wait_ge(stored[bb], 16 * (NJ // 2) * (3 * (PASSES[p + 1][0] + 1)))
                    chunk(n + KT, b, h + KT // 2, p + 1, j)
                if what in ("y0", "y1"):
                    sp.wait_ge(stored[b], 16 * (h - 3))
                if what == "out":
                    sp.wait_ge(a_lo_made, KT)
                if exists(n - 2):
                    sp.wait_ge(res_made, n - 1)
                if what == "out":
                    sp.dma_start(side[:, b, :].rearrange("p (t c) -> p t c", c=P),
                                 a["x"][0, cols, bass.ds(row, P)].rearrange("(t p) c -> p t c", p=P)).then_inc(side_loaded[b], 16)
                else:
                    g0 = 0 if what == "attn" else D
                    sp.dma_start(side[:, b, :], scratch["g"][g0:g0 + D][bass.ds(row, P), cols]).then_inc(side_loaded[b], 16)
                if what in ("y0", "y1"):
                    sp.dma_start(prev[:, b, :], scratch["m"][bass.ds(row, P), cols]).then_inc(prev_loaded[b], 16)

            for b in range(2):
                chunk(b, b, 0, 0, b)
            with sp.Fori(1, KT // 2) as i:
                for b in range(2):
                    chunk(2 * i + b, b, i, 0, 2 * i + b)
            tiles(sp, load)

        @blk.gpsimd
        def _(pool):
            def store(n, b, h, p, j):
                half, what = PASSES[p]
                pool.wait_ge(res_made, n + 1)
                if what == "out":
                    pool.dma_start(out[0, half * HALF:(half + 1) * HALF, bass.ds(j * P, P)].rearrange("(t p) c -> p t c", p=P),
                                   res[:, b, :].rearrange("p (t c) -> p t c", c=P)).then_inc(stored[b], 16)
                else:
                    pool.dma_start(scratch["m"][bass.ds(j * P, P), half * HALF:(half + 1) * HALF], res[:, b, :]).then_inc(stored[b], 16)
            tiles(pool, store)
            for b in range(2):
                pool.wait_ge(stored[b], 16 * (LAST + 1) // 2)

        @blk.tensor
        def _(pe):
            def product(n, b, h, p, j):
                half, what = PASSES[p]
                s = p % 2
                pe.wait_ge(w_lo_made, n + 1)
                pe.wait_ge(a_lo_made, KT * (p + 1))
                if exists(n - 2):
                    pe.wait_ge(res_made, n - 1)
                for kk in range(KT):
                    for step, (wv, av) in enumerate(((w_hi[b], a_hi[s]), (w_hi[b], a_lo[s]), (w_lo[b], a_hi[s]))):
                        for c in range(HALF // MM):
                            last = nc.tensor.matmul(acc[:, b, c * MM:(c + 1) * MM], wv[:, kk, :], av[:, kk, c * MM:(c + 1) * MM],
                                                    start=(kk == 0 and step == 0), stop=(kk == KT - 1 and step == 2))
                last.then_inc(multiplied, 1)
                if what == "out":
                    pe.wait_ge(out_gated, n - (OUT0 - 1))
                    for t in range(TT):
                        last = nc.tensor.transpose(tok[:, b, t, :], prev[:, b, t * P:(t + 1) * P], k["ident"][:, :])
                    last.then_inc(turned, 1)
            tiles(pe, product)

        @blk.scalar
        def _(act):
            def high_w(b, h):
                act.wait_ge(w_loaded[b], 16 * h + 16)
                nc.scalar.activation(w_hi[b][:, :, :], raw[:, b, :, :], ACT.Copy).then_inc(w_hi_made, 1)

            def high_a(c, b, h, p, j):
                if PASSES[p][1] in PART:
                    act.wait_ge(a_normed, c - (KT * p - normed_before[p] - 1))
                else:
                    act.wait_ge(a_loaded[b], 16 * h + 16)
                nc.scalar.activation(a_hi[p % 2][:, bass.ds(j, 1), :], a_raw[:, b, None, :], ACT.Copy).then_inc(a_hi_made, 1)

            def step(n, b, h, p, j):
                if not (isinstance(n, int) and n == LAST):
                    if exists(n - 1):
                        act.wait_ge(multiplied, n)
                    high_w(1 - b, h + b)
                if p + 1 < len(PASSES):
                    high_a(n + KT, b, h + KT // 2, p + 1, j)
                if PASSES[p][1] == "out":
                    act.wait_ge(multiplied, n + 1)
                    nc.scalar.activation(prev[:, b, :], acc[:, b, :], ACT.Copy, scale=k["gate"][:, bass.ds(j, 1)]).then_inc(out_gated, 1)

            for b in range(2):
                high_a(b, b, 0, 0, b)
            with act.Fori(1, KT // 2) as i:
                for b in range(2):
                    high_a(2 * i + b, b, i, 0, 2 * i + b)
            high_w(0, 0)
            tiles(act, step)

        @blk.vector
        def _(dve):
            def low_w(n, b):
                dve.wait_ge(w_hi_made, n + 1)
                if exists(n - 2):
                    dve.wait_ge(multiplied, n - 1)
                nc.vector.tensor_tensor(w_lo[b][:, :, :], raw[:, b, :, :], w_hi[b][:, :, :], ALU.subtract).then_inc(w_lo_made, 1)

            def low_a(c, b, h, p, j):
                dve.wait_ge(a_hi_made, c + 1)
                nc.vector.tensor_tensor(a_lo[p % 2][:, bass.ds(j, 1), :], a_raw[:, b, None, :], a_hi[p % 2][:, bass.ds(j, 1), :], ALU.subtract).then_inc(a_lo_made, 1)

            def norm_a(c, b, h, p, j):
                if PASSES[p][1] not in PART:
                    return
                part = PART[PASSES[p][1]]
                dve.wait_ge(a_loaded[b], 16 * h + 16)
                dve.wait_ge(rs_loaded[b], 16 * (h - (KT * p - normed_before[p]) // 2) + 16)
                nc.vector.scalar_tensor_tensor(a_raw[:, b, :], a_raw[:, b, :], k["ssmw"][:, part:part + KT][:, bass.ds(j, 1)], rs_row[:, b, :],
                                               ALU.mult, ALU.mult).then_inc(a_normed, 1)

            def step(n, b, h, p, j):
                what = PASSES[p][1]
                if not (isinstance(n, int) and n == LAST):
                    low_w(n + 1, 1 - b)
                if p + 1 < len(PASSES):
                    norm_a(n + KT, b, h + KT // 2, p + 1, j)
                    low_a(n + KT, b, h + KT // 2, p + 1, j)
                dve.wait_ge(side_loaded[b], 16 * h + 16)
                if exists(n - 2):
                    dve.wait_ge(stored[b], 16 * h)
                if what == "out":
                    dve.wait_ge(turned, n - (OUT0 - 1))
                    nc.vector.tensor_tensor(res[:, b, :], tok[:, b, :, :].rearrange("p t c -> p (t c)"), side[:, b, :], ALU.add).then_inc(res_made, 1)
                    return
                dve.wait_ge(multiplied, n + 1)
                if what == "attn":
                    nc.vector.tensor_tensor(res[:, b, :], acc[:, b, :], side[:, b, :], ALU.mult).then_inc(res_made, 1)
                    return
                nc.vector.tensor_tensor(res[:, b, :], acc[:, b, :], side[:, b, :], ALU.mult).then_inc(gated, 1)
                seen = NJ * (1 + PASSES[p][0])
                dve.wait_ge(gated, n - (seen - 1))
                dve.wait_ge(prev_loaded[b], 16 * (h - (seen // 2 - 1)))
                nc.vector.tensor_tensor(res[:, b, :], res[:, b, :], prev[:, b, :], ALU.add).then_inc(res_made, 1)

            for b in range(2):
                low_a(b, b, 0, 0, b)
            with dve.Fori(1, KT // 2) as i:
                for b in range(2):
                    low_a(2 * i + b, b, i, 0, 2 * i + b)
            low_w(0, 0)
            tiles(dve, step)
            dve.wait_ge(res_made, LAST + 1)


def columns(v, copies=1):
    v = np.asarray(v).reshape(-1)
    v = np.concatenate([v] * copies)
    return np.ascontiguousarray(v.reshape(-1, P).T)


def weight_tiles(w):
    rows, cols = w.shape
    return np.ascontiguousarray(w.reshape(rows // P, P, cols // P, P).transpose(2, 1, 0, 3))


def layouts(i):
    w_in = i["w_in"][0]
    o = {"x": i["x"], "w_ada": i["w_ada"], "rel_bias": i["rel_bias"], "onehot": bucket_onehot(),
         "c": columns(i["c"]), "b_ada": columns(i["b_ada"]), "norm_w": columns(i["norm_w"]), "conv_b": columns(i["conv_b"]),
         "ssm_norm_w": columns(i["ssm_norm_w"]), "q_norm_w": columns(i["q_norm_w"], P // HD), "k_norm_w": columns(i["k_norm_w"], P // HD),
         "dt_bias": i["dt_bias"].reshape(SH, 1), "sinks": i["sinks"].reshape(1, H), "a_log": i["a_log"].reshape(1, SH),
         "d_skip": columns(np.repeat(i["d_skip"].reshape(-1), HD)),
         "conv_w": np.ascontiguousarray(i["conv_w"][0].reshape(CW, XBC // P, P).transpose(2, 0, 1)),
         "w_attn_proj": weight_tiles(i["w_attn_proj"][0]), "w_out": weight_tiles(i["w_out"][0]),
         "w_ssm_proj_0": weight_tiles(i["w_ssm_proj"][0, 0:D]), "w_ssm_proj_1": weight_tiles(i["w_ssm_proj"][0, D:2 * D])}
    for _, col, count, name in KINDS:
        o["w_in_" + name] = weight_tiles(w_in[:, col:col + count * P])
    return {n: np.ascontiguousarray(v) for n, v in o.items()}


def kernel(**inputs):
    import concourse.bacc as bacc
    from concourse.bass_utils import run_bass_kernel_spmd

    nc = bacc.Bacc("TRN2", target_bir_lowering=False, num_devices=1)
    arrays, aps = {}, {}
    for name, v in layouts({n: np.asarray(v) for n, v in inputs.items()}).items():
        arrays["in_" + name] = v
        aps[name] = nc.dram_tensor("in_" + name, v.shape, mybir.dt.from_np(v.dtype), kind="ExternalInput").ap()
    out = nc.dram_tensor("out", (1, S, D), F32, kind="ExternalOutput").ap()
    build(nc, aps, out)
    r = run_bass_kernel_spmd(nc, [arrays], core_ids=[0])
    return r.results[0]["out"]
```

```python
import math
from contextlib import ExitStack

import numpy as np
import concourse.bass as bass
from concourse import mybir

F32, F32R, U32 = mybir.dt.float32, mybir.dt.float32r, mybir.dt.uint32
ALU, ACT, AX = mybir.AluOpType, mybir.ActivationFunctionType, mybir.AxisListType.X

P = 128
D = 1024
S = 2048
KT = D // P
H, KV, HD = 16, 4, 64
GRP = H // KV
SW, SH, SG, SN = 2048, 32, 4, 128
R = SH // SG
CW = 4
NBLK = S // P
EPS = 1e-6
NEG = -1e30
BUCKETS, MAXDIST = 32, 128
MM = 512

C_Q = 0
C_K = C_Q + H * HD
C_V = C_K + KV * HD
C_ZA = C_V + KV * HD
C_ZM = C_ZA + H * HD
C_XBC = C_ZM + SW
XBC = SW + 2 * SG * SN
C_DT = C_XBC + XBC
C_G = C_DT + SH

KINDS = [("plain", C_DT, 1, "dt"), ("plain", C_V, 2, "v"), ("norm", C_K, 2, "k"), ("norm", C_Q, 8, "q"),
         ("silu", C_ZA, 8, "za"), ("silu", C_ZM, 16, "zm"), ("conv", C_XBC, 24, "xbc"), ("gate", C_G, 16, "g")]
NTILES = sum(k[2] for k in KINDS)


def bucket_onehot():
    n = (127 - np.arange(2 * P)) % P
    exact = BUCKETS // 2
    nf = np.maximum(n, 1).astype(np.float32)
    large = exact + (np.log(nf / np.float32(exact)) / np.float32(math.log(MAXDIST / exact))
                     * np.float32(BUCKETS - exact)).astype(np.int32)
    b = np.where(n < exact, n, np.minimum(large, BUCKETS - 1))
    return (b[None, :] == np.arange(BUCKETS)[:, None]).astype(np.float32)


def exists(n):
    return not isinstance(n, int) or n >= 0


def pairs(eng, count, body):
    for b in range(2):
        body(b, b, 0)
    with eng.Fori(1, count // 2) as i:
        for b in range(2):
            body(2 * i + b, b, i)


def dram_ap(t, offset, ap):
    return bass.AP(tensor=t.tensor, offset=offset, ap=ap)


def build(nc, a, out):
    scratch = {n: nc.dram_tensor("scr_" + n, (c * P, S), F32, kind="Internal").ap()
               for _, _, c, n in KINDS}
    scratch["attn"] = nc.dram_tensor("scr_attn", (D, S), F32, kind="Internal").ap()
    scratch["y"] = nc.dram_tensor("scr_y", (SW, S), F32, kind="Internal").ap()
    scratch["m"] = nc.dram_tensor("scr_m", (D, S), F32, kind="Internal").ap()
    scratch["rs"] = nc.dram_tensor("scr_rs", (SW // P, S), F32, kind="Internal").ap()
    scratch["rowcum"] = nc.dram_tensor("scr_rowcum", (NBLK * SH, P), F32, kind="Internal").ap()
    scratch["bias"] = nc.dram_tensor("scr_bias", (H, 2 * P), F32, kind="Internal").ap()
    with ExitStack() as ctx:
        def sb(n, s, d=F32):
            return ctx.enter_context(nc.sbuf_tensor(n, s, d))
        k = dict(
            ident=sb("ident", [P, P]), ones=sb("ones", [P, P]), headones=sb("headones", [P, P]),
            triu=sb("triu", [P, P]), tril=sb("tril", [P, P]), neg=sb("neg", [P, P]),
            negcur=sb("negcur", [P, P]),
            bias=sb("bias", [P, H, P]), sink=sb("sink", [P, H]),
            hscale=sb("hscale", [P, KT]), hshift=sb("hshift", [P, KT]), gate=sb("gate", [P, KT]),
            qw=sb("qw", [P, 1]), kw=sb("kw", [P, 1]), convw=sb("convw", [P, CW, XBC // P]),
            convb=sb("convb", [P, XBC // P]), dskip=sb("dskip", [P, SW // P]), ssmw=sb("ssmw", [P, SW // P]),
            dtb=sb("dtb", [SH, 1]), aneg=sb("aneg", [P, SH]), eps=sb("eps", [P, 1]),
        )
        setup(nc, a, scratch, k)
        with ExitStack() as hctx:
            h = [hctx.enter_context(nc.sbuf_tensor(n, [P, KT, S], F32R)) for n in ("h_hi", "h_lo")]
            normalise(nc, a, k, h)
            project(nc, a, scratch, k, h)
        with ExitStack() as dctx:
            dec = {n: dctx.enter_context(nc.sbuf_tensor("dec_" + n, [P, NBLK * SH], F32))
                   for n in ("dt", "cum", "toend", "chunk")}
            decays(nc, scratch, k, dec)
            mixers(nc, scratch, k, dec)
        merge(nc, a, scratch, k, out)


class Stage:

    def __init__(self, nc, name):
        self.nc, self.name, self.ctx = nc, name, ExitStack()

    def __enter__(self):
        return self

    def __exit__(self, *e):
        return self.ctx.__exit__(*e)

    def sb(self, n, s, d=F32):
        return self.ctx.enter_context(self.nc.sbuf_tensor(f"{self.name}_{n}", s, d))

    def ps(self, n, s):
        return self.ctx.enter_context(self.nc.psum_tensor(f"{self.name}_psum_{n}", s, F32))

    def sem(self, n):
        return self.ctx.enter_context(self.nc.semaphore(f"{self.name}_{n}"))

    def block(self):
        return self.ctx.enter_context(self.nc.Block())


def setup(nc, a, scratch, k):
    with Stage(nc, "setup") as st:
        W3 = 3 * D
        wada = st.sb("wada", [P, 2, W3])
        acc = st.sb("acc", [P, W3])
        ccol = st.sb("ccol", [P, KT]); chalf = st.sb("chalf", [P, KT]); ctan = st.sb("ctan", [P, KT])
        bada = st.sb("bada", [P, 3 * KT]); mod = st.sb("mod", [P, 3 * KT]); nw = st.sb("nw", [P, KT])
        onehot = st.sb("onehot", [BUCKETS, 2 * P]); rel = st.sb("rel", [BUCKETS, H]); brow = st.sb("brow", [H, 2 * P])
        al = st.sb("al", [P, SH]); cw = st.sb("cw", [P, CW, XBC // P]); cb = st.sb("cb", [P, XBC // P])
        qk = st.sb("qk", [P, 2]); flip = st.sb("flip", [P, P]); skew = st.sb("skew", [P, H, P])
        pm = st.ps("mod", [P, 512]); pb = st.ps("bias", [H, 2 * P]); pf = st.ps("flipped", [P, H, P])
        small, onesem, wsem = st.sem("small_loaded"), st.sem("bias_in_loaded"), [st.sem("wada0_loaded"), st.sem("wada1_loaded")]
        consts = st.sem("consts_made")
        ctanh, silu, accd, modp, brp, brs, bst, bld, fin, al_e, chd, modd = [st.sem(n) for n in (
            "c_tanh", "c_silu", "ada_accumulated", "mod_product", "bias_rows_product", "bias_rows_copied",
            "bias_rows_stored", "skew_loaded", "columns_made", "a_exponential", "c_halved", "mod_made")]
        flipped, bias_made = st.sem("bias_flipped"), st.sem("bias_made")
        half = P // 2
        blk = st.block()
        NSMALL, CONSTS = 11, 17

        @blk.sync
        def _(sp):
            sp.dma_start(ccol[:, :], a["c"]).then_inc(small, 16)
            for j in range(KT):
                if j >= 2:
                    sp.wait_ge(accd, j - 1)
                sp.dma_start(wada[:, j % 2, :], a["w_ada"][0, j * P:(j + 1) * P, :]).then_inc(wsem[j % 2], 16)

        @blk.scalar
        def _(act):
            act.dma_start(onehot[:, :], a["onehot"]).then_inc(onesem, 16)
            act.dma_start(rel[:, :], a["rel_bias"]).then_inc(onesem, 16)
            n = 0
            for dst, src in (
                (bada[:, :], a["b_ada"]),
                (nw[:, :], a["norm_w"]),
                (cb[:, :], a["conv_b"]),
                (k["ssmw"][:, :], a["ssm_norm_w"]),
                (qk[:, 0:1], a["q_norm_w"]),
                (qk[:, 1:2], a["k_norm_w"]),
                (k["dtb"][:, :], a["dt_bias"]),
                (k["sink"][:, :], a["sinks"].to_broadcast([P, H])),
                (al[:, :], a["a_log"].to_broadcast([P, SH])),
                (k["dskip"][:, :], a["d_skip"]),
                (cw[:, :, :], a["conv_w"]),
            ):
                act.dma_start(dst, src).then_inc(small, 16)
                n += 1
            assert n == NSMALL
            act.wait_ge(chd, 1)
            nc.scalar.activation(ctan[:, :], chalf[:, :], ACT.Tanh).then_inc(ctanh, 1)
            nc.scalar.activation(al[:, :], al[:, :], ACT.Exp).then_inc(al_e, 1)
            act.wait_ge(brs, 1)
            act.dma_start(scratch["bias"], brow[:, :]).then_inc(bst, 16)
            act.wait_ge(bst, 16)
            act.dma_start(skew[:, :, :], dram_ap(scratch["bias"], 0, [[1, P], [2 * P, H], [1, P]])).then_inc(bld, 16)
            act.wait_ge(flipped, 1)
            nc.scalar.activation(k["bias"][:, :, :], pf[:, :, :], ACT.Copy).then_inc(bias_made, 1)
            act.wait_ge(bias_made, 1)

        @blk.gpsimd
        def _(pool):
            made = [0]

            def const(ins):
                made[0] += 1
                ins.then_inc(consts, 1)
                pool.wait_ge(consts, made[0])

            def select(t, keep, coefficients, fill):
                base, part, col = coefficients
                const(nc.gpsimd.affine_select(out=t[:, :], in_=t[:, :], compare_op=keep, fill=fill, base=base,
                                              pattern=[[col, P]], channel_multiplier=part))

            const(pool.memset(k["eps"][:, :], EPS))
            const(pool.memset(flip[:, :], 0.0))
            select(flip, ALU.not_equal, (1 - P, 1, 1), 1.0)
            const(pool.memset(k["ones"][:, :], 1.0))
            const(pool.memset(k["ident"][:, :], 0.0))
            select(k["ident"], ALU.not_equal, (0, 1, -1), 1.0)
            const(pool.memset(k["triu"][:, :], 1.0))
            select(k["triu"], ALU.is_ge, (0, -1, 1), 0.0)
            const(pool.memset(k["tril"][:, :], 1.0))
            select(k["tril"], ALU.is_gt, (0, 1, -1), 0.0)
            const(pool.memset(k["neg"][:, :], 0.0))
            select(k["neg"], ALU.is_ge, (0, 1, -1), NEG)
            const(pool.memset(k["negcur"][:, :], NEG))
            select(k["negcur"], ALU.is_ge, (0, 1, -1), 0.0)
            const(pool.memset(k["headones"][:, :], 0.0))
            for hh in range(P // HD):
                const(pool.memset(k["headones"][hh * HD:(hh + 1) * HD, hh * HD:(hh + 1) * HD], 1.0))
            assert made[0] == CONSTS

        @blk.tensor
        def _(pe):
            pe.wait_ge(onesem, 32)
            nc.tensor.matmul(pb[:, :], rel[:, :], onehot[:, :], start=True, stop=True).then_inc(brp, 1)
            pe.wait_ge(bld, 16)
            pe.wait_ge(consts, CONSTS)
            for g in range(H * P // MM):
                hs = slice(g * MM // P, (g + 1) * MM // P)
                last = nc.tensor.matmul(pf[:, hs, :], flip[:, :], skew[:, hs, :], start=True, stop=True)
            last.then_inc(flipped, 1)
            pe.wait_ge(accd, KT)
            for m in range(3 * KT):
                last = nc.tensor.matmul(pm[:, m:m + 1], acc[:, m * P:(m + 1) * P], k["ones"][:, 0:1], start=True, stop=True)
            last.then_inc(modp, 1)

        @blk.vector
        def _(dve):
            dve.wait_ge(small, 16 * (NSMALL + 1))
            nc.vector.tensor_scalar(chalf[:, :], ccol[:, :], 0.5, None, ALU.mult).then_inc(chd, 1)
            dve.wait_ge(ctanh, 1)
            nc.vector.scalar_tensor_tensor(chalf[:, :], ctan[:, :], 1.0, chalf[:, :], ALU.add, ALU.mult).then_inc(silu, 1)
            dve.wait_ge(brp, 1)
            nc.vector.tensor_copy(brow[:, :], pb[:, :]).then_inc(brs, 1)
            dve.wait_ge(silu, 1)
            for j in range(KT):
                dve.wait_ge(wsem[j % 2], 16 * (j // 2 + 1))
                if j == 0:
                    nc.vector.tensor_scalar(acc[:, :], wada[:, 0, :], chalf[:, 0:1], None, ALU.mult).then_inc(accd, 1)
                else:
                    dve.wait_ge(accd, j)
                    nc.vector.scalar_tensor_tensor(acc[:, :], wada[:, j % 2, :], chalf[:, j:j + 1], acc[:, :],
                                                   ALU.mult, ALU.add).then_inc(accd, 1)
            nc.vector.tensor_scalar(k["convw"][:, :, :], cw[:, :, :], 0.5, None, ALU.mult)
            nc.vector.tensor_scalar(k["convb"][:, :], cb[:, :], 0.5, None, ALU.mult)
            nc.vector.tensor_scalar(k["qw"][:, :], qk[:, 0:1], HD ** -0.5, None, ALU.mult)
            nc.vector.tensor_copy(k["kw"][:, :], qk[:, 1:2])
            dve.wait_ge(al_e, 1)
            nc.vector.tensor_scalar(k["aneg"][:, :], al[:, :], -1.0, None, ALU.mult)
            dve.wait_ge(modp, 1)
            nc.vector.tensor_tensor(mod[:, :], pm[:, 0:3 * KT], bada[:, :], ALU.add).then_inc(modd, 1)
            dve.wait_ge(modd, 1)
            nc.vector.tensor_copy(k["hshift"][:, :], mod[:, 0:KT])
            nc.vector.scalar_tensor_tensor(k["hscale"][:, :], mod[:, KT:2 * KT], 1.0, nw[:, :], ALU.add, ALU.mult)
            nc.vector.tensor_scalar(k["gate"][:, :], mod[:, 2 * KT:3 * KT], 0.5, None, ALU.mult).then_inc(fin, 1)
            dve.wait_ge(fin, 1)


def ends(eng, count, body):
    for b in range(2):
        body(b, b, 0, True)
    with eng.Fori(1, count // 2 - 1) as i:
        for b in range(2):
            body(2 * i + b, b, i, True)
    for b in range(2):
        body(count - 2 + b, b, count // 2 - 1, b == 0)


def normalise(nc, a, k, h):
    h_hi, h_lo = h
    with Stage(nc, "norm") as st:
        x = st.sb("x", [P, 2, D]); xn = st.sb("xn", [P, 2, D]); h32 = st.sb("h32", [P, 2, D])
        ss = st.sb("ss", [P, 2]); root = st.sb("root", [P, 2]); rstd = st.sb("rstd", [P, 2])
        tp = st.ps("tp", [P, 2, D])
        x_loaded = [st.sem("x0_loaded"), st.sem("x1_loaded")]
        squares, rooted, rstd_made, x_normed, transposed, scaled, h_made, hi_made, lo_made = [st.sem(n) for n in (
            "squares", "rooted", "rstd_made", "x_normed", "transposed", "scaled", "h_made", "hi_made", "lo_made")]
        blk = st.block()

        @blk.sync
        def _(sp):
            def load(t, b, j):
                if exists(t - 2):
                    sp.wait_ge(x_normed, t - 1)
                sp.dma_start(x[:, b, :], a["x"][0, bass.ds(t * P, P), :]).then_inc(x_loaded[b], 16)
            pairs(sp, NBLK, load)

        @blk.scalar
        def _(act):
            def norm(t, b, j):
                act.wait_ge(x_loaded[b], 16 * j + 16)
                if exists(t - 2):
                    act.wait_ge(transposed, t - 1)
                nc.scalar.activation(xn[:, b, :], x[:, b, :], ACT.Square, accum_out=ss[:, b:b + 1]).then_inc(squares, 1)
                act.wait_ge(squares, t + 1)
                nc.scalar.activation(root[:, b:b + 1], ss[:, b:b + 1], ACT.Sqrt, bias=k["eps"][:, :], scale=1.0 / D).then_inc(rooted, 1)
                act.wait_ge(rstd_made, t + 1)
                nc.scalar.activation(xn[:, b, :], x[:, b, :], ACT.Copy, scale=rstd[:, b:b + 1]).then_inc(x_normed, 1)

            def step(t, b, j, more):
                if more:
                    norm(t + 1, 1 - b, j + b)
                act.wait_ge(h_made, t + 1)
                nc.scalar.activation(h_hi[:, :, bass.ds(t * P, P)],
                                     h32[:, b, :].rearrange("p (k t) -> p k t", k=KT), ACT.Copy).then_inc(hi_made, 1)

            norm(0, 0, 0)
            ends(act, NBLK, step)

        @blk.tensor
        def _(pe):
            def turn(t, b, j):
                pe.wait_ge(x_normed, t + 1)
                if exists(t - 2):
                    pe.wait_ge(scaled, t - 1)
                for kk in range(KT):
                    last = nc.tensor.transpose(tp[:, b, kk * P:(kk + 1) * P], xn[:, b, kk * P:(kk + 1) * P], k["ident"][:, :])
                last.then_inc(transposed, 1)
            pairs(pe, NBLK, turn)

        @blk.vector
        def _(dve):
            def invert(t, b):
                dve.wait_ge(rooted, t + 1)
                nc.vector.reciprocal(rstd[:, b:b + 1], root[:, b:b + 1]).then_inc(rstd_made, 1)

            def low(t, b):
                dve.wait_ge(hi_made, t + 1)
                nc.vector.tensor_tensor(h_lo[:, :, bass.ds(t * P, P)], h32[:, b, :].rearrange("p (k t) -> p k t", k=KT),
                                        h_hi[:, :, bass.ds(t * P, P)], ALU.subtract).then_inc(lo_made, 1)

            def step(t, b, j, more):
                if more:
                    invert(t + 1, 1 - b)
                dve.wait_ge(transposed, t + 1)
                hv = h32[:, b, :].rearrange("p (k t) -> p k t", k=KT)
                if exists(t - 2):
                    dve.wait_ge(lo_made, t - 1)
                nc.vector.tensor_tensor(hv, tp[:, b, :].rearrange("p (k t) -> p k t", k=KT),
                                        k["hscale"][:, :, None].to_broadcast([P, KT, P]), ALU.mult).then_inc(scaled, 1)
                dve.wait_ge(scaled, t + 1)
                nc.vector.tensor_tensor(hv, hv, k["hshift"][:, :, None].to_broadcast([P, KT, P]), ALU.add).then_inc(h_made, 1)
                if exists(t - 1):
                    low(t - 1, 1 - b)

            invert(0, 0)
            ends(dve, NBLK, step)
            low(NBLK - 1, 1)
            dve.wait_ge(lo_made, NBLK)


def project(nc, a, scratch, k, h):
    h_hi, h_lo = h
    with Stage(nc, "proj") as st:
        raw = st.sb("raw", [P, 2, KT, P])
        w_hi = [st.sb(f"w_hi{b}", [P, KT, P], F32R) for b in range(2)]
        w_lo = [st.sb(f"w_lo{b}", [P, KT, P], F32R) for b in range(2)]
        xin = st.sb("xin", [P, CW - 1 + S]); u = st.sb("u", [P, S]); res = st.sb("res", [P, 2, S])
        acc = st.ps("acc", [P, 2, S])
        w_loaded = [st.sem("w0_loaded"), st.sem("w1_loaded")]
        stored = [st.sem("res0_stored"), st.sem("res1_stored")]
        hi_made, lo_made, multiplied, squared, summed, res_begun, tapped, u_made, logged, res_made, padded = [
            st.sem(n) for n in ("hi_made", "lo_made", "multiplied", "squared", "summed", "res_begun",
                                "tapped", "u_made", "logged", "res_made", "padded")]
        blk = st.block()

        NORM0 = sum(c for kind, _, c, _ in KINDS[:[x[0] for x in KINDS].index("norm")])
        NORM_END = NORM0 + sum(c for kind, _, c, _ in KINDS if kind == "norm")

        def tiles(eng, body):
            n0 = 0
            for kind, col, count, name in KINDS:
                last = n0 + count == NTILES
                begin = count if kind == "plain" or n0 == NORM0 else 2 if n0 == NORM_END else 0
                end = count - 2 if last else count
                for e in range(begin):
                    body(n0 + e, (n0 + e) % 2, (n0 + e) // 2, kind, col, name, e)
                if begin < end:
                    with eng.Fori(begin // 2, end // 2) as i:
                        for e in range(2):
                            body(2 * i + (n0 + e), (n0 + e) % 2, i + (n0 + e) // 2, kind, col, name, 2 * i + e)
                    for e in range(end, count):
                        body(n0 + e, (n0 + e) % 2, (n0 + e) // 2, kind, col, name, e)
                n0 += count

        def norm_before(n, kind):
            return NORM0 < n <= NORM_END if isinstance(n, int) else kind == "norm"

        before = {}
        for kind, _, count, name in KINDS:
            before[name] = sum(c for kk, _, c, nm in KINDS[:[x[3] for x in KINDS].index(name)] if kk == kind)

        @blk.sync
        def _(sp):
            def load(n, b, j, kind, col, name, e):
                if exists(n - 2):
                    sp.wait_ge(lo_made, n - 1)
                sp.dma_start(raw[:, b, :, :], a["w_in_" + name][bass.ds(e, 1)].rearrange("o p k c -> (o p) k c")).then_inc(w_loaded[b], 16)
            tiles(sp, load)

        @blk.tensor
        def _(pe):
            def sums(n, b):
                pe.wait_ge(squared, n - NORM0)
                for c in range(S // MM):
                    last = nc.tensor.matmul(acc[:, b, c * MM:(c + 1) * MM], k["headones"][:, :], u[:, c * MM:(c + 1) * MM],
                                            start=True, stop=True)
                last.then_inc(summed, 1)

            def product(n, b, j, kind, col, name, e):
                pe.wait_ge(lo_made, n + 1)
                if exists(n - 2):
                    pe.wait_ge(u_made, n - 1)
                for kk in range(KT):
                    if kk == 2 and norm_before(n, kind):
                        sums(n, 1 - b)
                    for step, (wv, hv) in enumerate(((w_hi[b], h_hi), (w_hi[b], h_lo), (w_lo[b], h_hi))):
                        for c in range(S // MM):
                            last = nc.tensor.matmul(acc[:, b, c * MM:(c + 1) * MM], wv[:, kk, :], hv[:, kk, c * MM:(c + 1) * MM],
                                                    start=(kk == 0 and step == 0), stop=(kk == KT - 1 and step == 2))
                last.then_inc(multiplied, 1)

            tiles(pe, product)

        @blk.scalar
        def _(act):
            def high(b, j):
                act.wait_ge(w_loaded[b], 16 * j + 16)
                nc.scalar.activation(w_hi[b][:, :, :], raw[:, b, :, :], ACT.Copy).then_inc(hi_made, 1)

            def finish(n, b, j, kind, col, name, e):
                if not (isinstance(n, int) and n == NTILES - 1):
                    high(1 - b, j + b)
                if exists(n - 2):
                    act.wait_ge(stored[b], 16 * j)
                act.wait_ge(multiplied, n + 1)
                src = acc[:, b, :]
                if kind == "plain":
                    nc.scalar.activation(u[:, :], src, ACT.Copy).then_inc(u_made, 1)
                elif kind == "gate":
                    nc.scalar.activation(u[:, :], src, ACT.Tanh, scale=0.5).then_inc(u_made, 1)
                elif kind == "silu":
                    nc.scalar.activation(res[:, b, :], src, ACT.Copy, scale=0.5).then_inc(res_begun, 1)
                    nc.scalar.activation(u[:, :], src, ACT.Tanh, scale=0.5).then_inc(u_made, 1)
                elif kind == "conv":
                    nc.scalar.activation(xin[:, CW - 1:], src, ACT.Copy)
                    nc.scalar.activation(res[:, b, :], src, ACT.Identity, bias=k["convb"][:, bass.ds(e, 1)],
                                         scale=k["convw"][:, CW - 1, bass.ds(e, 1)]).then_inc(res_begun, 1)
                    act.wait_ge(tapped, 3 * e + 3)
                    nc.scalar.activation(u[:, :], res[:, b, :], ACT.Tanh).then_inc(u_made, 1)
                elif kind == "norm":
                    nc.scalar.activation(res[:, b, :], src, ACT.Copy).then_inc(res_begun, 1)
                    nc.scalar.activation(u[:, :], src, ACT.Square).then_inc(squared, 1)
                    act.wait_ge(summed, e + (before[name] + 1))
                    nc.scalar.activation(u[:, :], src, ACT.Ln, bias=k["eps"][:, :], scale=1.0 / HD).then_inc(logged, 1)
                    act.wait_ge(logged, e + (before[name] + 1))
                    nc.scalar.activation(u[:, :], u[:, :], ACT.Exp, scale=-0.5).then_inc(u_made, 1)
                act.wait_ge(res_made, n + 1)
                act.dma_start(scratch[name][bass.ds(e * P, P), :], res[:, b, :]).then_inc(stored[b], 16)

            high(0, 0)
            tiles(act, finish)
            for b in range(2):
                act.wait_ge(stored[b], 16 * ((NTILES + 1 - b) // 2))

        @blk.vector
        def _(dve):
            def low(n, b):
                dve.wait_ge(hi_made, n + 1)
                if exists(n - 2):
                    dve.wait_ge(multiplied, n - 1)
                nc.vector.tensor_tensor(w_lo[b][:, :, :], raw[:, b, :, :], w_hi[b][:, :, :], ALU.subtract).then_inc(lo_made, 1)

            def finish(n, b, j, kind, col, name, e):
                if not (isinstance(n, int) and n == NTILES - 1):
                    low(n + 1, 1 - b)
                if kind == "conv":
                    for c in range(CW - 1):
                        if c == 0:
                            dve.wait_ge(res_begun, e + 1 + BEGUN[name])
                        else:
                            dve.wait_ge(tapped, 3 * e + c)
                        nc.vector.scalar_tensor_tensor(res[:, b, :], xin[:, c:c + S], k["convw"][:, c, bass.ds(e, 1)],
                                                       res[:, b, :], ALU.mult, ALU.add).then_inc(tapped, 1)
                dve.wait_ge(u_made, n + 1)
                if kind == "plain":
                    nc.vector.tensor_copy(res[:, b, :], u[:, :]).then_inc(res_made, 1)
                elif kind == "gate":
                    nc.vector.tensor_scalar(res[:, b, :], u[:, :], 1.0, None, ALU.add).then_inc(res_made, 1)
                elif kind in ("silu", "conv"):
                    nc.vector.scalar_tensor_tensor(res[:, b, :], u[:, :], 1.0, res[:, b, :], ALU.add, ALU.mult).then_inc(res_made, 1)
                elif kind == "norm":
                    nc.vector.scalar_tensor_tensor(res[:, b, :], res[:, b, :], k[name + "w"][:, :], u[:, :],
                                                   ALU.mult, ALU.mult).then_inc(res_made, 1)

            order = [x for x in KINDS if x[0] in ("norm", "silu", "conv")]
            BEGUN = {x[3]: sum(y[2] for y in order[:i]) for i, x in enumerate(order)}
            dve.memset(xin[:, 0:CW - 1], 0.0).then_inc(padded, 1)
            dve.wait_ge(padded, 1)
            low(0, 0)
            tiles(dve, finish)
            dve.wait_ge(res_made, NTILES)


def decays(nc, scratch, k, dec):
    NCH = NBLK * SH
    TERMS = 8
    with Stage(nc, "decay") as st:
        dtt = st.sb("dtt", [SH, S]); x = st.sb("x", [P, NCH]); u = st.sb("u", [P, NCH]); v = st.sb("v", [P, NCH])
        w = st.sb("w", [P, NCH]); rows = st.sb("rows", [P, 4, P]); dta = st.sb("dta", [P, NCH])
        pt = st.ps("pt", [P, NCH]); pc = st.ps("pc", [P, NCH]); pe_ = st.ps("pe", [P, NCH]); pr = st.ps("pr", [P, 4, P])
        loaded, biased, turned, cumulated, v1, a1, stored, done = [st.sem(n) for n in (
            "loaded", "biased", "turned", "cumulated", "vector_step", "scalar_step", "rows_stored", "done")]
        blk = st.block()

        @blk.sync
        def _(sp):
            sp.dma_start(dtt[:, :], scratch["dt"][0:SH, :]).then_inc(loaded, 16)
            sp.wait_ge(done, 1)
            sp.dma_start(scratch["rowcum"].rearrange("(m p) l -> p m l", p=P), rows[:, :, :]).then_inc(stored, 16)
            sp.wait_ge(stored, 16)

        @blk.tensor
        def _(pe):
            pe.wait_ge(biased, 1)
            for c in range(NBLK):
                last = nc.tensor.transpose(pt[:, c * SH:(c + 1) * SH], dtt[:, c * P:(c + 1) * P], k["ident"][0:SH, 0:SH])
            last.then_inc(turned, 1)
            pe.wait_ge(cumulated, 1)
            nc.tensor.matmul(pc[:, :], k["triu"][:, :], dta[:, :], start=True, stop=True)
            nc.tensor.matmul(pe_[:, :], k["ones"][:, :], dta[:, :], start=True, stop=True)
            for m in range(4):
                last = nc.tensor.matmul(pr[:, m, :], dta[:, m * P:(m + 1) * P], k["triu"][:, :], start=True, stop=True)
            last.then_inc(turned, 1)

        @blk.scalar
        def _(act):
            act.wait_ge(v1, 2)
            nc.scalar.activation(u[:, :], u[:, :], ACT.Exp, scale=-1.0).then_inc(a1, 1)
            act.wait_ge(turned, 2)
            nc.scalar.activation(dec["chunk"][:, :], pe_[:, :], ACT.Exp).then_inc(a1, 1)
            act.wait_ge(v1, 3 + 4 + TERMS + 3)
            nc.scalar.activation(dec["toend"][:, :], w[:, :], ACT.Exp).then_inc(a1, 1)
            act.wait_ge(a1, 3)

        @blk.vector
        def _(dve):
            dve.wait_ge(loaded, 16)
            nc.vector.tensor_scalar(dtt[:, :], dtt[:, :], k["dtb"][:, :], None, ALU.add).then_inc(biased, 1)
            dve.wait_ge(turned, 1)
            step = [0]

            def chain(ins):
                step[0] += 1
                ins.then_inc(v1, 1)
                dve.wait_ge(v1, step[0])

            chain(nc.vector.tensor_copy(x[:, :], pt[:, :]))
            chain(nc.vector.scalar_tensor_tensor(u[:, :], x[:, :], -1.0, x[:, :], ALU.mult, ALU.max))
            dve.wait_ge(a1, 1)
            chain(nc.vector.tensor_scalar(v[:, :], u[:, :], 2.0, None, ALU.add))
            chain(nc.vector.reciprocal(v[:, :], v[:, :]))
            chain(nc.vector.tensor_tensor(u[:, :], u[:, :], v[:, :], ALU.mult))
            chain(nc.vector.tensor_tensor(v[:, :], u[:, :], u[:, :], ALU.mult))
            chain(nc.vector.tensor_scalar(w[:, :], v[:, :], 1.0 / (2 * TERMS + 1), None, ALU.mult))
            for n in range(TERMS - 1, 0, -1):
                chain(nc.vector.scalar_tensor_tensor(w[:, :], w[:, :], 1.0 / (2 * n + 1), v[:, :], ALU.add, ALU.mult))
            chain(nc.vector.scalar_tensor_tensor(w[:, :], w[:, :], 1.0, u[:, :], ALU.add, ALU.mult))
            chain(nc.vector.tensor_scalar(x[:, :], x[:, :], 0.0, None, ALU.max))
            chain(nc.vector.scalar_tensor_tensor(dec["dt"][:, :], w[:, :], 2.0, x[:, :], ALU.mult, ALU.add))
            assert step[0] == 3 + 4 + TERMS + 2
            nc.vector.tensor_tensor(dta[:, :].rearrange("p (c h) -> p c h", h=SH),
                                    dec["dt"][:, :].rearrange("p (c h) -> p c h", h=SH),
                                    k["aneg"][:, None, :].to_broadcast([P, NBLK, SH]), ALU.mult).then_inc(cumulated, 1)
            dve.wait_ge(turned, 2)
            nc.vector.tensor_copy(rows[:, :, :], pr[:, :, :]).then_inc(done, 1)
            nc.vector.tensor_copy(dec["cum"][:, :], pc[:, :]).then_inc(done, 1)
            dve.wait_ge(done, 2)
            dve.wait_ge(a1, 2)
            chain(nc.vector.tensor_tensor(w[:, :], pe_[:, :], dec["cum"][:, :], ALU.subtract))


def mixers(nc, scratch, k, dec):
    assert KV == SG
    G = SG
    XT = R * HD // P
    PAIRS = GRP // 2
    UNITS = 2 * G
    TURNS = NBLK // 2
    with Stage(nc, "mix") as st:
        q = st.sb("q", [P, 2, PAIRS, P]); za = st.sb("za", [P, 2, PAIRS, P]); vt = st.sb("vt", [HD, 2, P])
        bias_cur = st.sb("bias_cur", [P, H, P]); bias_prev = st.sb("bias_prev", [P, H, P])
        keys = [st.sb(f"keys{g}", [P, 2, P]) for g in range(G)]
        vals = [[st.sb(f"vals{g}_{s}", [P, HD]) for s in range(2)] for g in range(G)]
        sc = st.sb("sc", [P, 2, GRP, P]); sp_ = st.sb("sp", [P, GRP, P]); probs = st.sb("probs", [P, GRP, P])
        pcur = st.sb("pcur", [P, GRP, P]); pprev = st.sb("pprev", [P, GRP, P]); carrier = st.sb("carrier", [P, 1])
        mx = st.sb("mx", [P, 2, GRP]); nmx = st.sb("nmx", [P, 2, GRP]); es = st.sb("es", [P, 2, GRP])
        den = st.sb("den", [P, 2, GRP]); rden = st.sb("rden", [P, 2, GRP]); o = st.sb("o", [P, 2, PAIRS, P])
        score = st.ps("score", [P, 2, PAIRS, 2, P])
        p_pt = st.ps("pt", [P, GRP, P]); p_av = st.ps("av", [P, 4, P])
        bt = st.sb("bt", [P, 2, P]); ct = st.sb("ct", [P, 2, P]); xt = st.sb("xt", [P, 4, XT, P]); zt = st.sb("zt", [P, 2, XT, P])
        row = st.sb("row", [P, 2, R, P]); seg = st.sb("seg", [P, 2, R, P]); cx = st.sb("cx", [P, 2, R, P])
        cbm = st.sb("cbm", [P, 2, P]); btok = st.sb("btok", [P, 2, P]); xdt = st.sb("xdt", [P, 2, R, HD]); xend = st.sb("xend", [P, 2, R, HD])
        state = [st.sb(f"state{g}", [P, R, HD]) for g in range(G)]
        y = st.sb("y", [P, 2, XT, P]); ysq = st.sb("ysq", [P, XT, P]); ysum = st.sb("ysum", [P, P])
        logs = st.sb("logs", [P, NBLK * G]); rs = st.sb("rs", [P, NBLK * G]); rs_rows = st.sb("rs_rows", [NBLK * G, P])
        p_xt = st.ps("xt", [P, XT, P]); p_cb = st.ps("cb", [P, 4, P]); p_y = st.ps("y", [P, XT, P]); p_st = st.ps("st", [P, R, HD])
        a_loaded = [st.sem(f"attention_in{b}_loaded") for b in range(2)]
        s_loaded = [st.sem(f"scan_in{b}_loaded") for b in range(2)]
        o_stored = [st.sem(f"o{b}_stored") for b in range(2)]
        y_stored = [st.sem(f"y{b}_stored") for b in range(2)]
        za_loaded = [st.sem(f"attention_gate{b}_loaded") for b in range(2)]
        x_loaded = [st.sem(f"scan_values{b}_loaded") for b in range(2)]
        zm_loaded = [st.sem(f"scan_gate{b}_loaded") for b in range(2)]
        rs_stored = st.sem("rs_stored")
        A_LOADS, S_LOADS = 4 * 16, 3 * 16
        ready, scored, v_turned, v_made, cur_biased, prev_biased, chosen, maxed, sink_maxed, negated, sink_shifted, exp_made, sink_exp, \
            denominated, inverted, normalised, p_turned, p_copied, cur_made, prev_made, weighed, gated = [st.sem(n) for n in (
                "ready", "scored", "v_turned", "v_made", "cur_biased", "prev_biased", "chosen", "maxed", "sink_maxed", "negated",
                "sink_shifted", "exp_made", "sink_exp", "denominated", "inverted", "normalised", "p_turned", "p_copied", "cur_made",
                "prev_made", "weighed", "gated")]
        cb_made, x_turned, b_turned, b_copied, seg_made, masked, xdt_made, xend_made, row_exp, seg_exp, c_scaled, m_made, y_made, \
            states_made, decayed, state_new, skipped, z_gated, squared, halved, y_added, y_summed, logged, rstd_made, rs_turned, rs_copied = [st.sem(n) for n in (
                "cb_made", "x_turned", "b_turned", "b_copied", "seg_made", "masked", "xdt_made", "xend_made", "row_exp", "seg_exp",
                "c_scaled", "m_made", "y_made", "states_made", "decayed", "state_new", "skipped", "z_gated", "squared", "halved",
                "y_added", "y_summed", "logged", "rstd_made", "rs_turned", "rs_copied")]
        blk = st.block()
        p_sums = p_cb[:, 2, 0:NBLK * G].rearrange("p (s g i) -> p s g i", s=2, g=G)
        b_psum = p_st[:, 0:P // HD, :].rearrange("p r d -> p (r d)")
        v_psum = p_st[:, P // HD, :]

        def ahead(i, m, by):
            return i + (m + by) // UNITS, (m + by) % UNITS

        def steps(eng, step):
            for m in range(UNITS):
                step(0, m, UNITS)
            with eng.Fori(1, TURNS - 1) as i:
                for m in range(UNITS):
                    step(i, m, UNITS)
            for m in range(UNITS):
                step(TURNS - 1, m, UNITS - 1 - m)

        def heads(t):
            return t.rearrange("q (half pair) k -> q half pair k", half=2)

        def loads(b, i, m):
            return i * (UNITS // 2) + (m // 2 + 1)

        @blk.sync
        def _(sp):
            def load_first(i, m):
                g, b, s = m % G, m % 2, m // G
                t = bass.ds((i * 2 + s) * P, P)
                src = scratch["rowcum"][bass.ds((i * 2 + s) * SH + g * R, R), :].rearrange("(o h) l -> o h l", o=1)
                sp.dma_start(row[:, b, :, :], src.to_broadcast([P, R, P])).then_inc(s_loaded[b], 16)
                sp.dma_start(bt[:, b, :], scratch["xbc"][SW + g * SN:SW + (g + 1) * SN, t]).then_inc(s_loaded[b], 16)
                sp.dma_start(ct[:, b, :], scratch["xbc"][SW + (SG + g) * SN:SW + (SG + g + 1) * SN, t]).then_inc(s_loaded[b], 16)
                sp.dma_start(q[:, b, :, :], scratch["q"][g * GRP * HD:(g + 1) * GRP * HD, t].rearrange("(c p) t -> p c t", p=P)).then_inc(a_loaded[b], 16)
                sp.dma_start(keys[g][0:HD, s, :], scratch["k"][g * HD:(g + 1) * HD, t]).then_inc(a_loaded[b], 16)
                sp.dma_start(keys[g][HD:P, s, :], scratch["k"][g * HD:(g + 1) * HD, t]).then_inc(a_loaded[b], 16)
                sp.dma_start(vt[:, b, :], scratch["v"][g * HD:(g + 1) * HD, t]).then_inc(a_loaded[b], 16)

                sp.dma_start(xt[:, m % 4, :, :], scratch["xbc"][g * R * HD:(g + 1) * R * HD, t].rearrange("(c p) t -> p c t", p=P)).then_inc(x_loaded[b], 16)

            def load_scan_gate(i, m):
                g, b, s = m % G, m % 2, m // G
                sp.dma_start(zt[:, b, :, :], scratch["zm"][g * R * HD:(g + 1) * R * HD, bass.ds((i * 2 + s) * P, P)]
                             .rearrange("(c p) t -> p c t", p=P)).then_inc(zm_loaded[b], 16)

            def load_gate(i, m):
                g, b, s = m % G, m % 2, m // G
                sp.dma_start(za[:, b, :, :], scratch["za"][g * GRP * HD:(g + 1) * GRP * HD, bass.ds((i * 2 + s) * P, P)]
                             .rearrange("(c p) t -> p c t", p=P)).then_inc(za_loaded[b], 16)

            def step(i, m, left):
                n, g, b, s = i * UNITS + m, m % G, m % 2, m // G
                t = bass.ds((i * 2 + s) * P, P)
                if left >= 2:
                    sp.wait_ge(v_turned, n + 1)
                    sp.wait_ge(seg_exp, n + 1)
                    sp.wait_ge(c_scaled, n + 1)
                    load_first(*ahead(i, m, 2))
                sp.wait_ge(ready, 1)
                sp.wait_ge(gated, n + 1)
                sp.dma_start(scratch["attn"][g * GRP * HD:(g + 1) * GRP * HD, t].rearrange("(c p) t -> p c t", p=P), o[:, b, :, :]).then_inc(o_stored[b], 16)
                if left >= 2:
                    load_gate(*ahead(i, m, 2))
                sp.wait_ge(z_gated, n + 1)
                sp.dma_start(scratch["y"][g * R * HD:(g + 1) * R * HD, t].rearrange("(c p) t -> p c t", p=P), y[:, b, :, :]).then_inc(y_stored[b], 16)
                if left >= 2:
                    load_scan_gate(*ahead(i, m, 2))

            for m in range(2):
                load_first(0, m)
                load_gate(0, m)
                load_scan_gate(0, m)
            steps(sp, step)
            sp.wait_ge(rs_copied, 1)
            to = scratch["rs"].rearrange("(g c) (i s t) -> s g i c t", c=XT, s=2, t=P)
            for s in range(2):
                for g in range(G):
                    r0 = (s * G + g) * TURNS
                    sp.dma_start(to[s, g], rs_rows[r0:r0 + TURNS, None, :].to_broadcast([TURNS, XT, P])).then_inc(rs_stored, 16)
            sp.wait_ge(rs_stored, 16 * 2 * G)
            for b in range(2):
                sp.wait_ge(o_stored[b], 16 * NBLK * G // 2)
                sp.wait_ge(y_stored[b], 16 * NBLK * G // 2)

        @blk.tensor
        def _(pe):
            def scores(i, m):
                n, g, b, s = i * UNITS + m, m % G, m % 2, m // G
                pe.wait_ge(a_loaded[b], A_LOADS * loads(b, i, m))
                if exists(n - 1):
                    if exists(n - 1 - G):
                        pe.wait_ge(prev_biased, n - G)
                    else:
                        pe.wait_ge(cur_biased, n)
                both = exists(n - G)
                for h in range(GRP):
                    half, pair = h % 2, h // 2
                    r = slice(HD * half, HD * half + HD)
                    if both:
                        last = nc.tensor.matmul(score[:, half, pair, :, :], q[r, b, pair, :], keys[g][r, :, :], start=True, stop=True)
                    else:
                        last = nc.tensor.matmul(score[:, half, pair, s, :], q[r, b, pair, :], keys[g][r, s, :], start=True, stop=True)
                last.then_inc(scored, 1)

            def prepare(i, m):
                n, b = i * UNITS + m, m % 2
                pe.wait_ge(s_loaded[b], S_LOADS * loads(b, i, m))
                if exists(n - 1):
                    pe.wait_ge(masked, n)
                nc.tensor.matmul(p_cb[:, 0, :], bt[:, b, :], ct[:, b, :], start=True, stop=True).then_inc(cb_made, 1)
                if exists(n - 1):
                    pe.wait_ge(xdt_made, n)
                pe.wait_ge(x_loaded[b], 16 * loads(b, i, m))
                for c in range(XT):
                    last = nc.tensor.transpose(p_xt[:, c, :], xt[:, m % 4, c, :], k["ident"][:, :])
                last.then_inc(x_turned, 1)
                if exists(n - 2):
                    pe.wait_ge(state_new, n + (G - 1))
                elif exists(n - 1):
                    pe.wait_ge(b_copied, n)
                    pe.wait_ge(v_made, n)
                nc.tensor.transpose(b_psum, bt[:, b, :], k["ident"][:, :]).then_inc(b_turned, 1)
                nc.tensor.transpose(v_psum, vt[:, b, :], k["ident"][0:HD, 0:HD]).then_inc(v_turned, 1)

            def turn_p(i, m):
                n, b = i * UNITS + m, m % 2
                pe.wait_ge(normalised, n + 1)
                if exists(n - 1):
                    pe.wait_ge(p_copied, n)
                for h in range(GRP):
                    last = nc.tensor.transpose(p_pt[:, h, :], sc[:, b, h, :], k["ident"][:, :])
                last.then_inc(p_turned, 1)

            def outputs(i, m, more):
                n, g, b = i * UNITS + m, m % G, m % 2
                pe.wait_ge(xdt_made, n + 1)
                pe.wait_ge(m_made, n + 1)
                pe.wait_ge(c_scaled, n + 1)
                pe.wait_ge(state_new, n + 1)
                if exists(n - 1):
                    pe.wait_ge(skipped, n)
                for r in range(R):
                    to = p_y[HD * (r % 2):HD * (r % 2) + HD, r // 2, :]
                    nc.tensor.matmul(to, xdt[:, b, r, :], seg[:, b, r, :], start=True, stop=False)
                    last = nc.tensor.matmul(to, state[g][:, r, :], cx[:, b, r, :], start=False, stop=True)
                last.then_inc(y_made, 1)
                pe.wait_ge(b_copied, n + (2 if more else 1))
                pe.wait_ge(v_made, n + (2 if more else 1))
                pe.wait_ge(xend_made, n + 1)
                nc.tensor.matmul(p_st[:, :, :], btok[:, b, :], xend[:, b, :, :], start=True, stop=True).then_inc(states_made, 1)

            def weigh(i, m):
                n, g, s = i * UNITS + m, m % G, m // G
                both = exists(n - G)
                if exists(n - 1):
                    pe.wait_ge(gated, n)
                pe.wait_ge(cur_made, n + 1)
                if both:
                    pe.wait_ge(prev_made, n + 1 - G)
                for half in range(2):
                    to = p_av[HD * half:HD * half + HD, 0:PAIRS, :]
                    hs = slice(PAIRS * half, PAIRS * half + PAIRS)
                    last = nc.tensor.matmul(to, vals[g][s][:, :], pcur[:, hs, :], start=True, stop=not both)
                    if both:
                        last = nc.tensor.matmul(to, vals[g][1 - s][:, :], pprev[:, hs, :], start=False, stop=True)
                last.then_inc(weighed, 1)

            def norm(i, m, after):
                n = i * UNITS + m
                pe.wait_ge(y_added, n + 1)
                pe.wait_ge(masked, n + 1 + after)
                nc.tensor.matmul(p_sums[:, m // G, m % G, bass.ds(i, 1)], ysum[:, :], k["ones"][:, 0:1], start=True, stop=True).then_inc(y_summed, 1)

            def step(i, m, left):
                turn_p(i, m)
                outputs(i, m, left)
                weigh(i, m)
                if exists(i * UNITS + m - 1):
                    norm(*ahead(i, m, -1), 2 if left else 1)
                if left >= 2:
                    scores(*ahead(i, m, 2))
                    prepare(*ahead(i, m, 2))

            pe.wait_ge(ready, 1)
            for m in range(2):
                scores(0, m)
                prepare(0, m)
            steps(pe, step)
            norm(TURNS - 1, UNITS - 1, 0)
            pe.wait_ge(rstd_made, 1)
            nc.tensor.transpose(p_cb[0:NBLK * G, 0, :], rs[:, :], k["ident"][:, :]).then_inc(rs_turned, 1)

        @blk.scalar
        def _(act):
            def copies(i, m):
                n, g, b, s = i * UNITS + m, m % G, m % 2, m // G
                act.wait_ge(v_turned, n + 1)
                nc.scalar.activation(vals[g][s][:, :], v_psum, ACT.Copy).then_inc(v_made, 1)
                act.wait_ge(b_turned, n + 1)
                nc.scalar.activation(btok[:, b, :], b_psum, ACT.Copy).then_inc(b_copied, 1)

            def exponentials(i, m):
                n, g, b, s = i * UNITS + m, m % G, m % 2, m // G
                act.wait_ge(s_loaded[b], S_LOADS * loads(b, i, m))
                if exists(n - 2):
                    act.wait_ge(y_made, n - 1)
                nc.scalar.activation(cx[:, b, :, :], row[:, b, :, :], ACT.Exp).then_inc(row_exp, 1)
                for r in range(R):
                    last = nc.scalar.activation(seg[:, b, r, :], row[:, b, r, :], ACT.Relu, scale=-1.0, bias=dec["cum"][:, bass.ds((i * 2 + s) * SH + (g * R + r), 1)])
                last.then_inc(seg_made, 1)
                act.wait_ge(seg_made, n + 1)
                nc.scalar.activation(seg[:, b, :, :], seg[:, b, :, :], ACT.Exp, scale=-1.0).then_inc(seg_exp, 1)

            def probabilities(i, m):
                n, b = i * UNITS + m, m % 2
                act.wait_ge(negated, n + 1)
                for h in range(GRP):
                    last = nc.scalar.activation(sc[:, b, h, :], sc[:, b, h, :], ACT.Exp, bias=nmx[:, b, h:h + 1], accum_out=den[:, b, h:h + 1])
                last.then_inc(exp_made, 1)
                act.wait_ge(sink_shifted, n + 1)
                nc.scalar.activation(es[:, b, :], es[:, b, :], ACT.Exp).then_inc(sink_exp, 1)
                act.wait_ge(inverted, n + 1)
                act.wait_ge(exp_made, n + 1)
                for h in range(GRP):
                    last = nc.scalar.activation(sc[:, b, h, :], sc[:, b, h, :], ACT.Copy, scale=rden[:, b, h:h + 1])
                last.then_inc(normalised, 1)

            def step(i, m, left):
                n, b = i * UNITS + m, m % 2
                act.wait_ge(p_turned, n + 1)
                if exists(n - 1):
                    act.wait_ge(cur_made, n)
                nc.scalar.activation(probs[:, :, :], p_pt[:, :, :], ACT.Copy).then_inc(p_copied, 1)
                if left:
                    exponentials(*ahead(i, m, 1))
                    probabilities(*ahead(i, m, 1))
                if left >= 2:
                    copies(*ahead(i, m, 2))

            copies(0, 0)
            exponentials(0, 0)
            probabilities(0, 0)
            copies(0, 1)
            steps(act, step)
            act.wait_ge(y_summed, NBLK * G)
            act.wait_ge(masked, NBLK * G)
            nc.scalar.activation(logs[:, :], p_cb[:, 2, 0:NBLK * G], ACT.Ln, bias=k["eps"][:, :], scale=1.0 / (R * HD)).then_inc(logged, 1)
            act.wait_ge(logged, 1)
            nc.scalar.activation(rs[:, :], logs[:, :], ACT.Exp, scale=-0.5).then_inc(rstd_made, 1)
            act.wait_ge(rs_turned, 1)
            nc.scalar.activation(rs_rows[:, :], p_cb[0:NBLK * G, 0, :], ACT.Copy).then_inc(rs_copied, 1)

        @blk.gpsimd
        def _(pool):
            def end_inputs(i, m):
                n, g, b, s = i * UNITS + m, m % G, m % 2, m // G
                pool.wait_ge(ready, 1)
                pool.wait_ge(xdt_made, n + 1)
                if exists(n - 2):
                    pool.wait_ge(states_made, n - 1)
                nc.gpsimd.tensor_tensor(xend[:, b, :, :], xdt[:, b, :, :],
                                        dec["toend"][:, bass.ds((i * 2 + s) * SH + g * R, R)][:, :, None].to_broadcast([P, R, HD]),
                                        ALU.mult).then_inc(xend_made, 1)

            def masks(i, m):
                n = i * UNITS + m
                pool.wait_ge(ready, 1)
                pool.wait_ge(p_copied, n + 1)
                if exists(n - 1):
                    pool.wait_ge(weighed, n)
                if m == 0:
                    nc.gpsimd.tensor_tensor(carrier[:, :], k["ones"][:, 0:1], k["ones"][:, 0:1], ALU.add)
                if exists(n - G):
                    nc.gpsimd.affine_select(out=pprev[:, :, :], in_=probs[:, :, :], compare_op=ALU.is_gt, fill=0.0, base=0,
                                            pattern=[[0, GRP], [-1, P]], channel_multiplier=1).then_inc(prev_made, 1)
                nc.gpsimd.affine_select(out=pcur[:, :, :], in_=probs[:, :, :], compare_op=ALU.is_ge, fill=0.0, base=0,
                                        pattern=[[0, GRP], [1, P]], channel_multiplier=-1).then_inc(cur_made, 1)

            def sum_squares(i, m):
                n = i * UNITS + m
                pool.wait_ge(squared, n + 1)
                nc.gpsimd.tensor_tensor(ysq[:, 0:XT // 2, :], ysq[:, 0:XT // 2, :], ysq[:, XT // 2:XT, :], ALU.add).then_inc(halved, 1)
                pool.wait_ge(halved, n + 1)
                if exists(n - 1):
                    pool.wait_ge(y_summed, n)
                nc.gpsimd.tensor_tensor(ysum[:, :], ysq[:, 0, :], ysq[:, 1, :], ALU.add).then_inc(y_added, 1)

            def decay(i, m):
                n, g, s = i * UNITS + m, m % G, m // G
                pool.wait_ge(ready, 1)
                pool.wait_ge(y_made, n + 1)
                nc.gpsimd.tensor_tensor(state[g][:, :, :], state[g][:, :, :],
                                        dec["chunk"][:, bass.ds((i * 2 + s) * SH + g * R, R)][:, :, None].to_broadcast([P, R, HD]),
                                        ALU.mult).then_inc(decayed, 1)

            def gate_scan(i, m):
                n, b = i * UNITS + m, m % 2
                pool.wait_ge(zm_loaded[b], 16 * loads(b, i, m))
                pool.wait_ge(skipped, n + 1)
                nc.gpsimd.tensor_tensor(y[:, b, :, :], y[:, b, :, :], zt[:, b, :, :], ALU.mult).then_inc(z_gated, 1)
                pool.wait_ge(z_gated, n + 1)
                if exists(n - 1):
                    pool.wait_ge(y_added, n)
                nc.gpsimd.tensor_tensor(ysq[:, :, :], y[:, b, :, :], y[:, b, :, :], ALU.mult).then_inc(squared, 1)

            def step(i, m, left):
                masks(i, m)
                if exists(i * UNITS + m - 1):
                    sum_squares(*ahead(i, m, -1))
                if left:
                    end_inputs(*ahead(i, m, 1))
                decay(i, m)
                gate_scan(i, m)

            end_inputs(0, 0)
            steps(pool, step)
            sum_squares(TURNS - 1, UNITS - 1)
            pool.wait_ge(y_added, NBLK * G)

        @blk.vector
        def _(dve):
            def scan_inputs(i, m):
                n, g, b, s = i * UNITS + m, m % G, m % 2, m // G
                dve.wait_ge(cb_made, n + 1)
                nc.vector.tensor_tensor(cbm[:, b, :], p_cb[:, 0, :], k["triu"][:, :], ALU.mult).then_inc(masked, 1)
                dve.wait_ge(x_turned, n + 1)
                if exists(n - 2):
                    dve.wait_ge(xend_made, n - 1)
                    dve.wait_ge(y_made, n - 1)
                nc.vector.tensor_tensor(xdt[:, b, :, :], p_xt[:, :, :].rearrange("p c (h d) -> p (c h) d", d=HD),
                                        dec["dt"][:, bass.ds((i * 2 + s) * SH + g * R, R)][:, :, None].to_broadcast([P, R, HD]), ALU.mult).then_inc(xdt_made, 1)

            def maxima(i, m):
                n, g, b, s = i * UNITS + m, m % G, m % 2, m // G
                hs = slice(g * GRP, (g + 1) * GRP)
                bcv, bpv = (t[:, hs, :].rearrange("q (pair half) k -> q half pair k", half=2) for t in (bias_cur, bias_prev))
                dve.wait_ge(scored, n + 1)
                if exists(n - 2):
                    dve.wait_ge(p_turned, n - 1)
                nc.vector.tensor_tensor(heads(sc[:, b, :, :]), score[:, :, :, s, :], bcv, ALU.add).then_inc(cur_biased, 1)
                if exists(n - G):
                    nc.vector.tensor_tensor(heads(sp_[:, :, :]), score[:, :, :, 1 - s, :], bpv, ALU.add).then_inc(prev_biased, 1)
                    dve.wait_ge(cur_biased, n + 1)
                    dve.wait_ge(prev_biased, n + 1 - G)
                    nc.vector.tensor_tensor(sc[:, b, :, :], sc[:, b, :, :], sp_[:, :, :], ALU.max).then_inc(chosen, 1)
                    dve.wait_ge(chosen, n + 1 - G)
                dve.wait_ge(cur_biased, n + 1)
                nc.vector.tensor_reduce(mx[:, b, :], sc[:, b, :, :], AX, ALU.max).then_inc(maxed, 1)
                dve.wait_ge(maxed, n + 1)
                mxv, nmv, esv = (t[:, b, :].rearrange("q (half pair) -> q half pair", half=2) for t in (mx, nmx, es))
                sink = k["sink"][:, hs].rearrange("q (pair half) -> q half pair", half=2)
                nc.vector.tensor_tensor(mxv, mxv, sink, ALU.max).then_inc(sink_maxed, 1)
                dve.wait_ge(sink_maxed, n + 1)
                nc.vector.tensor_scalar(nmx[:, b, :], mx[:, b, :], -1.0, None, ALU.mult).then_inc(negated, 1)
                nc.vector.tensor_tensor(esv, sink, mxv, ALU.subtract).then_inc(sink_shifted, 1)

            def denominators(i, m):
                n, b = i * UNITS + m, m % 2
                dve.wait_ge(exp_made, n + 1)
                dve.wait_ge(sink_exp, n + 1)
                nc.vector.tensor_tensor(den[:, b, :], den[:, b, :], es[:, b, :], ALU.add).then_inc(denominated, 1)
                dve.wait_ge(denominated, n + 1)
                nc.vector.reciprocal(rden[:, b, :], den[:, b, :]).then_inc(inverted, 1)

            def scaled_c(i, m):
                n, b = i * UNITS + m, m % 2
                dve.wait_ge(row_exp, n + 1)
                nc.vector.tensor_tensor(cx[:, b, :, :], cx[:, b, :, :], ct[:, b, None, :].to_broadcast([P, R, P]), ALU.mult).then_inc(c_scaled, 1)

            def scaled_cb(i, m):
                n, b = i * UNITS + m, m % 2
                dve.wait_ge(seg_exp, n + 1)
                dve.wait_ge(masked, n + 1)
                nc.vector.tensor_tensor(seg[:, b, :, :], seg[:, b, :, :], cbm[:, b, None, :].to_broadcast([P, R, P]), ALU.mult).then_inc(m_made, 1)

            def skip(i, m):
                n, g, b = i * UNITS + m, m % G, m % 2
                dve.wait_ge(y_made, n + 1)
                dve.wait_ge(x_loaded[b], 16 * loads(b, i, m))
                if exists(n - 2):
                    dve.wait_ge(squared, n - 1)
                    dve.wait_ge(y_stored[b], 16 * (i * (UNITS // 2) + m // 2))
                for c in range(XT):
                    last = nc.vector.scalar_tensor_tensor(y[:, b, c, :], xt[:, m % 4, c, :], k["dskip"][:, g * XT + c:g * XT + c + 1], p_y[:, c, :],
                                                          ALU.mult, ALU.add)
                last.then_inc(skipped, 1)

            def new_state(i, m):
                n, g = i * UNITS + m, m % G
                dve.wait_ge(states_made, n + 1)
                dve.wait_ge(decayed, n + 1)
                nc.vector.tensor_tensor(state[g][:, :, :], state[g][:, :, :], p_st[:, :, :], ALU.add).then_inc(state_new, 1)

            def gate(i, m):
                n, b = i * UNITS + m, m % 2
                dve.wait_ge(weighed, n + 1)
                dve.wait_ge(za_loaded[b], 16 * loads(b, i, m))
                if exists(n - 2):
                    dve.wait_ge(o_stored[b], 16 * (i * (UNITS // 2) + m // 2))
                nc.vector.tensor_tensor(o[:, b, :, :], p_av[:, 0:PAIRS, :], za[:, b, :, :], ALU.mult).then_inc(gated, 1)

            def step(i, m, left):
                if left:
                    scan_inputs(*ahead(i, m, 1))
                    maxima(*ahead(i, m, 1))
                skip(i, m)
                gate(i, m)
                if left:
                    scaled_c(*ahead(i, m, 1))
                new_state(i, m)
                if left:
                    denominators(*ahead(i, m, 1))
                    scaled_cb(*ahead(i, m, 1))

            for g in range(G):
                nc.vector.memset(state[g][:, :, :], 0.0).then_inc(state_new, 1)
            nc.vector.tensor_tensor(bias_cur[:, :, :], k["bias"][:, :, :], k["neg"][:, None, :].to_broadcast([P, H, P]), ALU.add).then_inc(ready, 1)
            nc.vector.tensor_tensor(bias_prev[:, :, :], k["bias"][:, :, :], k["negcur"][:, None, :].to_broadcast([P, H, P]), ALU.add).then_inc(ready, 1)
            dve.wait_ge(state_new, G)
            dve.wait_ge(ready, 2)
            scan_inputs(0, 0)
            maxima(0, 0)
            scaled_c(0, 0)
            denominators(0, 0)
            scaled_cb(0, 0)
            steps(dve, step)
            dve.wait_ge(state_new, G + NBLK * G)


def merge(nc, a, scratch, k, out):
    HALF = S // 2
    PASSES = [(half, what) for half in range(2) for what in ("attn", "y0", "y1")] + [(0, "out"), (1, "out")]
    NJ = D // P
    TT = HALF // P
    LAST = NJ * len(PASSES) - 1
    PART = {"y0": 0, "y1": KT}
    normed_before = [KT * sum(w in PART for _, w in PASSES[:p]) for p in range(len(PASSES) + 1)]

    with Stage(nc, "merge") as st:
        a_raw = st.sb("a_raw", [P, 2, HALF]); rs_row = st.sb("rs_row", [P, 2, HALF])
        rs_loaded = [st.sem(f"rs{b}_loaded") for b in range(2)]
        a_hi = [st.sb(f"a_hi{b}", [P, KT, HALF], F32R) for b in range(2)]
        a_lo = [st.sb(f"a_lo{b}", [P, KT, HALF], F32R) for b in range(2)]
        raw = st.sb("raw", [P, 2, KT, P])
        w_hi = [st.sb(f"w_hi{b}", [P, KT, P], F32R) for b in range(2)]
        w_lo = [st.sb(f"w_lo{b}", [P, KT, P], F32R) for b in range(2)]
        side = st.sb("side", [P, 2, HALF])
        prev = st.sb("prev", [P, 2, HALF])
        res = st.sb("res", [P, 2, HALF])
        acc = st.ps("acc", [P, 2, HALF]); tok = st.ps("tok", [P, 2, TT, P])
        w_loaded = [st.sem(f"w{b}_loaded") for b in range(2)]
        a_loaded = [st.sem(f"a{b}_loaded") for b in range(2)]
        side_loaded = [st.sem(f"side{b}_loaded") for b in range(2)]
        prev_loaded = [st.sem(f"prev{b}_loaded") for b in range(2)]
        stored = [st.sem(f"res{b}_stored") for b in range(2)]
        a_normed, w_hi_made, w_lo_made, a_hi_made, a_lo_made, multiplied, gated, out_gated, turned, res_made = [st.sem(n) for n in (
            "a_normed", "w_hi_made", "w_lo_made", "a_hi_made", "a_lo_made", "multiplied", "gated", "out_gated", "turned", "res_made")]
        blk = st.block()
        weight = {"attn": a["w_attn_proj"], "y0": a["w_ssm_proj_0"], "y1": a["w_ssm_proj_1"], "out": a["w_out"]}
        source = {"attn": scratch["attn"], "y0": scratch["y"][0:D, :], "y1": scratch["y"][D:2 * D, :], "out": scratch["m"]}
        OUT0 = NJ * sum(w != "out" for _, w in PASSES)

        def tiles(eng, body):
            for p in range(len(PASSES)):
                n0 = NJ * p
                lo, hi = (1 if n0 in (0, OUT0) else 0), NJ // 2 - (1 if p == len(PASSES) - 1 else 0)
                if lo:
                    for b in range(2):
                        body(n0 + b, b, n0 // 2, p, b)
                with eng.Fori(lo, hi) as i:
                    for b in range(2):
                        body(2 * i + (n0 + b), b, i + n0 // 2, p, 2 * i + b)
                if hi < NJ // 2:
                    for b in range(2):
                        body(LAST - 1 + b, b, LAST // 2, p, NJ - 2 + b)

        @blk.sync
        def _(sp):
            def chunk(c, b, h, p, j):
                half, what = PASSES[p]
                if exists(c - 2):
                    sp.wait_ge(a_lo_made, c - 1)
                sp.dma_start(a_raw[:, b, :], source[what][bass.ds(j * P, P), half * HALF:(half + 1) * HALF]).then_inc(a_loaded[b], 16)
                if what in PART:
                    rs = scratch["rs"][PART[what]:PART[what] + KT, half * HALF:(half + 1) * HALF][bass.ds(j, 1), :]
                    sp.dma_start(rs_row[:, b, :], rs.to_broadcast([P, HALF])).then_inc(rs_loaded[b], 16)

            def load_w(b, p, j):
                sp.dma_start(raw[:, b, :, :], weight[PASSES[p][1]][bass.ds(j, 1)].rearrange("o p k c -> (o p) k c")).then_inc(w_loaded[b], 16)

            def load(n, b, h, p, j):
                half, what = PASSES[p]
                cols = slice(half * HALF, (half + 1) * HALF)
                row = j * P if isinstance(j, int) else sp.snap(j * P)
                if exists(n - 2):
                    sp.wait_ge(w_lo_made, n - 1)
                    load_w(b, p, j)
                if p + 1 < len(PASSES):
                    if PASSES[p + 1][1] == "out":
                        for bb in range(2):
                            sp.wait_ge(stored[bb], 16 * (NJ // 2) * (3 * (PASSES[p + 1][0] + 1)))
                    chunk(n + KT, b, h + KT // 2, p + 1, j)
                if what in ("y0", "y1"):
                    sp.wait_ge(stored[b], 16 * (h - 3))
                if what == "out":
                    sp.wait_ge(a_lo_made, KT)
                if exists(n - 2):
                    sp.wait_ge(res_made, n - 1)
                if what == "out":
                    sp.dma_start(side[:, b, :].rearrange("p (t c) -> p t c", c=P),
                                 a["x"][0, cols, bass.ds(row, P)].rearrange("(t p) c -> p t c", p=P)).then_inc(side_loaded[b], 16)
                else:
                    g0 = 0 if what == "attn" else D
                    sp.dma_start(side[:, b, :], scratch["g"][g0:g0 + D][bass.ds(row, P), cols]).then_inc(side_loaded[b], 16)
                if what in ("y0", "y1"):
                    sp.dma_start(prev[:, b, :], scratch["m"][bass.ds(row, P), cols]).then_inc(prev_loaded[b], 16)

            for b in range(2):
                load_w(b, 0, b)
                chunk(b, b, 0, 0, b)
            with sp.Fori(1, KT // 2) as i:
                for b in range(2):
                    chunk(2 * i + b, b, i, 0, 2 * i + b)
            tiles(sp, load)

        @blk.gpsimd
        def _(pool):
            def store(n, b, h, p, j):
                half, what = PASSES[p]
                pool.wait_ge(res_made, n + 1)
                if what == "out":
                    pool.dma_start(out[0, half * HALF:(half + 1) * HALF, bass.ds(j * P, P)].rearrange("(t p) c -> p t c", p=P),
                                   res[:, b, :].rearrange("p (t c) -> p t c", c=P)).then_inc(stored[b], 16)
                else:
                    pool.dma_start(scratch["m"][bass.ds(j * P, P), half * HALF:(half + 1) * HALF], res[:, b, :]).then_inc(stored[b], 16)
            tiles(pool, store)
            for b in range(2):
                pool.wait_ge(stored[b], 16 * (LAST + 1) // 2)

        @blk.tensor
        def _(pe):
            def turn(n, b):
                pe.wait_ge(out_gated, n - OUT0)
                for t in range(TT):
                    last = nc.tensor.transpose(tok[:, b, t, :], prev[:, b, t * P:(t + 1) * P], k["ident"][:, :])
                last.then_inc(turned, 1)

            def product(n, b, h, p, j):
                half, what = PASSES[p]
                s = p % 2
                pe.wait_ge(w_lo_made, n + 1)
                first = isinstance(n, int) and n == 0
                if not first:
                    pe.wait_ge(a_lo_made, KT * (p + 1))
                if exists(n - 2):
                    pe.wait_ge(res_made, n - 1)
                for kk in range(KT):
                    if first:
                        pe.wait_ge(a_lo_made, kk + 1)
                    if kk == KT // 2 and what == "out" and not (isinstance(n, int) and n == OUT0):
                        turn(n, 1 - b)
                    for step, (wv, av) in enumerate(((w_hi[b], a_hi[s]), (w_hi[b], a_lo[s]), (w_lo[b], a_hi[s]))):
                        for c in range(HALF // MM):
                            last = nc.tensor.matmul(acc[:, b, c * MM:(c + 1) * MM], wv[:, kk, :], av[:, kk, c * MM:(c + 1) * MM],
                                                    start=(kk == 0 and step == 0), stop=(kk == KT - 1 and step == 2))
                last.then_inc(multiplied, 1)

            tiles(pe, product)
            turn(LAST + 1, LAST % 2)

        @blk.scalar
        def _(act):
            def high_w(b, h):
                act.wait_ge(w_loaded[b], 16 * h + 16)
                nc.scalar.activation(w_hi[b][:, :, :], raw[:, b, :, :], ACT.Copy).then_inc(w_hi_made, 1)

            def high_a(c, b, h, p, j):
                if PASSES[p][1] in PART:
                    act.wait_ge(a_normed, c - (KT * p - normed_before[p] - 1))
                else:
                    act.wait_ge(a_loaded[b], 16 * h + 16)
                nc.scalar.activation(a_hi[p % 2][:, bass.ds(j, 1), :], a_raw[:, b, None, :], ACT.Copy).then_inc(a_hi_made, 1)

            def step(n, b, h, p, j):
                if not (isinstance(n, int) and n == LAST):
                    if exists(n - 1):
                        act.wait_ge(multiplied, n)
                    high_w(1 - b, h + b)
                if p + 1 < len(PASSES):
                    high_a(n + KT, b, h + KT // 2, p + 1, j)
                if PASSES[p][1] == "out":
                    act.wait_ge(multiplied, n + 1)
                    nc.scalar.activation(prev[:, b, :], acc[:, b, :], ACT.Copy, scale=k["gate"][:, bass.ds(j, 1)]).then_inc(out_gated, 1)

            high_w(0, 0)
            for b in range(2):
                high_a(b, b, 0, 0, b)
            with act.Fori(1, KT // 2) as i:
                for b in range(2):
                    high_a(2 * i + b, b, i, 0, 2 * i + b)
            tiles(act, step)

        @blk.vector
        def _(dve):
            def low_w(n, b):
                dve.wait_ge(w_hi_made, n + 1)
                if exists(n - 2):
                    dve.wait_ge(multiplied, n - 1)
                nc.vector.tensor_tensor(w_lo[b][:, :, :], raw[:, b, :, :], w_hi[b][:, :, :], ALU.subtract).then_inc(w_lo_made, 1)

            def low_a(c, b, h, p, j):
                dve.wait_ge(a_hi_made, c + 1)
                nc.vector.tensor_tensor(a_lo[p % 2][:, bass.ds(j, 1), :], a_raw[:, b, None, :], a_hi[p % 2][:, bass.ds(j, 1), :], ALU.subtract).then_inc(a_lo_made, 1)

            def norm_a(c, b, h, p, j):
                if PASSES[p][1] not in PART:
                    return
                part = PART[PASSES[p][1]]
                dve.wait_ge(a_loaded[b], 16 * h + 16)
                dve.wait_ge(rs_loaded[b], 16 * (h - (KT * p - normed_before[p]) // 2) + 16)
                nc.vector.scalar_tensor_tensor(a_raw[:, b, :], a_raw[:, b, :], k["ssmw"][:, part:part + KT][:, bass.ds(j, 1)], rs_row[:, b, :],
                                               ALU.mult, ALU.mult).then_inc(a_normed, 1)

            def step(n, b, h, p, j):
                what = PASSES[p][1]
                if not (isinstance(n, int) and n == LAST):
                    low_w(n + 1, 1 - b)
                if p + 1 < len(PASSES):
                    norm_a(n + KT, b, h + KT // 2, p + 1, j)
                    low_a(n + KT, b, h + KT // 2, p + 1, j)
                dve.wait_ge(side_loaded[b], 16 * h + 16)
                if exists(n - 2):
                    dve.wait_ge(stored[b], 16 * h)
                if what == "out":
                    dve.wait_ge(turned, n - (OUT0 - 1))
                    nc.vector.tensor_tensor(res[:, b, :], tok[:, b, :, :].rearrange("p t c -> p (t c)"), side[:, b, :], ALU.add).then_inc(res_made, 1)
                    return
                dve.wait_ge(multiplied, n + 1)
                if what == "attn":
                    nc.vector.tensor_tensor(res[:, b, :], acc[:, b, :], side[:, b, :], ALU.mult).then_inc(res_made, 1)
                    return
                nc.vector.tensor_tensor(res[:, b, :], acc[:, b, :], side[:, b, :], ALU.mult).then_inc(gated, 1)
                seen = NJ * (1 + PASSES[p][0])
                dve.wait_ge(gated, n - (seen - 1))
                dve.wait_ge(prev_loaded[b], 16 * (h - (seen // 2 - 1)))
                nc.vector.tensor_tensor(res[:, b, :], res[:, b, :], prev[:, b, :], ALU.add).then_inc(res_made, 1)

            low_w(0, 0)
            for b in range(2):
                low_a(b, b, 0, 0, b)
            with dve.Fori(1, KT // 2) as i:
                for b in range(2):
                    low_a(2 * i + b, b, i, 0, 2 * i + b)
            tiles(dve, step)
            dve.wait_ge(res_made, LAST + 1)


def columns(v, copies=1):
    v = np.asarray(v).reshape(-1)
    v = np.concatenate([v] * copies)
    return np.ascontiguousarray(v.reshape(-1, P).T)


def weight_tiles(w):
    rows, cols = w.shape
    return np.ascontiguousarray(w.reshape(rows // P, P, cols // P, P).transpose(2, 1, 0, 3))


def layouts(i):
    w_in = i["w_in"][0]
    o = {"x": i["x"], "w_ada": i["w_ada"], "rel_bias": i["rel_bias"], "onehot": bucket_onehot(),
         "c": columns(i["c"]), "b_ada": columns(i["b_ada"]), "norm_w": columns(i["norm_w"]), "conv_b": columns(i["conv_b"]),
         "ssm_norm_w": columns(i["ssm_norm_w"]), "q_norm_w": columns(i["q_norm_w"], P // HD), "k_norm_w": columns(i["k_norm_w"], P // HD),
         "dt_bias": i["dt_bias"].reshape(SH, 1), "sinks": i["sinks"].reshape(1, H), "a_log": i["a_log"].reshape(1, SH),
         "d_skip": columns(np.repeat(i["d_skip"].reshape(-1), HD)),
         "conv_w": np.ascontiguousarray(i["conv_w"][0].reshape(CW, XBC // P, P).transpose(2, 0, 1)),
         "w_attn_proj": weight_tiles(i["w_attn_proj"][0]), "w_out": weight_tiles(i["w_out"][0]),
         "w_ssm_proj_0": weight_tiles(i["w_ssm_proj"][0, 0:D]), "w_ssm_proj_1": weight_tiles(i["w_ssm_proj"][0, D:2 * D])}
    for _, col, count, name in KINDS:
        o["w_in_" + name] = weight_tiles(w_in[:, col:col + count * P])
    return {n: np.ascontiguousarray(v) for n, v in o.items()}


def kernel(**inputs):
    import concourse.bacc as bacc
    from concourse.bass_utils import run_bass_kernel_spmd

    nc = bacc.Bacc("TRN2", target_bir_lowering=False, num_devices=1)
    arrays, aps = {}, {}
    for name, v in layouts({n: np.asarray(v) for n, v in inputs.items()}).items():
        arrays["in_" + name] = v
        aps[name] = nc.dram_tensor("in_" + name, v.shape, mybir.dt.from_np(v.dtype), kind="ExternalInput").ap()
    out = nc.dram_tensor("out", (1, S, D), F32, kind="ExternalOutput").ap()
    build(nc, aps, out)
    r = run_bass_kernel_spmd(nc, [arrays], core_ids=[0])
    return r.results[0]["out"]
```
